# Optimizing a Trainium2 kernel written in Bass

```python
import jax, jax.numpy as jnp
from jax import lax
import numpy as np

D_MODEL = 1024
BATCH = 1
SEQ = 512
DEPTH = 1

CTX_LEN = 256
GRID_W = 64
HEAD_DIM = 128
N_Q_HEADS = D_MODEL // HEAD_DIM
N_KV_HEADS = N_Q_HEADS // 4
GQA_GROUP = N_Q_HEADS // N_KV_HEADS
ROPE_AXIS_DIM = HEAD_DIM // 2
ROPE_THETA = 10000.0
Q_BLOCK = 128
CONV_DIM = D_MODEL
CONV_WIDTH = 31
PEER_HEADS = 8
PEER_N_KEYS = 128
PEER_EXPERTS = PEER_N_KEYS * PEER_N_KEYS
PEER_TOPK = 16
PEER_KEY_DIM = 256
PEER_HALF = PEER_KEY_DIM // 2
PEER_CHUNK = 128
N_MOD = 6
EPS = 1e-6
Q_W = N_Q_HEADS * HEAD_DIM
KV_W = N_KV_HEADS * HEAD_DIM
IN_SPLITS = (Q_W, Q_W + KV_W, Q_W + 2 * KV_W, Q_W + 2 * KV_W + 2 * CONV_DIM, Q_W + 2 * KV_W + 2 * CONV_DIM + D_MODEL)
IN_W = IN_SPLITS[-1] + D_MODEL


def rmsnorm(x, g):
    xf = x.astype(jnp.float32)
    y = xf * lax.rsqrt(jnp.mean(xf * xf, axis=-1, keepdims=True) + EPS)
    return (y * g.astype(jnp.float32)).astype(x.dtype)

def layernorm(x, g, b):
    xf = x.astype(jnp.float32)
    mu = jnp.mean(xf, axis=-1, keepdims=True)
    var = jnp.mean(jnp.square(xf - mu), axis=-1, keepdims=True)
    y = (xf - mu) * lax.rsqrt(var + EPS) * g.astype(jnp.float32) + b.astype(jnp.float32)
    return y.astype(x.dtype)

def modulate(h, shift, scale):
    return h * (1 + scale) + shift

def axial_rope_tables(n_tokens, dtype):
    rows = n_tokens // GRID_W
    row = jnp.repeat(jnp.arange(rows, dtype=jnp.float32), GRID_W)
    col = jnp.tile(jnp.arange(GRID_W, dtype=jnp.float32), rows)
    inv = ROPE_THETA ** (-jnp.arange(0, ROPE_AXIS_DIM, 2, dtype=jnp.float32) / ROPE_AXIS_DIM)
    ang_r = row[:, None] * inv
    ang_c = col[:, None] * inv
    return (jnp.cos(ang_r)[:, None, :].astype(dtype), jnp.sin(ang_r)[:, None, :].astype(dtype),
            jnp.cos(ang_c)[:, None, :].astype(dtype), jnp.sin(ang_c)[:, None, :].astype(dtype))

def rotate(xa, cos, sin):
    x1, x2 = jnp.split(xa, 2, axis=-1)
    return jnp.concatenate([x1 * cos - x2 * sin, x1 * sin + x2 * cos], axis=-1)

def apply_rope(x, rope):
    cos_r, sin_r, cos_c, sin_c = rope
    xr, xc = jnp.split(x, 2, axis=-1)
    return jnp.concatenate([rotate(xr, cos_r, sin_r), rotate(xc, cos_c, sin_c)], axis=-1)

def attend(q, k, v):
    B, T = q.shape[0], q.shape[1]
    nb = T // Q_BLOCK
    scale = HEAD_DIM ** -0.5
    qb = q.reshape(B, nb, Q_BLOCK, N_KV_HEADS, GQA_GROUP, HEAD_DIM).transpose(1, 0, 2, 3, 4, 5)

    def block(qi):
        s = jnp.einsum('bqkgd,bskd->bkgqs', qi, k).astype(jnp.float32) * scale
        p = jax.nn.softmax(s, axis=-1).astype(v.dtype)
        return jnp.einsum('bkgqs,bskd->bqkgd', p, v)

    o = lax.map(block, qb)
    return o.transpose(1, 0, 2, 3, 4, 5).reshape(B, T, Q_W)

def conformer_conv(u, lw):
    a, b = jnp.split(u, 2, axis=-1)
    g = a * jax.nn.sigmoid(b)
    pad = CONV_WIDTH // 2
    g = lax.conv_general_dilated(g, lw['conv_dw'][:, None, :], window_strides=(1,), padding=[(pad, pad)],
                                 dimension_numbers=('NWC', 'WIO', 'NWC'), feature_group_count=CONV_DIM)
    g = layernorm(g + lw['conv_b'], lw['conv_ln_g'], lw['conv_ln_b'])
    return jax.nn.silu(g) @ lw['w_conv_o']

def context_kv(h, lw):
    B, T, _ = h.shape
    kv = h @ lw['w_in'][:, Q_W:Q_W + 2 * KV_W]
    k, v = jnp.split(kv, 2, axis=-1)
    k = rmsnorm(k.reshape(B, T, N_KV_HEADS, HEAD_DIM), lw['k_norm_g'])
    return k, v.reshape(B, T, N_KV_HEADS, HEAD_DIM)

def token_mixer(h, lw, rope, k_ctx, v_ctx):
    B, T, _ = h.shape
    q, k, v, u, ga, gc = jnp.split(h @ lw['w_in'], IN_SPLITS, axis=-1)
    q = rmsnorm(q.reshape(B, T, N_Q_HEADS, HEAD_DIM), lw['q_norm_g'])
    k = rmsnorm(k.reshape(B, T, N_KV_HEADS, HEAD_DIM), lw['k_norm_g'])
    v = v.reshape(B, T, N_KV_HEADS, HEAD_DIM)
    if rope is not None:
        q = apply_rope(q, rope)
        k = jnp.concatenate([apply_rope(k, rope), k_ctx], axis=1)
        v = jnp.concatenate([v, v_ctx], axis=1)
    y_att = attend(q, k, v) @ lw['w_attn_o']
    y_conv = conformer_conv(u, lw)
    merged = jax.nn.sigmoid(ga) * y_att + jax.nn.sigmoid(gc) * y_conv
    return merged @ lw['w_out']

def peer_ffn(h, lw):
    B, T, D = h.shape
    wq, keys, u_tab, v_tab = lw['peer_wq'], lw['peer_keys'], lw['peer_u'], lw['peer_v']

    def chunk(xc):
        q = (xc @ wq).reshape(PEER_CHUNK, PEER_HEADS, 2, PEER_HALF)
        s = jnp.einsum('thpd,hpnd->thpn', q, keys)
        s_top, i_top = lax.top_k(s, PEER_TOPK)
        n_cand = PEER_TOPK * PEER_TOPK
        cand_s = (s_top[:, :, 0, :, None] + s_top[:, :, 1, None, :]).reshape(PEER_CHUNK, PEER_HEADS, n_cand)
        cand_i = (i_top[:, :, 0, :, None] * PEER_N_KEYS + i_top[:, :, 1, None, :]).reshape(PEER_CHUNK, PEER_HEADS, n_cand)
        best_s, best_pos = lax.top_k(cand_s, PEER_TOPK)
        eid = jnp.take_along_axis(cand_i, best_pos, axis=-1)
        w = jax.nn.softmax(best_s.astype(jnp.float32), axis=-1).astype(xc.dtype)
        act = jax.nn.gelu(jnp.einsum('thkd,td->thk', jnp.take(u_tab, eid, axis=0), xc), approximate=False)
        return jnp.einsum('thk,thkd->td', w * act, jnp.take(v_tab, eid, axis=0))

    y = lax.map(chunk, h.reshape(-1, PEER_CHUNK, D))
    return y.reshape(B, T, D)

def first_inputs(seed: int = 0) -> dict:
    key = jax.random.key(seed)
    ks = jax.random.split(key, 24)
    L, D = DEPTH, D_MODEL

    def nrm(k, shape, scale):
        return jax.random.normal(k, shape, jnp.float32) * scale

    return {
        'x': nrm(ks[0], (BATCH, SEQ, D), 1.0),
        'c': nrm(ks[1], (BATCH, D), 1.0),
        'ctx': nrm(ks[2], (BATCH, CTX_LEN, D), 1.0),
        'c_ctx': nrm(ks[3], (D,), 1.0),
        'w_mod': nrm(ks[4], (L, D, N_MOD * D), 0.5 * D ** -0.5),
        'b_mod': nrm(ks[5], (L, N_MOD * D), 0.01),
        'norm1_g': 1.0 + nrm(ks[6], (L, D), 0.1),
        'norm2_g': 1.0 + nrm(ks[7], (L, D), 0.1),
        'w_in': nrm(ks[8], (L, D, IN_W), D ** -0.5),
        'q_norm_g': 1.0 + nrm(ks[9], (L, HEAD_DIM), 0.1),
        'k_norm_g': 1.0 + nrm(ks[10], (L, HEAD_DIM), 0.1),
        'w_attn_o': nrm(ks[11], (L, Q_W, D), Q_W ** -0.5),
        'conv_dw': nrm(ks[12], (L, CONV_WIDTH, CONV_DIM), CONV_WIDTH ** -0.5),
        'conv_b': nrm(ks[13], (L, CONV_DIM), 0.01),
        'conv_ln_g': 1.0 + nrm(ks[14], (L, CONV_DIM), 0.1),
        'conv_ln_b': nrm(ks[15], (L, CONV_DIM), 0.01),
        'w_conv_o': nrm(ks[16], (L, CONV_DIM, D), CONV_DIM ** -0.5),
        'w_out': nrm(ks[17], (L, D, D), D ** -0.5),
        'peer_wq': nrm(ks[18], (L, D, PEER_HEADS * PEER_KEY_DIM), D ** -0.5),
        'peer_keys': nrm(ks[19], (L, PEER_HEADS, 2, PEER_N_KEYS, PEER_HALF), PEER_HALF ** -0.5),
        'peer_u': nrm(ks[20], (L, PEER_EXPERTS, D), D ** -0.5),
        'peer_v': nrm(ks[21], (L, PEER_EXPERTS, D), 0.5),
        'final_norm_g': 1.0 + nrm(ks[22], (D,), 0.1),
    }

def first_block(x, c, ctx, c_ctx, w_mod, b_mod, norm1_g, norm2_g, w_in, q_norm_g, k_norm_g,
              w_attn_o, conv_dw, conv_b, conv_ln_g, conv_ln_b, w_conv_o, w_out,
              peer_wq, peer_keys, peer_u, peer_v, final_norm_g):
    S = x.shape[1]
    rope = axial_rope_tables(S, x.dtype)
    xs, cs = x, ctx
    for l in range(DEPTH):
        lw = {'w_in': w_in[l], 'q_norm_g': q_norm_g[l], 'k_norm_g': k_norm_g[l], 'w_attn_o': w_attn_o[l],
              'conv_dw': conv_dw[l], 'conv_b': conv_b[l], 'conv_ln_g': conv_ln_g[l], 'conv_ln_b': conv_ln_b[l],
              'w_conv_o': w_conv_o[l], 'w_out': w_out[l], 'peer_wq': peer_wq[l], 'peer_keys': peer_keys[l],
              'peer_u': peer_u[l], 'peer_v': peer_v[l]}
        last = l == DEPTH - 1
        sh1, sc1, g1, sh2, sc2, g2 = [m[:, None, :] for m in
                                      jnp.split(jax.nn.silu(c) @ w_mod[l] + b_mod[l], N_MOD, axis=-1)]
        csh1, csc1, cg1, csh2, csc2, cg2 = jnp.split(jax.nn.silu(c_ctx) @ w_mod[l] + b_mod[l], N_MOD, axis=-1)
        hc = modulate(rmsnorm(cs, norm1_g[l]), csh1, csc1)
        k_c, v_c = context_kv(hc, lw)
        hx = modulate(rmsnorm(xs, norm1_g[l]), sh1, sc1)
        xs = xs + g1 * token_mixer(hx, lw, rope, k_c, v_c)
        if not last:
            cs = cs + cg1 * token_mixer(hc, lw, None, None, None)
        hx = modulate(rmsnorm(xs, norm2_g[l]), sh2, sc2)
        xs = xs + g2 * peer_ffn(hx, lw)
        if not last:
            hc = modulate(rmsnorm(cs, norm2_g[l]), csh2, csc2)
            cs = cs + cg2 * peer_ffn(hc, lw)
    return rmsnorm(xs, final_norm_g)


N_MIXERS = 4
HEAD_DIM_2 = 64
N_Q_HEADS_2 = D_MODEL // HEAD_DIM_2
N_KV_HEADS_2 = 4
GQA_GROUP_2 = N_Q_HEADS_2 // N_KV_HEADS_2
ATTN_Q_DIM = N_Q_HEADS_2 * HEAD_DIM_2
ATTN_KV_DIM = N_KV_HEADS_2 * HEAD_DIM_2
ATTN_IN_DIM = ATTN_Q_DIM + 2 * ATTN_KV_DIM
SWA_WINDOW = 128
SWA_BLOCK = 128
MOBA_BLOCK = 256
MOBA_TOP_K = 3
MOBA_Q_CHUNK = 64
GLA_HEADS = 4
GLA_KEY_DIM = D_MODEL // (2 * GLA_HEADS)
GLA_VAL_DIM = D_MODEL // GLA_HEADS
GLA_GATE_RANK = 16
GLA_GATE_TEMP = 16.0
GLA_IN_DIM = 2 * GLA_HEADS * GLA_KEY_DIM + 2 * GLA_HEADS * GLA_VAL_DIM + GLA_GATE_RANK
HGRN_EXPAND = 128
HGRN_HEADS = D_MODEL // HGRN_EXPAND
HGRN_KEY_DIM = HGRN_EXPAND
HGRN_VAL_DIM = D_MODEL // HGRN_HEADS
HGRN_IN_DIM = 4 * D_MODEL
LIN_CHUNK = 64
D_FF = ((8 * D_MODEL + 3 * 256 - 1) // (3 * 256)) * 256
RMS_EPS = 1e-6


def rms_norm(x, w):
    xf = x.astype(jnp.float32)
    y = xf * lax.rsqrt(jnp.mean(xf * xf, axis=-1, keepdims=True) + RMS_EPS)
    return (y * w.astype(jnp.float32)).astype(x.dtype)

def head_rms_norm(o, w):
    return o * lax.rsqrt(jnp.mean(o * o, axis=-1, keepdims=True) + RMS_EPS) * w.astype(jnp.float32)

def alibi_slopes(n_heads):
    return jnp.exp2(-8.0 * jnp.arange(1, n_heads + 1, dtype=jnp.float32) / n_heads)

def split_qkv(h, w_in):
    B, T, _ = h.shape
    proj = h @ w_in
    q = proj[..., :ATTN_Q_DIM].reshape(B, T, N_KV_HEADS_2, GQA_GROUP_2, HEAD_DIM_2)
    k = proj[..., ATTN_Q_DIM:ATTN_Q_DIM + ATTN_KV_DIM].reshape(B, T, N_KV_HEADS_2, HEAD_DIM_2)
    v = proj[..., ATTN_Q_DIM + ATTN_KV_DIM:].reshape(B, T, N_KV_HEADS_2, HEAD_DIM_2)
    return q, k, v

def sliding_window_sink_attention(h, w_in, sinks, w_out):
    B, T, _ = h.shape
    L = SWA_BLOCK
    nb = T // L
    q, k, v = split_qkv(h, w_in)
    qb = q.reshape(B, nb, L, N_KV_HEADS_2, GQA_GROUP_2, HEAD_DIM_2)

    def with_prev(a):
        a = a.reshape(B, nb, L, N_KV_HEADS_2, HEAD_DIM_2)
        prev = jnp.concatenate([jnp.zeros_like(a[:, :1]), a[:, :-1]], axis=1)
        return jnp.concatenate([prev, a], axis=2)

    kw, vw = with_prev(k), with_prev(v)
    s = jnp.einsum('bnqhgd,bnkhd->bnhgqk', qb, kw, preferred_element_type=jnp.float32) * (HEAD_DIM_2 ** -0.5)
    dist = (L + jnp.arange(L))[:, None] - jnp.arange(2 * L)[None, :]
    band = (dist >= 0) & (dist < SWA_WINDOW)
    has_prev = (jnp.arange(nb)[:, None, None] > 0) | (jnp.arange(2 * L)[None, None, :] >= L)
    mask = band[None] & has_prev
    slopes = alibi_slopes(N_Q_HEADS_2).reshape(N_KV_HEADS_2, GQA_GROUP_2)
    s = s - slopes[:, :, None, None] * dist.astype(jnp.float32)
    s = jnp.where(mask[None, :, None, None], s, -jnp.inf)
    sink = sinks.astype(jnp.float32).reshape(N_KV_HEADS_2, GQA_GROUP_2)[:, :, None, None]
    m = jnp.maximum(jnp.max(s, axis=-1, keepdims=True), sink)
    p = jnp.exp(s - m)
    denom = jnp.sum(p, axis=-1, keepdims=True) + jnp.exp(sink - m)
    o = jnp.einsum('bnhgqk,bnkhd->bnqhgd', p / denom, vw.astype(jnp.float32))
    return o.reshape(B, T, ATTN_Q_DIM).astype(h.dtype) @ w_out

def moba_attention(h, w_in, w_out):
    B, T, _ = h.shape
    Lb, Qc = MOBA_BLOCK, MOBA_Q_CHUNK
    q, k, v = split_qkv(h, w_in)
    Tp = ((T + Lb - 1) // Lb) * Lb
    pad = Tp - T
    q = jnp.pad(q.astype(jnp.float32), ((0, 0), (0, pad), (0, 0), (0, 0), (0, 0))) * (HEAD_DIM_2 ** -0.5)
    k = jnp.pad(k.astype(jnp.float32), ((0, 0), (0, pad), (0, 0), (0, 0)))
    v = jnp.pad(v.astype(jnp.float32), ((0, 0), (0, pad), (0, 0), (0, 0)))
    nblk, nq = Tp // Lb, Tp // Qc
    n_sel = min(MOBA_TOP_K, nblk)
    kb = k.reshape(B, nblk, Lb, N_KV_HEADS_2, HEAD_DIM_2).transpose(0, 3, 1, 2, 4)
    vb = v.reshape(B, nblk, Lb, N_KV_HEADS_2, HEAD_DIM_2).transpose(0, 3, 1, 2, 4)
    k_mean = jnp.mean(kb, axis=3)
    gate = jnp.einsum('bthgd,bhnd->bhtn', q, k_mean)
    t_blk = jnp.arange(Tp) // Lb
    past = jnp.arange(nblk)[None, :] < t_blk[:, None]
    gate = jnp.where(past, gate, -jnp.inf)
    _, sel_idx = lax.top_k(gate, n_sel)
    sel_valid = jnp.arange(n_sel)[None, :] < t_blk[:, None]
    q_chunks = q.reshape(B, nq, Qc, N_KV_HEADS_2, GQA_GROUP_2, HEAD_DIM_2).transpose(1, 0, 2, 3, 4, 5)
    idx_chunks = sel_idx.reshape(B, N_KV_HEADS_2, nq, Qc, n_sel).transpose(2, 0, 1, 3, 4)
    valid_chunks = sel_valid.reshape(nq, Qc, n_sel)
    slopes = alibi_slopes(N_Q_HEADS_2).reshape(N_KV_HEADS_2, GQA_GROUP_2)
    gather_blocks = jax.vmap(jax.vmap(lambda blocks, ix: blocks[ix]))

    def attend(args):
        c, qc, idx, valid = args
        t_q = c * Qc + jnp.arange(Qc)
        own = (c * Qc) // Lb
        k_own = lax.dynamic_index_in_dim(kb, own, axis=2, keepdims=False)
        v_own = lax.dynamic_index_in_dim(vb, own, axis=2, keepdims=False)
        k_sel = gather_blocks(kb, idx)
        v_sel = gather_blocks(vb, idx)
        s_sel = jnp.einsum('bqhgd,bhqnkd->bhgqnk', qc, k_sel)
        dist_sel = (t_q[:, None, None] - (idx[..., None] * Lb + jnp.arange(Lb))).astype(jnp.float32)
        s_sel = s_sel - slopes[None, :, :, None, None, None] * dist_sel[:, :, None]
        s_sel = jnp.where(valid[:, :, None], s_sel, -jnp.inf)
        s_own = jnp.einsum('bqhgd,bhkd->bhgqk', qc, k_own)
        dist_own = t_q[:, None] - (own * Lb + jnp.arange(Lb))[None, :]
        s_own = s_own - slopes[:, :, None, None] * dist_own.astype(jnp.float32)
        s_own = jnp.where(dist_own >= 0, s_own, -jnp.inf)
        s_all = jnp.concatenate([s_sel.reshape(B, N_KV_HEADS_2, GQA_GROUP_2, Qc, n_sel * Lb), s_own], axis=-1)
        p = jax.nn.softmax(s_all, axis=-1)
        p_sel = p[..., :n_sel * Lb].reshape(B, N_KV_HEADS_2, GQA_GROUP_2, Qc, n_sel, Lb)
        p_own = p[..., n_sel * Lb:]
        return (jnp.einsum('bhgqnk,bhqnkd->bqhgd', p_sel, v_sel)
                + jnp.einsum('bhgqk,bhkd->bqhgd', p_own, v_own))

    o = lax.map(attend, (jnp.arange(nq), q_chunks, idx_chunks, valid_chunks))
    o = o.transpose(1, 0, 2, 3, 4, 5).reshape(B, Tp, ATTN_Q_DIM)[:, :T]
    return o.astype(h.dtype) @ w_out

def chunked_gated_linear_attention(q, k, v, log_g):
    B, T, H, K = q.shape
    V = v.shape[-1]
    L = LIN_CHUNK
    nc = T // L

    def to_chunks(a):
        return a.astype(jnp.float32).reshape(B, nc, L, H, a.shape[-1]).transpose(1, 0, 3, 2, 4)

    causal = jnp.tril(jnp.ones((L, L), dtype=bool))

    def step(S, inp):
        qc, kc, vc, gc = inp
        b = jnp.cumsum(gc, axis=2)
        b_last = b[:, :, -1:, :]
        q_dec = qc * jnp.exp(b)
        attn = jnp.einsum('bhtk,bhsk->bhts', q_dec, kc * jnp.exp(-b))
        attn = jnp.where(causal, attn, 0.0)
        o = jnp.einsum('bhts,bhsv->bhtv', attn, vc) + jnp.einsum('bhtk,bhkv->bhtv', q_dec, S)
        S = S * jnp.exp(b_last).swapaxes(-1, -2) + jnp.einsum('bhsk,bhsv->bhkv', kc * jnp.exp(b_last - b), vc)
        return S, o

    S0 = jnp.zeros((B, H, K, V), jnp.float32)
    _, o = lax.scan(step, S0, (to_chunks(q), to_chunks(k), to_chunks(v), to_chunks(log_g)))
    return o.transpose(1, 0, 3, 2, 4).reshape(B, T, H, V)

def gla_mixer(h, w_in, w_decay_up, b_decay, out_norm, w_out):
    B, T, _ = h.shape
    proj = h @ w_in
    dk, dv = GLA_HEADS * GLA_KEY_DIM, GLA_HEADS * GLA_VAL_DIM
    q = proj[..., :dk].reshape(B, T, GLA_HEADS, GLA_KEY_DIM).astype(jnp.float32) * (GLA_KEY_DIM ** -0.5)
    k = proj[..., dk:2 * dk].reshape(B, T, GLA_HEADS, GLA_KEY_DIM)
    v = proj[..., 2 * dk:2 * dk + dv].reshape(B, T, GLA_HEADS, GLA_VAL_DIM)
    g = proj[..., 2 * dk + dv:2 * dk + 2 * dv].reshape(B, T, GLA_HEADS, GLA_VAL_DIM)
    a = proj[..., 2 * dk + 2 * dv:]
    log_alpha = jax.nn.log_sigmoid((a @ w_decay_up + b_decay).astype(jnp.float32)) / GLA_GATE_TEMP
    log_alpha = log_alpha.reshape(B, T, GLA_HEADS, GLA_KEY_DIM)
    o = chunked_gated_linear_attention(q, k, v, log_alpha)
    o = head_rms_norm(o, out_norm) * jax.nn.silu(g.astype(jnp.float32))
    return o.reshape(B, T, dv).astype(h.dtype) @ w_out

def hgrn2_mixer(h, w_in, lower_bound, out_norm, w_out):
    B, T, _ = h.shape
    proj = h @ w_in
    d = D_MODEL
    q = jax.nn.silu(proj[..., :d].astype(jnp.float32)) * (HGRN_KEY_DIM ** -0.5)
    f = lower_bound + (1.0 - lower_bound) * jax.nn.sigmoid(proj[..., d:2 * d].astype(jnp.float32))
    i = proj[..., 2 * d:3 * d]
    g = proj[..., 3 * d:]
    shp_k = (B, T, HGRN_HEADS, HGRN_KEY_DIM)
    o = chunked_gated_linear_attention(q.reshape(shp_k), (1.0 - f).reshape(shp_k),
                                       i.reshape(B, T, HGRN_HEADS, HGRN_VAL_DIM), jnp.log(f).reshape(shp_k))
    o = head_rms_norm(o, out_norm) * jax.nn.silu(g.astype(jnp.float32)).reshape(B, T, HGRN_HEADS, HGRN_VAL_DIM)
    return o.reshape(B, T, HGRN_HEADS * HGRN_VAL_DIM).astype(h.dtype) @ w_out

def swiglu_ffn(h, w_gate_up, w_down):
    gu = h @ w_gate_up
    return (jax.nn.silu(gu[..., :D_FF]) * gu[..., D_FF:]) @ w_down

def second_inputs(seed: int = 0) -> dict:
    key = jax.random.key(seed)
    ks = jax.random.split(key, 20)
    n_a, n_b, n_c, n_d = [(DEPTH - kind + N_MIXERS - 1) // N_MIXERS for kind in range(N_MIXERS)]

    def normal(k, shape):
        return jax.random.normal(k, shape, jnp.float32)

    def dense(k, shape, fan_in):
        return normal(k, shape) * (fan_in ** -0.5)

    def gain(k, shape):
        return 1.0 + 0.02 * normal(k, shape)

    return {
        'x': normal(ks[0], (BATCH, SEQ, D_MODEL)),
        'norm_mix': gain(ks[1], (DEPTH, D_MODEL)),
        'norm_ffn': gain(ks[2], (DEPTH, D_MODEL)),
        'swa_w_in': dense(ks[3], (n_a, D_MODEL, ATTN_IN_DIM), D_MODEL),
        'swa_sinks': 0.5 * normal(ks[4], (n_a, N_Q_HEADS_2)),
        'swa_w_out': dense(ks[5], (n_a, ATTN_Q_DIM, D_MODEL), ATTN_Q_DIM),
        'moba_w_in': dense(ks[6], (n_b, D_MODEL, ATTN_IN_DIM), D_MODEL),
        'moba_w_out': dense(ks[7], (n_b, ATTN_Q_DIM, D_MODEL), ATTN_Q_DIM),
        'gla_w_in': dense(ks[8], (n_c, D_MODEL, GLA_IN_DIM), D_MODEL),
        'gla_w_decay_up': dense(ks[9], (n_c, GLA_GATE_RANK, GLA_HEADS * GLA_KEY_DIM), GLA_GATE_RANK),
        'gla_b_decay': 0.1 * normal(ks[10], (n_c, GLA_HEADS * GLA_KEY_DIM)),
        'gla_out_norm': gain(ks[11], (n_c, GLA_VAL_DIM)),
        'gla_w_out': dense(ks[12], (n_c, GLA_HEADS * GLA_VAL_DIM, D_MODEL), GLA_HEADS * GLA_VAL_DIM),
        'hgrn_w_in': dense(ks[13], (n_d, D_MODEL, HGRN_IN_DIM), D_MODEL),
        'hgrn_lb_logits': 0.5 * normal(ks[14], (DEPTH, HGRN_HEADS * HGRN_KEY_DIM)),
        'hgrn_out_norm': gain(ks[15], (n_d, HGRN_VAL_DIM)),
        'hgrn_w_out': dense(ks[16], (n_d, HGRN_HEADS * HGRN_VAL_DIM, D_MODEL), HGRN_HEADS * HGRN_VAL_DIM),
        'ffn_w_gate_up': dense(ks[17], (DEPTH, D_MODEL, 2 * D_FF), D_MODEL),
        'ffn_w_down': dense(ks[18], (DEPTH, D_FF, D_MODEL), D_FF),
        'final_norm': gain(ks[19], (D_MODEL,)),
    }

def second_block(x, norm_mix, norm_ffn, swa_w_in, swa_sinks, swa_w_out, moba_w_in, moba_w_out,
              gla_w_in, gla_w_decay_up, gla_b_decay, gla_out_norm, gla_w_out,
              hgrn_w_in, hgrn_lb_logits, hgrn_out_norm, hgrn_w_out,
              ffn_w_gate_up, ffn_w_down, final_norm):
    lb_p = jax.nn.softmax(hgrn_lb_logits.astype(jnp.float32), axis=0)
    lb_table = jnp.cumsum(lb_p, axis=0) - lb_p[0]
    for i in range(DEPTH):
        kind, j = i % N_MIXERS, i // N_MIXERS
        h = rms_norm(x, norm_mix[i])
        if kind == 0:
            mix = sliding_window_sink_attention(h, swa_w_in[j], swa_sinks[j], swa_w_out[j])
        elif kind == 1:
            mix = moba_attention(h, moba_w_in[j], moba_w_out[j])
        elif kind == 2:
            mix = gla_mixer(h, gla_w_in[j], gla_w_decay_up[j], gla_b_decay[j], gla_out_norm[j], gla_w_out[j])
        else:
            mix = hgrn2_mixer(h, hgrn_w_in[j], lb_table[i], hgrn_out_norm[j], hgrn_w_out[j])
        x = x + mix.astype(x.dtype)
        x = x + swiglu_ffn(rms_norm(x, norm_ffn[i]), ffn_w_gate_up[i], ffn_w_down[i]).astype(x.dtype)
    return rms_norm(x, final_norm)


def setup_inputs(seed=0):
    out = dict(first_inputs(seed))
    for name, value in second_inputs(seed + 1).items():
        if name != "x":
            out[name + "_2"] = value
    return out


def reference(
    x, c, ctx, c_ctx, w_mod, b_mod, norm1_g, norm2_g, w_in, q_norm_g, k_norm_g, w_attn_o,
    conv_dw, conv_b, conv_ln_g, conv_ln_b, w_conv_o, w_out, peer_wq, peer_keys, peer_u, peer_v,
    final_norm_g, norm_mix_2, norm_ffn_2, swa_w_in_2, swa_sinks_2, swa_w_out_2, moba_w_in_2,
    moba_w_out_2, gla_w_in_2, gla_w_decay_up_2, gla_b_decay_2, gla_out_norm_2, gla_w_out_2,
    hgrn_w_in_2, hgrn_lb_logits_2, hgrn_out_norm_2, hgrn_w_out_2, ffn_w_gate_up_2, ffn_w_down_2,
    final_norm_2,
):
    x = first_block(
        x, c, ctx, c_ctx, w_mod, b_mod, norm1_g, norm2_g, w_in, q_norm_g, k_norm_g, w_attn_o,
        conv_dw, conv_b, conv_ln_g, conv_ln_b, w_conv_o, w_out, peer_wq, peer_keys, peer_u,
        peer_v, final_norm_g,
    )
    return second_block(
        x, norm_mix_2, norm_ffn_2, swa_w_in_2, swa_sinks_2, swa_w_out_2, moba_w_in_2,
        moba_w_out_2, gla_w_in_2, gla_w_decay_up_2, gla_b_decay_2, gla_out_norm_2, gla_w_out_2,
        hgrn_w_in_2, hgrn_lb_logits_2, hgrn_out_norm_2, hgrn_w_out_2, ffn_w_gate_up_2,
        ffn_w_down_2, final_norm_2,
    )


_drawn_inputs = setup_inputs


def setup_inputs(seed=0):
    import zlib

    import numpy as np

    out = dict(_drawn_inputs(seed))
    spreads = {}
    factors = {'ctx': 4.949,
     'b_mod': 3.969,
     'norm1_g': 2.966,
     'q_norm_g': 8.0,
     'k_norm_g': 8.0,
     'conv_b': 8.0,
     'conv_ln_g': 3.062,
     'conv_ln_b': 8.0,
     'norm_mix_2': 5.83,
     'norm_ffn_2': 4.054,
     'swa_sinks_2': 30.808}
    for name, (base, spread) in spreads.items():
        noise = np.random.default_rng([zlib.crc32(name.encode()), seed]).standard_normal(out[name].shape)
        drawn = base * np.exp(spread * noise) if base else spread * noise
        out[name] = __import__('jax').numpy.asarray(drawn.astype(out[name].dtype))
    for name, factor in factors.items():
        out[name] = (out[name] * factor).astype(out[name].dtype)
    return out
```

```python
from contextlib import ExitStack

import concourse.bass as bass
from concourse import mybir

F32 = mybir.dt.float32
F32R = mybir.dt.float32r
BF16 = mybir.dt.bfloat16
U32 = mybir.dt.uint32
ACT = mybir.ActivationFunctionType
ALU = mybir.AluOpType
AX = mybir.AxisListType

P = 128
D = 1024
KT = D // P
T = 512
TT = T // P
CTX = 256
S1 = T + CTX
ST = S1 // P
NH, NKV = 8, 2
TAPS = 31
PAD = TAPS // 2
GW = T + 2 * PAD
HP = 16
PH = 8
TOPK = 16
NK = 128
NH2, NKV2, HD2 = 16, 4, 64
FF = 2816
FT = FF // P
EPS = 1e-6

MOD_N = 6 * KT
MOD = 0
U = MOD + MOD_N
KV = U + 2 * KT
Q = KV + 4
AO = Q + NH
CO = AO + 2 * KT
WO = CO + 2 * KT
WQ = WO + KT
EU = WQ + HP
EV = EU + NK
SW = EV + NK
SO = SW + 12
GU = SO + KT
DN = GU + 2 * FT
PANELS = DN + FT

RAW = 4
SPLIT = 2
BANKS = 4

SMALL = {}
_at = 0
for _name, _n in (("b_mod", MOD_N), ("norm1", KT), ("norm2", KT), ("final1", KT), ("conv_w", KT * TAPS),
                  ("conv_b", KT), ("ln_g", KT), ("ln_b", KT), ("q_g", 1), ("k_g", 1), ("mix", KT), ("ffn", KT),
                  ("final2", KT), ("c", 2 * KT), ("sinks", NH2), ("slopes", NH2), ("ident", P), ("ones", P),
                  ("perm", P), ("iota", P), ("zero", 1)):
    SMALL[_name] = (_at, _n)
    _at += _n
SMALL_N = _at

ARENA = 20736
A_G = 0
A_CONV = A_G + KT * GW
A_K = A_CONV + KT * T
A_V = A_K + NKV * S1
A_Q = A_V + ST * 2 * P
A_TMP = A_Q + NH * T
A_X = A_TMP + T
A_XCTX = A_X
A_COS = A_X
A_SIN = A_COS + T
A_QN = A_SIN + T
A_ROT = A_QN + 2 * T
A_P = A_X
A_PT = A_P + 2 * S1
A_M = A_X
A_XEND = A_X + 4608
assert A_XEND <= ARENA
A_S = 0
A_STAGE = (0, 8192)
A_V1 = 8192
A_I1 = A_V1 + 64 * TOPK
A_BS = A_I1 + 64 * TOPK
A_IJ = A_BS + 32 * TOPK
A_TK = A_IJ + 64 * TOPK
A_KEYS = A_TK + 2304
A_QK = 16384
A_TI = A_QK + 2 * T
A_TJ = A_TI + T
A_GE = A_TJ + T
A_BF = A_GE + 4 * T
assert A_KEYS + HP * P <= 16384 and A_BF + T // 2 <= ARENA
A_WR, A_GR, A_Z = 0, 4 * T, 8 * T
A_Q2 = 0
A_K2 = A_Q2 + 8 * T
A_V2 = A_K2 + 2 * T
A_DIST = A_V2 + TT * 2 * P
A_S2 = A_DIST + 2 * 256
A_PT2 = A_S2 + 2 * 1024
A_FF = 0


def build(nc, panels, small, xT_d, ctxT_d, rope_d, keys_d, dist_d, w_d, ge_d, out):
    with ExitStack() as ctx:
        def sb(name, shape, dt=F32):
            return ctx.enter_context(nc.sbuf_tensor(name, shape, dt))

        def sem(name):
            return ctx.enter_context(nc.semaphore(name))

        x = sb("x", [P, KT, T])
        raw = sb("raw", [P, RAW, D])
        whi = sb("whi", [P, SPLIT, D], F32R)
        wlo = sb("wlo", [P, SPLIT, D], F32R)
        a_hi = sb("a_hi", [P, KT, T], F32R)
        a_lo = sb("a_lo", [P, KT, T], F32R)
        b_hi = sb("b_hi", [P, KT, T], F32R)
        b_lo = sb("b_lo", [P, KT, T], F32R)
        sm = sb("sm", [P, SMALL_N])
        mod = sb("mod", [P, MOD_N, 2])
        gs1 = sb("gs1", [P, KT])
        gs1c = sb("gs1c", [P, KT])
        gs2 = sb("gs2", [P, KT])
        c_act = sb("c_act", [P, KT, 2])
        iota_b = sb("iota_b", [P, P], BF16)
        tiny = sb("tiny", [P, 64])
        sq = sb("sq", [P, 2, T])
        rstd = sb("rstd", [P, T])
        nt = sb("nt", [P, 2, T])
        ar = sb("ar", [P, ARENA])
        ps = ctx.enter_context(nc.psum_tensor("ps", [P, 8, T], F32))

        def area(at, *dims):
            n = 1
            for d in dims:
                n *= d
            v = ar[:, at:at + n]
            if len(dims) == 2:
                v = v.rearrange("p (a b) -> p a b", a=dims[0])
            elif len(dims) == 3:
                v = v.rearrange("p (a b c) -> p a b c", a=dims[0], b=dims[1])
            return v

        def col(name, i=0, n=1):
            at = SMALL[name][0] + i
            return sm[:, at:at + n]

        ident, ones, perm = col("ident", 0, P), col("ones", 0, P), col("perm", 0, P)
        f32 = lambda ap: ap.bitcast(F32)

        landed = [sem(f"landed{i}") for i in range(RAW)]
        hi_ready = sem("hi_ready")
        lo_ready = sem("lo_ready")
        used = sem("used")
        bank_free = sem("bank_free")
        small_in, x_in, ctx_in, rope_in, keys_in, dist_in = (
            sem(n) for n in ("small_in", "x_in", "ctx_in", "rope_in", "keys_in", "dist_in"))
        c_ready, mod_ready, mod_done = sem("c_ready"), sem("mod_ready"), sem("mod_done")
        sq_ready, sq_used, rt_ready, rstd_ready = (
            sem(n) for n in ("sq_ready", "sq_used", "rt_ready", "rstd_ready"))
        nt_ready, nhi_ready, h_ready = (sem(n) for n in ("nt_ready", "nhi_ready", "h_ready"))
        x_ready = sem("x_ready")
        gate_ready, pair_done = sem("gate_ready"), sem("pair_done")
        pad_ready, tap_done, pool_mul, pool_tap = (
            sem(n) for n in ("pad_ready", "tap_done", "pool_mul", "pool_tap"))
        ksq, kstat, krt, krstd, kn, krot, kcos, ksin, k_done = (
            sem(n) for n in ("ksq", "kstat", "krt", "krstd", "kn", "krot", "kcos", "ksin", "k_done"))
        v_feat_ready, v_turned, v_done = sem("v_feat_ready"), sem("v_turned"), sem("v_done")
        qs_ready, sc_ready, mx_ready, p_ready, rs_ready, pn_ready, pt_ready, pt_done, pv_ready, ohi_ready, o_ready = (
            sem(n) for n in ("qs_ready", "sc_ready", "mx_ready", "p_ready", "rs_ready", "pn_ready", "pt_ready",
                             "pt_done", "pv_ready", "ohi_ready", "o_ready"))
        cv_sum, cv_mu, cv_xc, cv_sq, cv_used, cv_var, cv_rt, cv_rstd, cv_t, cv_act, cv_hi, cv_ready = (
            sem(n) for n in ("cv_sum", "cv_mu", "cv_xc", "cv_sq", "cv_used", "cv_var", "cv_rt", "cv_rstd", "cv_t",
                             "cv_act", "cv_hi", "cv_ready"))
        co_mul = sem("co_mul")
        mhi_ready, m_ready = sem("mhi_ready"), sem("m_ready")
        qk_ready, s_ready, s_done = sem("qk_ready"), sem("s_ready"), sem("s_done")
        lv1, lv2, soft, soft_d, soft_e, ijw_t, ijw = (sem(n) for n in ("lv1", "lv2", "soft", "soft_d", "soft_e", "ijw_t", "ijw"))
        hot_ready, w_ready, w_staged = (sem(n) for n in ("hot_ready", "w_ready", "w_staged"))
        w_out = [sem(f"w_out{i}") for i in range(2)]
        ge_out = [sem(f"ge_out{i}") for i in range(4)]
        wg_in = [sem(f"wg_in{i}") for i in range(4)]
        z_ready, zhi_ready, zlo_ready, y_done = (sem(n) for n in ("z_ready", "zhi_ready", "zlo_ready", "y_done"))
        v2_feat, v2_turned, v2_done = sem("v2_feat"), sem("v2_turned"), sem("v2_done")
        sc2, bias2, mx2, nmx2, e2, snk2, den2, rec2, pn2, pt2, ptc2, pv2, ohi2, o2 = (
            sem(n) for n in ("sc2", "bias2", "mx2", "nmx2", "e2", "snk2", "den2", "rec2", "pn2", "pt2", "ptc2",
                             "pv2", "ohi2", "o2"))
        act_done, dhi_ready, dlo_ready, y2_done, out_done = (
            sem(n) for n in ("act_done", "dhi_ready", "dlo_ready", "y2_done", "out_done"))

        g_pad = area(A_G, KT, GW)
        conv = area(A_CONV, KT, T)
        kT = area(A_K, NKV, S1)
        v_tok = area(A_V, ST, 2 * P)
        qT = area(A_Q, NH, T)
        v_feat = area(A_Q, NKV, S1)
        q_slot = nt
        x_ctx = area(A_XCTX, KT, CTX)
        cos, sin = area(A_COS, T), area(A_SIN, T)
        q_n = area(A_QN, 2, T)
        q_rot = area(A_ROT, 2, T)
        prob = area(A_P, 2, S1)
        probT = area(A_PT, ST, T)
        merged = area(A_M, KT, T)
        scores = area(A_S, 64, NK)
        stage = [area(a, P, 64) for a in A_STAGE]
        v1, i1 = area(A_V1, 64, TOPK), area(A_I1, 64, TOPK)
        best = area(A_BS, 32, TOPK)
        ij = area(A_IJ, 2, 32 * TOPK)
        keys = area(A_KEYS, HP, P)
        q_key = area(A_QK, 2, T)
        tok_i, tok_j = area(A_TI, T), area(A_TJ, T)
        ge_slot = area(A_GE, 4, T)
        w_ring, ge_ring, z = area(A_WR, 4, T), area(A_GR, 4, T), area(A_Z, 2, T)
        hot = [v[:, :, :].rearrange("p a b -> p (a b)").bitcast(BF16).rearrange("p (t k n) -> p t k n", t=4, k=4)
               for v in (sq, nt)]
        tok_w = [q_key[:, 0, :], q_key[:, 1, :], rstd[:, :]]
        w_bf = area(A_BF, T // 2).bitcast(BF16)
        q2 = area(A_Q2, 8, T)
        k2 = area(A_K2, 2, T)
        v2 = area(A_V2, TT, 2 * P)
        v2_feat_sb = area(A_S2, 2, T)
        dist = area(A_DIST, 2, 256)
        s2 = area(A_S2, 2, 1024)
        p2T = area(A_PT2, 2, 512)
        hid = area(A_FF, FT, T)

        def r_of(g):
            return g - U if g < EV else g - U - NK


        block = ctx.enter_context(nc.Block())

        @block.sync
        def _(sp):
            sp.dma_start(sm[:, :], small).then_inc(small_in, 16)

            def load(g, u):
                sp.dma_start(raw[:, u, :], panels[g]).then_inc(landed[u], 16)

            def load_dyn(i, g0, u):
                sp.wait_ge(lo_ready, i * 4 + (g0 + u - RAW + 1 - U))
                send(i, g0, u)

            def send(i, g0, u):
                sp.dma_start(raw[:, u, :], panels[bass.ds(i * 4 + (g0 + u), 1)].rearrange("a p n -> (a p) n")).then_inc(landed[u], 16)

            for u in range(RAW):
                load(u, u)
            sp.dma_start(x[:, :, :], xT_d).then_inc(x_in, 16)
            sp.dma_start(x_ctx, ctxT_d).then_inc(ctx_in, 16)
            with sp.Fori(0, U // 4) as i:
                for u in range(4):
                    sp.wait_ge(used, i * 4 + (u + 1))
                    send(i, RAW, u)
            with sp.Fori(0, (KV - U - RAW) // 4) as i:
                for u in range(4):
                    load_dyn(i, U + RAW, u)
            sp.wait_ge(h_ready, 2 * KT)
            sp.dma_start(area(A_COS, 2, T), rope_d).then_inc(rope_in, 16)
            with sp.Fori(0, (WQ - KV) // 4) as i:
                for u in range(4):
                    load_dyn(i, KV, u)
            for u in range(4):
                load_dyn(0, WQ, u)
            sp.wait_ge(h_ready, 3 * KT)
            sp.dma_start(keys, keys_d).then_inc(keys_in, 16)
            with sp.Fori(1, (EV - WQ) // 4) as i:
                for u in range(4):
                    load_dyn(i, WQ, u)
            for u in range(4):
                load_dyn(0, EV, u)
            for done in w_out:
                sp.wait_ge(done, 16 * 4)
            for done in ge_out:
                sp.wait_ge(done, 16 * (NK // 4))

            def load_wg(i, u):
                sp.dma_start(w_ring[:, u, :], w_d[bass.ds(i * 4 + u, 1)].rearrange("a p n -> (a p) n")).then_inc(wg_in[u], 16)
                sp.dma_start(ge_ring[:, u, :], ge_d[bass.ds(i * 4 + u, 1)].rearrange("a p n -> (a p) n")).then_inc(wg_in[u], 16)

            for u in range(4):
                load_wg(0, u)
            with sp.Fori(1, NK // 4) as i:
                for u in range(4):
                    load_dyn(i, EV, u)
                    sp.wait_ge(z_ready, i * 4 + (u - 4 + 1))
                    load_wg(i, u)
            sp.wait_ge(z_ready, NK)
            sp.dma_start(area(A_DIST, 2, 256), dist_d).then_inc(dist_in, 16)
            with sp.Fori(0, (PANELS - SW) // 4) as i:
                for u in range(4):
                    load_dyn(i, SW, u)
            for u in range((PANELS - SW) % 4):
                load_dyn(0, PANELS - 2, u)
            sp.wait_ge(out_done, KT)
            sp.dma_start(out, x[:, :, :]).then_inc(x_in, 16)
            sp.wait_ge(x_in, 32)

        @block.tensor
        def _(pe):
            def panel(g, u, bank, hi, lo, free):
                pe.wait_ge(lo_ready, g + (1 - U))
                if free is not None:
                    pe.wait_ge(bank_free, free)
                for k in range(KT):
                    w_h = whi[:, u % SPLIT, k * P:(k + 1) * P]
                    w_l = wlo[:, u % SPLIT, k * P:(k + 1) * P]
                    pe.matmul(bank, w_h, hi[:, k, :], start=(k == 0), stop=False)
                    pe.matmul(bank, w_h, lo[:, k, :], start=False, stop=False)
                    last = pe.matmul(bank, w_l, hi[:, k, :], start=False, stop=(k == KT - 1))
                last.then_inc(used, 1)

            def strips(first, count, hi, lo, after=None):
                with pe.Fori(0, count // 4) as i:
                    for u in range(4):
                        panel(i * 4 + (first + u), u, ps[:, u, :], hi, lo, i * 4 + (r_of(first) + u + 1))
                        if after:
                            after(i, u)
                    if after:
                        after(i, 4)

            def norm_stats(n, src_width=T):
                for k in range(KT):
                    pe.wait_ge(sq_ready, n * KT + k + 1)
                    pe.matmul(ps[:, 4, 0:src_width], ones, sq[:, k % 2, 0:src_width], start=(k == 0),
                              stop=(k == KT - 1)).then_inc(sq_used, 1)

            pe.wait_ge(c_ready, 1)
            with pe.Fori(0, MOD_N // 4) as i:
                for u in range(4):
                    pe.wait_ge(landed[u], i * 16 + 16)
                    for k in range(KT):
                        last = pe.matmul(ps[:, 7, bass.ds(i * 8 + 2 * u, 2)], raw[:, u, k * P:(k + 1) * P], c_act[:, k, :],
                                         start=(k == 0), stop=(k == KT - 1))
                    last.then_inc(used, 1)
            norm_stats(0)
            pe.wait_ge(rt_ready, 1)
            norm_stats(1, CTX)

            pe.wait_ge(h_ready, KT)
            strips(U, 2 * KT, a_hi, a_lo)

            def split3(bank, wu, k, hi, lo, first, last):
                w_h = whi[:, wu % SPLIT, k * P:(k + 1) * P]
                w_l = wlo[:, wu % SPLIT, k * P:(k + 1) * P]
                pe.matmul(bank, w_h, hi, start=first, stop=False)
                pe.matmul(bank, w_h, lo, start=False, stop=False)
                return pe.matmul(bank, w_l, hi, start=False, stop=last)

            def head_stats(n, width=T):
                pe.wait_ge(ksq, n + 1)
                if n:
                    pe.wait_ge(krt, n)
                pe.matmul(ps[:, 4, 0:width], ones, sq[:, n % 2, 0:width], start=True, stop=True).then_inc(kstat, 1)

            def head_rot(n, m):
                pe.wait_ge(kn, n + 1)
                if m:
                    pe.wait_ge(ksin, m)
                pe.matmul(ps[:, 5, :], perm, q_n[:, n % 2, :], start=True, stop=True).then_inc(krot, 1)

            pe.wait_ge(h_ready, 2 * KT)
            for u in range(4):
                g = KV + u
                pe.wait_ge(lo_ready, g + (1 - U))
                pe.wait_ge(bank_free, r_of(g) + 1)
                for k in range(KT):
                    split3(ps[:, u, :], u, k, a_hi[:, k, :], a_lo[:, k, :], k == 0, k == KT - 1)
                for k in range(KT):
                    last = split3(ps[:, 6 + u // 2, u % 2 * CTX:(u % 2 + 1) * CTX], u, k, b_hi[:, k, 0:CTX], b_lo[:, k, 0:CTX], k == 0, k == KT - 1)
                last.then_inc(used, 1)
            for u in range(2):
                head_stats(2 * u)
                head_stats(2 * u + 1, CTX)
                head_rot(2 * u, u)
            for u in range(2):
                pe.wait_ge(v_feat_ready, 2 * (u + 1))
                pe.wait_ge(ksin, 2)
                if u:
                    pe.wait_ge(v_done, 1)
                for s in range(ST):
                    last = pe.transpose(ps[:, 4 + s // 3, (s % 3) * P:(s % 3 + 1) * P],
                                        v_feat[:, u, s * P:(s + 1) * P], ident)
                last.then_inc(v_turned, 1)

            def q_after(i, u):
                for v in ((u - 1,) if 0 < u < 4 else (3,) if u == 4 else ()):
                    n = i * 4 + (4 + v)
                    pe.wait_ge(ksq, n + 1)
                    pe.wait_ge(krt, n)
                    pe.matmul(ps[:, 4, :], ones, sq[:, v % 2, :], start=True, stop=True).then_inc(kstat, 1)
                    pe.wait_ge(kn, n + 1)
                    pe.wait_ge(ksin, i * 4 + (2 + v))
                    pe.matmul(ps[:, 5, :], perm, q_n[:, v % 2, :], start=True, stop=True).then_inc(krot, 1)

            strips(Q, NH, a_hi, a_lo, q_after)

            pe.wait_ge(k_done, NKV + NH)
            pe.wait_ge(v_done, NKV)
            pe.wait_ge(bank_free, r_of(AO) + 4)

            def att_scores(i, hu, t):
                n = (i * 2 + hu) * TT + t
                b = 2 * (t % 2)
                kv = ATT_KV[0]
                pe.matmul(ps[:, b, :], q_slot[:, hu, t * P:(t + 1) * P], kT[:, kv, 0:T], start=True, stop=True)
                pe.matmul(ps[:, b + 1, 0:CTX], q_slot[:, hu, t * P:(t + 1) * P], kT[:, kv, T:S1], start=True,
                          stop=True).then_inc(sc_ready, 1)

            ATT_KV = [0]
            for half in range(NKV):
                ATT_KV[0] = half
                with pe.Fori(2 * half, 2 * half + 2) as i:
                    for hu in range(2):
                        h = i * 2 + hu
                        pe.wait_ge(qs_ready, h + 1)
                        att_scores(i, hu, 0)
                        for t in range(TT):
                            n = h * TT + t
                            if t + 1 < TT:
                                att_scores(i, hu, t + 1)
                            pe.wait_ge(pn_ready, n + 1)
                            if t:
                                pe.wait_ge(pt_done, n)
                            for s in range(ST):
                                last = pe.transpose(ps[:, 4 + s // 3, (s % 3) * P:(s % 3 + 1) * P],
                                                    prob[:, t % 2, s * P:(s + 1) * P], ident)
                            last.then_inc(pt_ready, 1)
                        pe.wait_ge(pt_done, (h + 1) * TT)
                        for s in range(ST):
                            last = pe.matmul(ps[:, 6 + hu, :], v_tok[:, s, half * P:(half + 1) * P], probT[:, s, :],
                                             start=(s == 0), stop=(s == ST - 1))
                        last.then_inc(pv_ready, 1)

            pe.wait_ge(o_ready, NH)
            with pe.Fori(0, 2 * KT // 4) as i:
                for u in range(4):
                    hi, lo = (a_hi, a_lo) if u % 2 == 0 else (b_hi, b_lo)
                    panel(i * 4 + (AO + u), u, ps[:, u, :], hi, lo, i * 4 + (r_of(AO) + u + 1))

            pe.wait_ge(tap_done, 4 * TAPS)
            pe.wait_ge(pool_tap, 4 * TAPS)
            for k in range(KT):
                last = pe.matmul(ps[:, 4, :], ones, conv[:, k, :], start=(k == 0), stop=(k == KT - 1))
            last.then_inc(cv_sum, 1)
            for k in range(KT):
                pe.wait_ge(cv_sq, k + 1)
                pe.matmul(ps[:, 5, :], ones, sq[:, k % 2, :], start=(k == 0), stop=(k == KT - 1)).then_inc(cv_used, 1)

            pe.wait_ge(cv_ready, KT)
            with pe.Fori(0, 2 * KT // 4) as i:
                for u in range(4):
                    hi, lo = (a_hi, a_lo) if u % 2 == 0 else (b_hi, b_lo)
                    panel(i * 4 + (CO + u), u, ps[:, u, :], hi, lo, i * 4 + (r_of(CO) + u + 1))
            pe.wait_ge(m_ready, KT)
            strips(WO, KT, a_hi, a_lo)

            norm_stats(2)
            pe.wait_ge(h_ready, 3 * KT)
            pe.wait_ge(keys_in, 16)

            def key_scores(i, u):
                for v in ((u - 1,) if 0 < u < 4 else (3,) if u == 4 else ()):
                    pe.wait_ge(qk_ready, i * 4 + (v + 1))
                    for t in range(TT):
                        last = pe.matmul(ps[:, 4 + v, t * P:(t + 1) * P], q_key[:, v % 2, t * P:(t + 1) * P],
                                         keys[:, bass.ds(i * 4 + v, 1), :], start=True, stop=True)
                    last.then_inc(s_ready, 1)

            strips(WQ, HP, b_hi, b_lo, key_scores)

            strips(EU, NK // 2, b_hi, b_lo)

            pe.wait_ge(soft, 1)
            for a in range(3):
                src = ij[:, a, :] if a < 2 else best.rearrange("p a b -> p (a b)")
                for t in range(TT):
                    last = pe.transpose(ps[:, 4 + a, t * P:(t + 1) * P], src[:, t * P:(t + 1) * P], ident)
            last.then_inc(ijw_t, 1)

            def token_w(i, u):
                if u == 4:
                    return
                for v in range(2):
                    n = i * 8 + (2 * u + v)
                    pe.wait_ge(hot_ready, n + 1)
                    if v + 2 * u >= 4:
                        pe.wait_ge(w_ready, n - 3)
                    bank = 4 + (2 * u + v) % 4
                    for t in range(4):
                        for c in range(1, 4):
                            last = pe.matmul(ps[:, bank, t * P:(t + 1) * P], hot[v][:, t, 0, :], hot[v][:, t, c, :],
                                             start=(c == 1), stop=(c == 3))
                    last.then_inc(w_staged, 1)

            strips(EU + NK // 2, NK // 2, b_hi, b_lo, token_w)

            pe.wait_ge(bank_free, r_of(EU) + NK + 4)
            pe.wait_ge(w_ready, P)

            def rows(g, u, n, zsem, hi, lo, slot, start, stop, nsem):
                pe.wait_ge(lo_ready, g + (1 - U))
                pe.wait_ge(zsem, n + 1)
                for d in range(KT):
                    w_h = whi[:, u % SPLIT, d * P:(d + 1) * P]
                    w_l = wlo[:, u % SPLIT, d * P:(d + 1) * P]
                    pe.matmul(ps[:, d, :], w_h, hi[:, slot, :], start=start, stop=False)
                    pe.matmul(ps[:, d, :], w_h, lo[:, slot, :], start=False, stop=False)
                    last = pe.matmul(ps[:, d, :], w_l, hi[:, slot, :], start=False, stop=stop)
                last.then_inc(used, 1)

            for u in range(4):
                rows(EV + u, u, u, zlo_ready, a_hi, a_lo, u, u == 0, False, None)
            with pe.Fori(1, NK // 4 - 1) as i:
                for u in range(4):
                    rows(i * 4 + (EV + u), u, i * 4 + u, zlo_ready, a_hi, a_lo, u, False, False, None)
            for u in range(4):
                n = NK - 4 + u
                rows(EV + n, u, n, zlo_ready, a_hi, a_lo, u, False, n == NK - 1, None)

            pe.wait_ge(y_done, KT)
            norm_stats(3)
            norm_stats(4)
            pe.wait_ge(h_ready, 4 * KT)

            for u in range(4):
                panel(SW + u, u, ps[:, u, :], a_hi, a_lo, r_of(SW) + u + 1)
            for u in range(2):
                pe.wait_ge(v2_feat, u + 1)
                for s in range(TT):
                    last = pe.transpose(ps[:, 4 + u, s * P:(s + 1) * P], v2_feat_sb[:, u, s * P:(s + 1) * P], ident)
                last.then_inc(v2_turned, 1)
            strips(SW + 4, 8, a_hi, a_lo)

            pe.wait_ge(bank_free, r_of(SO) + 4)
            pe.wait_ge(v2_done, 2)
            groups = [(b, kt, half) for b in range(TT) for kt in range(2) for half in range(2)]

            def swa_scores(n):
                b, kt, half = groups[n]
                rows_ = slice(half * HD2, (half + 1) * HD2)
                if n >= 2:
                    pe.wait_ge(bias2, 4 * (n - 1))
                for r in range(4):
                    dst = ps[:, 2 * (n % 2) + r // 2, (r % 2) * 256 + (P if b == 0 else 0):(r % 2) * 256 + 256]
                    last = pe.matmul(dst, q2[rows_, kt * 4 + r, b * P:(b + 1) * P],
                                     k2[rows_, kt, max(b - 1, 0) * P:(b + 1) * P], start=True, stop=True)
                last.then_inc(sc2, 1)

            def swa_values(n):
                b, kt, half = groups[n]
                tiles = (1,) if b == 0 else (0, 1)
                pe.wait_ge(pn2, n + 1)
                if n:
                    pe.wait_ge(ptc2, n)
                for s in tiles:
                    for r in range(4):
                        last = pe.transpose(ps[:, 4 + s, r * P:(r + 1) * P], s2[:, n % 2, r * 256 + s * P:r * 256 + (s + 1) * P], ident)
                last.then_inc(pt2, 1)
                pe.wait_ge(ptc2, n + 1)
                if n >= 2:
                    pe.wait_ge(o2, n - 1)
                rows_ = slice(half * HD2, (half + 1) * HD2)
                kv = 2 * kt + half
                for s in tiles:
                    last = pe.matmul(ps[rows_, 6 + n % 2, :], v2[:, b - 1 + s, kv * HD2:(kv + 1) * HD2], p2T[:, s, :],
                                     start=(s == tiles[0]), stop=(s == 1))
                last.then_inc(pv2, 1)

            swa_scores(0)
            for n in range(len(groups)):
                if n + 1 < len(groups):
                    swa_scores(n + 1)
                swa_values(n)

            pe.wait_ge(o2, len(groups))
            strips(SO, KT, b_hi, b_lo)
            norm_stats(5)
            pe.wait_ge(h_ready, 5 * KT)
            strips(GU, 2 * FT, a_hi, a_lo)
            pe.wait_ge(bank_free, r_of(DN) + 4)
            for u in range(4):
                rows(DN + u, u, u, dlo_ready, b_hi, b_lo, u, u == 0, False, None)
            with pe.Fori(1, FT // 4) as i:
                for u in range(4):
                    rows(i * 4 + (DN + u), u, i * 4 + u, dlo_ready, b_hi, b_lo, u, False, False, None)
            for u in range(FT % 4):
                n = FT - FT % 4 + u
                rows(DN + n, u, n, dlo_ready, b_hi, b_lo, u, False, n == FT - 1, None)
            pe.wait_ge(y2_done, KT)
            norm_stats(6)

        @block.scalar
        def _(act):
            def hi(g, u, i=None):
                act.wait_ge(landed[u % RAW], (g // 4 + 1) * 16 if i is None else i)
                act.wait_ge(used, g - SPLIT + 1)
                act.activation(whi[:, u % SPLIT, :], raw[:, u % RAW, :], ACT.Copy).then_inc(hi_ready, 1)

            def hi_next(i, first, u):
                hi(i * 4 + (first + u + 1), u + 1, (i + (first + u + 1) // 4 + 1) * 16)

            def step(i, first, u):
                hi_next(i, first, u)
                act.wait_ge(used, i * 4 + (first + u + 1))

            def norm_sq(n, src, width=T):
                for k in range(KT):
                    if n or k >= 2:
                        act.wait_ge(sq_used, n * KT + k - 1)
                    act.activation(sq[:, k % 2, 0:width], src[:, k, 0:width], ACT.Square).then_inc(sq_ready, 1)
                act.wait_ge(sq_used, (n + 1) * KT)
                act.activation(rstd[:, 0:width], ps[:, 4, 0:width], ACT.Sqrt, bias=EPS, scale=1.0 / D).then_inc(rt_ready, 1)

            def norm_hi(n, dst, shift, width=T):
                for k in range(KT):
                    act.wait_ge(nt_ready, n * KT + k + 1)
                    act.activation(dst[:, k, 0:width], nt[:, k % 2, 0:width], ACT.Identity, bias=shift(k)).then_inc(nhi_ready, 1)

            act.wait_ge(small_in, 16)
            c_in = col("c", 0, 2 * KT).rearrange("p (a b) -> p a b", b=2)
            act.activation(c_act[:, :, :], c_in, ACT.Silu).then_inc(c_ready, 1)
            act.wait_ge(x_in, 16)
            norm_sq(0, x)
            norm_hi(0, a_hi, lambda k: mod[:, k, 0:1])
            act.wait_ge(ctx_in, 16)
            act.wait_ge(h_ready, KT)
            norm_sq(1, x_ctx, CTX)
            norm_hi(1, b_hi, lambda k: mod[:, k, 1:2], CTX)
            hi(U, 0)

            def gates(first, count, bank_of):
                with act.Fori(0, count // 4) as i:
                    for u in range(4):
                        step(i, first, u)
                        if u % 2:
                            act.activation(sq[:, u // 2, :], ps[:, bank_of(u), :], ACT.Sigmoid).then_inc(gate_ready, 1)

            gates(U, 2 * KT, lambda u: u)

            def head_sq(n, src, width=T):
                act.activation(sq[:, n % 2, 0:width], src, ACT.Square).then_inc(ksq, 1)

            def head_rt(n, width=T):
                act.wait_ge(kstat, n + 1)
                act.activation(rstd[:, 0:width], ps[:, 4, 0:width], ACT.Sqrt, bias=EPS, scale=1.0 / P).then_inc(krt, 1)

            for u in range(4):
                hi_next(0, KV, u)
            act.wait_ge(used, KV + 2)
            for u in range(2):
                if u:
                    act.wait_ge(kn, 2)
                head_sq(2 * u, ps[:, u, :])
                head_sq(2 * u + 1, ps[:, 6, u * CTX:(u + 1) * CTX], CTX)
                for n, w in ((2 * u, T), (2 * u + 1, CTX)):
                    if n:
                        act.wait_ge(kn, n)
                    head_rt(n, w)
            with act.Fori(0, NH // 4) as i:
                for u in range(5):
                    if u < 4:
                        step(i, Q, u)
                        head_sq(u, ps[:, u, :])
                        act.wait_ge(kstat, i * 4 + (4 + u + 1))
                        act.wait_ge(kn, i * 4 + (4 + u))
                        act.activation(rstd[:, :], ps[:, 4, :], ACT.Sqrt, bias=EPS, scale=1.0 / P).then_inc(krt, 1)

            def att(i, hu, t):
                n = (i * 2 + hu) * TT + t
                act.wait_ge(mx_ready, n + 1)
                act.activation(prob[:, t % 2, :], ps[:, 2 * (t % 2):2 * (t % 2) + 2, :].rearrange("p a b -> p (a b)")[:, 0:S1],
                               ACT.Exp, bias=tiny[:, t:t + 1], scale=P ** -0.5, accum_out=tiny[:, 8 + t:9 + t]).then_inc(p_ready, 1)

            def att_T(i, hu, t):
                n = (i * 2 + hu) * TT + t
                act.wait_ge(pt_ready, n + 1)
                act.activation(probT[:, :, t * P:(t + 1) * P].rearrange("p (a s) n -> p a s n", a=2),
                               ps[:, 4:6, 0:3 * P].rearrange("p a (s n) -> p a s n", n=P), ACT.Copy).then_inc(pt_done, 1)

            with act.Fori(0, NH // 2) as i:
                for hu in range(2):
                    att(i, hu, 0)
                    for t in range(TT):
                        if t + 1 < TT:
                            att(i, hu, t + 1)
                        att_T(i, hu, t)
                    act.wait_ge(pv_ready, i * 2 + (hu + 1))
                    act.activation(b_hi[:, bass.ds(i * 2 + hu, 1), :], ps[:, 6 + hu, :], ACT.Copy).then_inc(ohi_ready, 1)

            gates(AO, 2 * KT, lambda u: u - 1)

            for k in range(KT):
                act.wait_ge(cv_xc, k + 1)
                if k >= 2:
                    act.wait_ge(cv_used, k - 1)
                act.activation(sq[:, k % 2, :], conv[:, k, :], ACT.Square).then_inc(cv_sq, 1)
            act.wait_ge(cv_used, KT)
            act.activation(rstd[:, :], ps[:, 5, :], ACT.Sqrt, bias=EPS, scale=1.0 / D).then_inc(cv_rt, 1)
            for k in range(KT):
                act.wait_ge(cv_t, k + 1)
                if k >= 2:
                    act.wait_ge(cv_ready, k - 1)
                act.activation(sq[:, k % 2, :], nt[:, k % 2, :], ACT.Silu, bias=col("ln_b", k), scale=col("ln_g", k)).then_inc(cv_act, 1)
                act.wait_ge(cv_act, k + 1)
                act.activation(b_hi[:, k, :], sq[:, k % 2, :], ACT.Copy).then_inc(cv_hi, 1)

            gates(CO, 2 * KT, lambda u: u - 1)
            act.wait_ge(used, WO)
            for k in range(KT):
                act.wait_ge(pair_done, KT + k + 1)
                act.activation(a_hi[:, k, :], merged[:, k, :], ACT.Copy).then_inc(mhi_ready, 1)

            def only_panels(first, count):
                with act.Fori(0, count // 4) as i:
                    for u in range(4):
                        hi_next(i, first, u)

            only_panels(WO, KT)
            act.wait_ge(x_ready, KT)
            norm_sq(2, x)
            norm_hi(2, b_hi, lambda k: mod[:, 3 * KT + k, 0:1])

            with act.Fori(0, HP // 4) as i:
                for u in range(4):
                    step(i, WQ, u)
                    act.activation(q_key[:, u % 2, :], ps[:, u, :], ACT.Copy)\
                       .then_inc(bank_free, 1)
                    act.wait_ge(bank_free, i * 4 + (4 + r_of(WQ) + u + 1))
                    act.sem_inc(qk_ready, 1)

            def gelu(i, u):
                hi_next(i, EU, u)
                act.wait_ge(used, i * 4 + (EU + u + 1))
                if not isinstance(i, int) or i:
                    act.wait_ge(ge_out[u], i * 16)
                act.activation(ge_slot[:, u, :], ps[:, u, :], ACT.Gelu).then_inc(bank_free, 1)
                act.wait_ge(bank_free, i * 4 + (4 + r_of(EU) + u + 1))
                act.dma_start(ge_d[bass.ds(i * 4 + u, 1)].rearrange("a p n -> (a p) n"), ge_slot[:, u, :]).then_inc(ge_out[u], 16)

            for u in range(4):
                gelu(0, u)
            with act.Fori(1, NK // 8) as i:
                for u in range(4):
                    gelu(i, u)
            act.wait_ge(soft_d, 1)
            act.activation(best, best, ACT.Exp).then_inc(soft_e, 1)

            def stage_w(j, chunk, c, u):
                for v in range(2):
                    batch = 8 * c + 2 * u + v
                    act.wait_ge(w_staged, j * 32 + (chunk * 16 + batch + 1))
                    act.activation(stage[chunk][:, :, batch * 4:batch * 4 + 4],
                                   ps[:, 4 + batch % 4, :].rearrange("p (t k) -> p k t", t=4), ACT.Copy).then_inc(w_ready, 1)

            def chunks(j):
                for chunk in range(2):
                    for c in range(2):
                        for u in range(4):
                            gelu(j * 4 + (NK // 8 + 2 * chunk + c), u)
                            if c == u == 0 and (not isinstance(j, int) or j):
                                act.wait_ge(w_out[chunk], j * 16)
                            stage_w(j, chunk, c, u)
                    act.wait_ge(w_ready, j * 32 + (chunk + 1) * 16)
                    act.dma_start(w_d.rearrange("i j (c t) -> c j i t", t=64)[bass.ds(j * 2 + chunk, 1)].rearrange("c j i t -> (c j) i t"),
                                  stage[chunk]).then_inc(w_out[chunk], 16)

            chunks(0)
            with act.Fori(1, 4) as j:
                chunks(j)

            def z_hi(i, u):
                n = i * 4 + u
                act.wait_ge(z_ready, n + 1)
                if not isinstance(i, int) or i:
                    act.wait_ge(used, n + (EV - 4 + 1))
                act.activation(a_hi[:, u, :], z[:, u % 2, :], ACT.Copy).then_inc(zhi_ready, 1)

            for u in range(4):
                hi_next(0, EV, u)
                z_hi(0, u)
            with act.Fori(1, NK // 4) as i:
                for u in range(4):
                    hi_next(i, EV, u)
                    z_hi(i, u)

            act.wait_ge(y_done, KT)
            norm_sq(3, x)
            act.wait_ge(x_ready, 2 * KT)
            norm_sq(4, x)
            norm_hi(3, a_hi, lambda k: col("zero"))
            only_panels(SW, 12)

            groups = [(b, kt, half) for b in range(TT) for kt in range(2) for half in range(2)]

            def swa_exp(n):
                o = 32 * (n % 2)
                act.wait_ge(nmx2, n + 1)
                for r in range(4):
                    last = act.activation(s2[:, n % 2, r * 256:(r + 1) * 256], s2[:, n % 2, r * 256:(r + 1) * 256], ACT.Exp,
                                          bias=tiny[:, o + 4 + r:o + 5 + r], accum_out=tiny[:, o + 8 + r:o + 9 + r])
                    last.then_inc(e2, 1)
                for r in range(4):
                    h = 8 * groups[n][1] + 4 * groups[n][2] + r
                    act.activation(tiny[:, o + 12 + r:o + 13 + r], col("sinks", h), ACT.Exp, bias=tiny[:, o + 4 + r:o + 5 + r]).then_inc(snk2, 1)

            def swa_out(n):
                b, kt, half = groups[n]
                act.wait_ge(pt2, n + 1)
                if b == 0:
                    act.activation(p2T[:, 1, :], ps[:, 5, :], ACT.Copy).then_inc(ptc2, 1)
                else:
                    act.activation(p2T[:, :, :], ps[:, 4:6, :], ACT.Copy).then_inc(ptc2, 1)
                act.wait_ge(pv2, n + 1)
                rows_ = slice(half * HD2, (half + 1) * HD2)
                act.activation(b_hi[rows_, kt * 4:kt * 4 + 4, b * P:(b + 1) * P],
                               ps[rows_, 6 + n % 2, :].rearrange("p (r t) -> p r t", r=4), ACT.Copy).then_inc(ohi2, 1)

            swa_exp(0)
            for n in range(len(groups)):
                if n + 1 < len(groups):
                    swa_exp(n + 1)
                swa_out(n)

            only_panels(SO, KT)
            act.wait_ge(x_ready, 3 * KT)
            norm_sq(5, x)
            norm_hi(4, a_hi, lambda k: col("zero"))
            with act.Fori(0, 2 * FT // 4) as i:
                for u in range(4):
                    step(i, GU, u)
                    if u % 2 == 0:
                        act.activation(sq[:, u // 2, :], ps[:, u, :], ACT.Silu).then_inc(gate_ready, 1)

            def hid_hi(i, u):
                n = i * 4 + u
                if not isinstance(i, int) or i:
                    act.wait_ge(used, n + (DN - 4 + 1))
                act.activation(b_hi[:, u, :], hid[:, bass.ds(n, 1), :] if not isinstance(n, int) else hid[:, n, :],
                               ACT.Copy).then_inc(dhi_ready, 1)

            act.wait_ge(act_done, FT)
            for u in range(4):
                hi_next(0, DN, u)
                hid_hi(0, u)
            with act.Fori(1, FT // 4) as i:
                for u in range(4):
                    hi_next(i, DN, u)
                    hid_hi(i, u)
            hi_next(FT // 4, DN, 0)
            for u in range(FT % 4):
                hid_hi(FT // 4, u)
            act.wait_ge(y2_done, KT)
            norm_sq(6, x)

        @block.vector
        def _(dve):
            def lo(g, u):
                dve.wait_ge(hi_ready, g + (1 - U))
                dve.tensor_tensor(wlo[:, u % SPLIT, :], raw[:, u % RAW, :], f32(whi[:, u % SPLIT, :]), ALU.subtract).then_inc(lo_ready, 1)

            def lo_next(i, first, u):
                lo(i * 4 + (first + u + 1), u + 1)

            def step(i, first, u):
                lo_next(i, first, u)
                dve.wait_ge(used, i * 4 + (first + u + 1))

            def norm_rstd(n, width=T):
                dve.wait_ge(rt_ready, n + 1)
                dve.reciprocal(rstd[:, 0:width], rstd[:, 0:width]).then_inc(rstd_ready, 1)
                dve.wait_ge(rstd_ready, n + 1)

            def norm_apply(m, src, gain, shift, hi_, lo_, width=T):
                def low(k):
                    dve.wait_ge(nhi_ready, m * KT + k + 1)
                    dve.scalar_tensor_tensor(lo_[:, k, 0:width], nt[:, k % 2, 0:width], shift(k), f32(hi_[:, k, 0:width]),
                                             ALU.add, ALU.subtract).then_inc(h_ready, 1)
                for k in range(KT):
                    if k >= 2:
                        low(k - 2)
                        dve.wait_ge(h_ready, m * KT + k - 1)
                    elif m:
                        dve.wait_ge(h_ready, m * KT)
                    dve.scalar_tensor_tensor(nt[:, k % 2, 0:width], src[:, k, 0:width], gain(k), rstd[:, 0:width],
                                             ALU.mult, ALU.mult).then_inc(nt_ready, 1)
                low(KT - 2)
                low(KT - 1)

            dve.wait_ge(used, U)
            dve.tensor_tensor(mod[:, :, :], ps[:, 7, 0:2 * MOD_N].rearrange("p (n c) -> p n c", c=2),
                              col("b_mod", 0, MOD_N).unsqueeze(2).to_broadcast([P, MOD_N, 2]), ALU.add).then_inc(mod_done, 1)
            dve.wait_ge(mod_done, 1)
            for dst, at, c, gname in ((gs1, KT, 0, "norm1"), (gs1c, KT, 1, "norm1"), (gs2, 4 * KT, 0, "norm2")):
                dve.scalar_tensor_tensor(dst[:, :], mod[:, at:at + KT, c], 1.0, col(gname, 0, KT), ALU.add, ALU.mult).then_inc(mod_done, 1)
            for _ in range(4):
                dve.sem_inc(bank_free, 1)
            dve.wait_ge(mod_done, 4)
            dve.wait_ge(x_in, 16)
            norm_rstd(0)
            norm_apply(0, x, lambda k: gs1[:, k:k + 1], lambda k: mod[:, k, 0:1], a_hi, a_lo)
            norm_rstd(1, CTX)
            norm_apply(1, x_ctx, lambda k: gs1c[:, k:k + 1], lambda k: mod[:, k, 1:2], b_hi, b_lo, CTX)

            def taps(i, lo_tap, hi_tap):
                for j in range(lo_tap, hi_tap):
                    n = i * TAPS + j
                    acc = conv[:, bass.ds(i * 2, 1), :]
                    src = g_pad[:, bass.ds(i * 2, 1), j:j + T]
                    w = sm[:, bass.ds(i * (2 * TAPS) + (SMALL["conv_w"][0] + j), 1)]
                    if j == 0:
                        b = sm[:, bass.ds(i * 2 + SMALL["conv_b"][0], 1)]
                        dve.tensor_scalar(acc, src, w, b, ALU.mult, ALU.add).then_inc(tap_done, 1)
                    else:
                        dve.wait_ge(tap_done, n)
                        dve.scalar_tensor_tensor(acc, src, w, acc, ALU.mult, ALU.add).then_inc(tap_done, 1)

            lo(U, 0)
            dve.wait_ge(pad_ready, 1)
            with dve.Fori(0, KT // 2) as i:
                for u in range(4):
                    step(i, U, u)
                    if u % 2:
                        p = i * 2 + u // 2
                        dve.wait_ge(gate_ready, p + 1)
                        dve.tensor_tensor(g_pad[:, bass.ds(p, 1), PAD:PAD + T], sq[:, u // 2, :], ps[:, u - 1, :],
                                          ALU.mult).then_inc(pair_done, 1)
                        dve.wait_ge(pair_done, p + 1)
                        dve.sem_inc(bank_free, 2)
                    if u:
                        taps(i, (u - 1) * 11, min(u * 11, TAPS))

            def head(n, m, src, gain, dst, width=T, rotate=True):
                dve.wait_ge(krt, n + 1)
                dve.reciprocal(rstd[:, 0:width], rstd[:, 0:width]).then_inc(krstd, 1)
                dve.wait_ge(krstd, n + 1)
                if not rotate:
                    return dve.scalar_tensor_tensor(dst, src, gain, rstd[:, 0:width], ALU.mult, ALU.mult).then_inc(kn, 1)
                dve.scalar_tensor_tensor(q_n[:, n % 2, :], src, gain, rstd[:, :], ALU.mult, ALU.mult).then_inc(kn, 1)

            def turn(n, m, slot, dst):
                dve.wait_ge(kn, n + 1)
                dve.tensor_tensor(q_rot[:, 0, :], q_n[:, slot, :], cos, ALU.mult).then_inc(kcos, 1)
                dve.wait_ge(krot, m + 1)
                dve.tensor_tensor(q_rot[:, 1, :], ps[:, 5, :], sin, ALU.mult).then_inc(ksin, 1)
                dve.wait_ge(kcos, m + 1)
                dve.wait_ge(ksin, m + 1)
                dve.tensor_tensor(dst, q_rot[:, 0, :], q_rot[:, 1, :], ALU.add).then_inc(k_done, 1)
                dve.wait_ge(k_done, m + 1)

            for u in range(4):
                lo_next(0, KV, u)
            dve.wait_ge(rope_in, 16)
            for u in range(2):
                dve.wait_ge(used, KV + 2)
                head(2 * u, u, ps[:, u, :], col("k_g"), None)
                head(2 * u + 1, u, ps[:, 6, u * CTX:(u + 1) * CTX], col("k_g"), kT[:, u, T:S1], CTX, False)
                dve.wait_ge(kn, 2 * u + 2)
                dve.sem_inc(bank_free, 1)
                turn(2 * u, u, 0, kT[:, u, 0:T])
            dve.wait_ge(used, KV + 4)
            for u in range(2):
                dve.tensor_copy(v_feat[:, u, 0:T], ps[:, 2 + u, :]).then_inc(v_feat_ready, 1)
                dve.tensor_copy(v_feat[:, u, T:S1], ps[:, 7, u * CTX:(u + 1) * CTX]).then_inc(v_feat_ready, 1)
            dve.wait_ge(v_feat_ready, 4)
            dve.sem_inc(bank_free, 2)
            for u in range(2):
                dve.wait_ge(v_turned, u + 1)
                dve.tensor_copy(v_tok[:, :, u * P:(u + 1) * P].rearrange("p (a s) n -> p a s n", a=2),
                                ps[:, 4:6, 0:3 * P].rearrange("p a (s n) -> p a s n", n=P)).then_inc(v_done, 1)
            with dve.Fori(0, NH // 4) as i:
                for u in range(4):
                    step(i, Q, u)
                    n = i * 4 + (4 + u)
                    m = i * 4 + (2 + u)
                    dve.wait_ge(krt, n + 1)
                    dve.reciprocal(rstd[:, :], rstd[:, :]).then_inc(krstd, 1)
                    dve.wait_ge(krstd, n + 1)
                    dve.scalar_tensor_tensor(q_n[:, u % 2, :], ps[:, u, :], col("q_g"), rstd[:, :], ALU.mult, ALU.mult).then_inc(kn, 1)
                    dve.wait_ge(kn, n + 1)
                    dve.sem_inc(bank_free, 1)
                    turn(n, m, u % 2, qT[:, bass.ds(i * 4 + u, 1), :])

            def att_max(i, hu, t):
                n = (i * 2 + hu) * TT + t
                dve.wait_ge(sc_ready, n + 1)
                dve.tensor_reduce(tiny[:, 4 + t:5 + t], ps[:, 2 * (t % 2):2 * (t % 2) + 2, :].rearrange("p a b -> p (a b)")[:, 0:S1],
                                  AX.X, ALU.max).then_inc(rs_ready, 1)
                dve.wait_ge(rs_ready, n * 3 + 1)

            def att_in(i, hu, t):
                n3 = ((i * 2 + hu) * TT + t) * 3
                dve.wait_ge(sc_ready, (i * 2 + hu) * TT + (t + 1))
                dve.tensor_reduce(tiny[:, 4 + t:5 + t], ps[:, 2 * (t % 2):2 * (t % 2) + 2, :].rearrange("p a b -> p (a b)")[:, 0:S1],
                                  AX.X, ALU.max).then_inc(rs_ready, 1)

            def att_neg(i, hu, t, done):
                dve.wait_ge(rs_ready, done)
                dve.tensor_scalar(tiny[:, t:t + 1], tiny[:, 4 + t:5 + t], -(P ** -0.5), None, ALU.mult).then_inc(mx_ready, 1)

            def att_norm(i, hu, t, done):
                n = (i * 2 + hu) * TT + t
                dve.wait_ge(p_ready, n + 1)
                dve.reciprocal(tiny[:, 12 + t:13 + t], tiny[:, 8 + t:9 + t]).then_inc(rs_ready, 1)
                dve.wait_ge(rs_ready, done)
                dve.tensor_scalar(prob[:, t % 2, :], prob[:, t % 2, :], tiny[:, 12 + t:13 + t], None, ALU.mult).then_inc(pn_ready, 1)

            with dve.Fori(0, NH // 2) as i:
                for hu in range(2):
                    h = i * 2 + hu
                    c = h * (2 * TT)
                    dve.tensor_copy(q_slot[:, hu, :], qT[:, bass.ds(h, 1), :]).then_inc(qs_ready, 1)
                    k = 0
                    for t in range(-1, TT):
                        if t + 1 < TT:
                            att_in(i, hu, t + 1)
                            k += 1
                            att_neg(i, hu, t + 1, c + k)
                        if t >= 0:
                            k += 1
                            att_norm(i, hu, t, c + k)
                    dve.wait_ge(ohi_ready, h + 1)
                    dve.tensor_tensor(b_lo[:, bass.ds(h, 1), :], ps[:, 6 + hu, :], f32(b_hi[:, bass.ds(h, 1), :]), ALU.subtract).then_inc(o_ready, 1)

            with dve.Fori(0, KT // 2) as i:
                for u in range(4):
                    step(i, AO, u)
                    if u % 2:
                        p = i * 2 + u // 2
                        dve.wait_ge(gate_ready, p + (KT + 1))
                        dve.tensor_tensor(merged[:, bass.ds(p, 1), :], sq[:, u // 2, :], ps[:, u, :], ALU.mult).then_inc(co_mul, 1)
                        dve.wait_ge(co_mul, p + 1)
                        dve.sem_inc(bank_free, 2)

            dve.wait_ge(cv_sum, 1)
            dve.tensor_scalar(nt[:, 0, :], ps[:, 4, :], 1.0 / D, None, ALU.mult).then_inc(cv_mu, 1)
            dve.wait_ge(cv_mu, 1)
            for k in range(KT):
                dve.tensor_tensor(conv[:, k, :], conv[:, k, :], nt[:, 0, :], ALU.subtract).then_inc(cv_xc, 1)
            dve.wait_ge(cv_rt, 1)
            dve.reciprocal(rstd[:, :], rstd[:, :]).then_inc(cv_rstd, 1)
            dve.wait_ge(cv_rstd, 1)
            dve.wait_ge(cv_xc, KT)
            for k in range(KT + 1):
                if k < KT:
                    if k >= 2:
                        dve.wait_ge(cv_act, k - 1)
                    dve.tensor_tensor(nt[:, k % 2, :], conv[:, k, :], rstd[:, :], ALU.mult).then_inc(cv_t, 1)
                if k:
                    dve.wait_ge(cv_hi, k)
                    dve.tensor_tensor(b_lo[:, k - 1, :], sq[:, (k - 1) % 2, :], f32(b_hi[:, k - 1, :]), ALU.subtract).then_inc(cv_ready, 1)

            with dve.Fori(0, KT // 2) as i:
                for u in range(4):
                    step(i, CO, u)
                    if u % 2:
                        p = i * 2 + u // 2
                        dve.wait_ge(gate_ready, p + (2 * KT + 1))
                        dve.tensor_tensor(nt[:, u // 2, :], sq[:, u // 2, :], ps[:, u, :], ALU.mult).then_inc(co_mul, 1)
                        dve.wait_ge(co_mul, p + (KT + 1))
                        dve.sem_inc(bank_free, 2)
                        dve.tensor_tensor(merged[:, bass.ds(p, 1), :], merged[:, bass.ds(p, 1), :], nt[:, u // 2, :], ALU.add).then_inc(pair_done, 1)
            for k in range(KT):
                dve.wait_ge(mhi_ready, k + 1)
                dve.tensor_tensor(a_lo[:, k, :], merged[:, k, :], f32(a_hi[:, k, :]), ALU.subtract).then_inc(m_ready, 1)

            def add_to_x(first, count, gain, ready0):
                with dve.Fori(0, count // 4) as i:
                    for u in range(4):
                        step(i, first, u)
                        n = i * 4 + u
                        xn = x[:, bass.ds(n, 1), :]
                        if gain is None:
                            dve.tensor_tensor(xn, ps[:, u, :], xn, ALU.add).then_inc(x_ready, 1)
                        else:
                            dve.scalar_tensor_tensor(xn, ps[:, u, :], mod[:, bass.ds(n + gain, 1), 0], xn, ALU.mult, ALU.add).then_inc(x_ready, 1)
                        dve.wait_ge(x_ready, n + (ready0 + 1))
                        dve.sem_inc(bank_free, 1)

            add_to_x(WO, KT, 2 * KT, 0)
            norm_rstd(2)
            norm_apply(2, x, lambda k: gs2[:, k:k + 1], lambda k: mod[:, 3 * KT + k, 0:1], b_hi, b_lo)

            sc4 = scores.rearrange("p (t c) n -> p t c n", t=TT)
            with dve.Fori(0, HP // 4) as i:
                for u in range(5):
                    if u < 4:
                        lo_next(i, WQ, u)
                    if u:
                        dve.wait_ge(s_ready, i * 4 + u)
                        dve.tensor_copy(sc4[:, :, bass.ds(i * 4 + (u - 1), 1), :].rearrange("p t c n -> p t (c n)"),
                                        ps[:, 3 + u, :].rearrange("p (t n) -> p t n", n=P)).then_inc(s_done, 1)

            A = A_TK
            s_in, s_rep = area(A, NK), area(A + P, NK)
            v16 = area(A + 2 * P, TOPK)
            i16 = area(A + 2 * P + TOPK, TOPK).bitcast(U32)
            cand, cand_rep = area(A + 2 * P + 32, TOPK, TOPK), area(A + 2 * P + 32 + 256, TOPK, TOPK)
            pos = area(A + 2 * P + 32 + 512, TOPK).bitcast(U32)
            pos2 = area(A + 2 * P + 32 + 528, 2, TOPK).bitcast(U32)
            eq = area(A + 2 * P + 32 + 560, 2, TOPK * TOPK)
            held = tiny[:, 60:61]
            iota16 = col("iota", 0, TOPK)

            def flat(ap):
                return ap.rearrange("p a b -> p (a b)")

            def top16(did, settle, src, rep, vals, idx):
                did(dve.max(vals[:, 0:8], src))
                settle()
                did(dve.max_index(idx[:, 0:8], vals[:, 0:8], src))
                did(dve.match_replace(rep, vals[:, 0:8], src, -3.0e38))
                settle()
                did(dve.max(vals[:, 8:16], rep))
                settle()
                did(dve.max_index(idx[:, 8:16], vals[:, 8:16], rep))

            def counted(sem_, base):
                n = [0]

                def did(ins):
                    ins.then_inc(sem_, 1)
                    n[0] += 1

                def settle():
                    dve.wait_ge(sem_, base + n[0])
                    dve.memset(held, 0.0)
                return did, settle, n

            L1 = 8
            with dve.Fori(0, NK // 4 // 4) as i:
                for u in range(4):
                    lo_next(i, EU, u)
                    for v in range(2):
                        n = i * 8 + (2 * u + v)
                        did, settle, c = counted(lv1, n * L1)
                        did(dve.tensor_copy(s_in, scores[:, bass.ds(n, 1), :].rearrange("p a n -> p (a n)")))
                        settle()
                        top16(did, settle, s_in, s_rep, v16, i16)
                        settle()
                        did(dve.tensor_copy(v1[:, bass.ds(n, 1), :].rearrange("p a n -> p (a n)"), v16))
                        did(dve.tensor_copy(i1[:, bass.ds(n, 1), :].rearrange("p a n -> p (a n)"), i16))
                        settle()
                        assert c[0] == L1
            L2 = 12
            pair = lambda ap, n: ap[:, bass.ds(n, 1), :].rearrange("p a n -> p (a n)")
            with dve.Fori(0, NK // 4 // 4) as i:
                for u in range(4):
                    lo_next(i, EU + NK // 4, u)
                    n = i * 4 + u
                    did, settle, c = counted(lv2, n * L2)
                    did(dve.tensor_tensor(cand, pair(v1, n * 2).unsqueeze(2).to_broadcast([P, TOPK, TOPK]),
                                          pair(v1, n * 2 + 1).unsqueeze(1).to_broadcast([P, TOPK, TOPK]), ALU.add))
                    settle()
                    top16(did, settle, flat(cand), flat(cand_rep), v16, pos)
                    settle()
                    did(dve.tensor_copy(best[:, bass.ds(n, 1), :].rearrange("p a n -> p (a n)"), v16))
                    did(dve.tensor_scalar(pos2[:, 0, :], pos, 4, None, ALU.logical_shift_right))
                    did(dve.tensor_scalar(pos2[:, 1, :], pos, TOPK - 1, None, ALU.bitwise_and))
                    settle()
                    eq4 = eq.rearrange("p c (k a) -> p (c k) a", a=TOPK)
                    did(dve.tensor_tensor(eq4, pos2.rearrange("p c k -> p (c k)").unsqueeze(2).to_broadcast([P, 2 * TOPK, TOPK]),
                                          iota16.unsqueeze(1).to_broadcast([P, 2 * TOPK, TOPK]), ALU.is_equal))
                    settle()
                    eq5 = eq.rearrange("p c (k a) -> p c k a", a=TOPK)
                    did(dve.tensor_tensor(eq5, eq5, i1[:, bass.ds(n * 2, 2), :].unsqueeze(2).to_broadcast([P, 2, TOPK, TOPK]), ALU.mult))
                    settle()
                    did(dve.tensor_reduce(ij[:, :, bass.ds(n * TOPK, TOPK)], eq5, AX.X, ALU.add))
                    settle()
                    assert c[0] == L2, c
            did, settle, c = counted(soft_d, 0)
            b0 = best[:, :, 0:1].to_broadcast([P, 32, TOPK])
            mx = area(A, 32)
            dve.tensor_copy(mx.unsqueeze(2), best[:, :, 0:1]).then_inc(mx_ready, 1)
            dve.wait_ge(mx_ready, NH * TT + 1)
            dve.tensor_tensor(best, best, mx.unsqueeze(2).to_broadcast([P, 32, TOPK]), ALU.subtract).then_inc(soft_d, 1)
            dve.wait_ge(soft_e, 1)
            den = area(A + 32, 32)
            dve.tensor_reduce(den, best, AX.X, ALU.add).then_inc(mx_ready, 1)
            dve.wait_ge(mx_ready, NH * TT + 2)
            dve.reciprocal(mx, den).then_inc(mx_ready, 1)
            dve.wait_ge(mx_ready, NH * TT + 3)
            dve.tensor_tensor(best, best, mx.unsqueeze(2).to_broadcast([P, 32, TOPK]), ALU.mult).then_inc(soft, 1)
            dve.wait_ge(ijw_t, 1)
            dve.tensor_copy(tok_i, ps[:, 4, :]).then_inc(ijw, 1)
            dve.tensor_copy(tok_j, ps[:, 5, :]).then_inc(ijw, 1)
            dve.tensor_copy(w_bf, ps[:, 6, :]).then_inc(ijw, 1)
            dve.tensor_copy(iota_b[:, :], col("iota", 0, P)).then_inc(ijw, 1)
            dve.wait_ge(ijw, 3)
            dve.tensor_copy(tok_w[0], w_bf).then_inc(ijw, 1)
            dve.wait_ge(ijw, 5)
            dve.tensor_tensor(tok_w[2], ps[:, 6, :], tok_w[0], ALU.subtract).then_inc(ijw, 1)
            dve.wait_ge(ijw, 6)
            dve.tensor_copy(w_bf, tok_w[2]).then_inc(ijw, 1)
            dve.wait_ge(ijw, 7)
            dve.tensor_copy(tok_w[1], w_bf).then_inc(ijw, 1)
            dve.wait_ge(ijw, 8)
            dve.tensor_tensor(tok_w[2], tok_w[2], tok_w[1], ALU.subtract).then_inc(ijw, 1)
            dve.wait_ge(ijw, 9)
            with dve.Fori(0, NK // 2 // 4) as i:
                for u in range(4):
                    lo_next(i, EU + NK // 2, u)
                    for v in range(2):
                        n = i * 8 + (2 * u + v)
                        if u:
                            dve.wait_ge(w_staged, n - 1)
                        for t in range(4):
                            at = bass.ds(n * 4 + t, 1)
                            dve.tensor_scalar(hot[v][:, t, 0, :], iota_b[:, :], tok_j[:, at], None, ALU.is_equal)
                            for c in range(3):
                                last = dve.tensor_scalar(hot[v][:, t, c + 1, :], iota_b[:, :], tok_i[:, at], tok_w[c][:, at],
                                                         ALU.is_equal, ALU.mult)
                        last.then_inc(hot_ready, 1)

            def weigh(i, u):
                n = i * 4 + u
                dve.wait_ge(wg_in[u], (i + 1) * 32)
                if not isinstance(i, int) or u >= 2 or i:
                    dve.wait_ge(zlo_ready, n - 1)
                dve.tensor_tensor(z[:, u % 2, :], w_ring[:, u, :], ge_ring[:, u, :], ALU.mult).then_inc(z_ready, 1)

            def z_lo(i, u):
                dve.wait_ge(zhi_ready, i * 4 + (u + 1))
                dve.tensor_tensor(a_lo[:, u, :], z[:, u % 2, :], f32(a_hi[:, u, :]), ALU.subtract).then_inc(zlo_ready, 1)

            for u in range(4):
                weigh(0, u)
                lo_next(0, EV, u)
                z_lo(0, u)
            with dve.Fori(1, NK // 4) as i:
                for u in range(4):
                    weigh(i, u)
                    lo_next(i, EV, u)
                    z_lo(i, u)
            dve.wait_ge(used, SW)
            for k in range(KT):
                dve.scalar_tensor_tensor(x[:, k, :], ps[:, k, :], mod[:, 5 * KT + k, 0:1], x[:, k, :], ALU.mult, ALU.add).then_inc(y_done, 1)
            norm_rstd(3)
            dve.wait_ge(y_done, KT)
            for k in range(KT):
                dve.scalar_tensor_tensor(x[:, k, :], x[:, k, :], col("final1", k), rstd[:, :], ALU.mult, ALU.mult).then_inc(x_ready, 1)
            norm_rstd(4)
            norm_apply(3, x, lambda k: col("mix", k), lambda k: col("zero"), a_hi, a_lo)

            for u in range(4):
                lo_next(0, SW, u)
            for u in range(2):
                dve.wait_ge(used, SW + u + 1)
                dve.tensor_copy(k2[:, u, :], ps[:, u, :]).then_inc(bank_free, 1)
            for u in range(2):
                dve.wait_ge(used, SW + u + 3)
                dve.tensor_copy(v2_feat_sb[:, u, :], ps[:, 2 + u, :]).then_inc(v2_feat, 1)
            dve.wait_ge(v2_feat, 2)
            dve.sem_inc(bank_free, 2)
            for u in range(2):
                dve.wait_ge(v2_turned, u + 1)
                dve.tensor_copy(v2[:, :, u * P:(u + 1) * P], ps[:, 4 + u, :].rearrange("p (s n) -> p s n", n=P)).then_inc(v2_done, 1)
            with dve.Fori(0, 2) as i:
                for u in range(4):
                    step(i, SW + 4, u)
                    dve.tensor_scalar(q2[:, bass.ds(i * 4 + u, 1), :], ps[:, u, :], HD2 ** -0.5, None, ALU.mult).then_inc(bank_free, 1)

            groups = [(b, kt, half) for b in range(TT) for kt in range(2) for half in range(2)]

            def swa_bias(n):
                b, kt, half = groups[n]
                o = 32 * (n % 2)
                dve.wait_ge(sc2, n + 1)
                if n >= 2:
                    dve.wait_ge(pt2, n - 1)
                if b == 0:
                    for r in range(4):
                        h = 8 * kt + 4 * half + r
                        dve.tensor_scalar(s2[:, n % 2, r * 256:r * 256 + P], dist[:, 1, 0:P], col("slopes", h), None, ALU.mult)
                for r in range(4):
                    h = 8 * kt + 4 * half + r
                    at = P if b == 0 else 0
                    dve.scalar_tensor_tensor(s2[:, n % 2, r * 256 + at:(r + 1) * 256], dist[:, 0, at:256], col("slopes", h),
                                             ps[:, 2 * (n % 2) + r // 2, (r % 2) * 256 + at:(r % 2) * 256 + 256],
                                             ALU.mult, ALU.add).then_inc(bias2, 1)
                dve.wait_ge(bias2, 4 * (n + 1))
                dve.tensor_reduce(tiny[:, o:o + 4], s2[:, n % 2, :].rearrange("p (r n) -> p r n", r=4), AX.X, ALU.max).then_inc(mx2, 1)
                dve.wait_ge(mx2, 2 * n + 1)
                h = 8 * kt + 4 * half
                dve.tensor_tensor(tiny[:, o:o + 4], tiny[:, o:o + 4], col("sinks", h, 4), ALU.max).then_inc(mx2, 1)
                dve.wait_ge(mx2, 2 * n + 2)
                dve.tensor_scalar(tiny[:, o + 4:o + 8], tiny[:, o:o + 4], -1.0, None, ALU.mult).then_inc(nmx2, 1)

            def swa_norm(n):
                o = 32 * (n % 2)
                dve.wait_ge(e2, 4 * (n + 1))
                dve.wait_ge(snk2, 4 * (n + 1))
                dve.tensor_tensor(tiny[:, o + 16:o + 20], tiny[:, o + 8:o + 12], tiny[:, o + 12:o + 16], ALU.add).then_inc(den2, 1)
                dve.wait_ge(den2, n + 1)
                dve.reciprocal(tiny[:, o + 20:o + 24], tiny[:, o + 16:o + 20]).then_inc(rec2, 1)
                dve.wait_ge(rec2, n + 1)
                pr = s2[:, n % 2, :].rearrange("p (r n) -> p r n", r=4)
                dve.tensor_tensor(pr, pr, tiny[:, o + 20:o + 24].unsqueeze(2).to_broadcast([P, 4, 256]), ALU.mult).then_inc(pn2, 1)

            def swa_lo(n):
                b, kt, half = groups[n]
                rows_ = slice(half * HD2, (half + 1) * HD2)
                dve.wait_ge(ohi2, n + 1)
                at = slice(b * P, (b + 1) * P)
                dve.tensor_tensor(b_lo[rows_, kt * 4:kt * 4 + 4, at], ps[rows_, 6 + n % 2, :].rearrange("p (r t) -> p r t", r=4),
                                  f32(b_hi[rows_, kt * 4:kt * 4 + 4, at]), ALU.subtract).then_inc(o2, 1)

            dve.wait_ge(dist_in, 16)
            dve.wait_ge(bank_free, r_of(SO) + 4)
            swa_bias(0)
            for n in range(len(groups)):
                if n + 1 < len(groups):
                    swa_bias(n + 1)
                swa_norm(n)
                swa_lo(n)

            add_to_x(SO, KT, None, 2 * KT)
            norm_rstd(5)
            norm_apply(4, x, lambda k: col("ffn", k), lambda k: col("zero"), a_hi, a_lo)

            with dve.Fori(0, 2 * FT // 4) as i:
                for u in range(4):
                    step(i, GU, u)
                    if u % 2:
                        p = i * 2 + u // 2
                        dve.wait_ge(gate_ready, p + (3 * KT + 1))
                        dve.tensor_tensor(hid[:, bass.ds(p, 1), :], sq[:, u // 2, :], ps[:, u, :], ALU.mult).then_inc(act_done, 1)
                        dve.wait_ge(act_done, p + 1)
                        dve.sem_inc(bank_free, 2)

            def hid_lo(i, u):
                n = i * 4 + u
                dve.wait_ge(dhi_ready, n + 1)
                dve.tensor_tensor(b_lo[:, u, :], hid[:, bass.ds(n, 1), :] if not isinstance(n, int) else hid[:, n, :],
                                  f32(b_hi[:, u, :]), ALU.subtract).then_inc(dlo_ready, 1)

            with dve.Fori(0, FT // 4) as i:
                for u in range(4):
                    lo_next(i, DN, u)
                    hid_lo(i, u)
            lo_next(FT // 4, DN, 0)
            for u in range(FT % 4):
                hid_lo(FT // 4, u)
            dve.wait_ge(used, PANELS)
            for k in range(KT):
                dve.tensor_tensor(x[:, k, :], ps[:, k, :], x[:, k, :], ALU.add).then_inc(y2_done, 1)
            norm_rstd(6)
            dve.wait_ge(y2_done, KT)
            for k in range(KT):
                dve.scalar_tensor_tensor(x[:, k, :], x[:, k, :], col("final2", k), rstd[:, :], ALU.mult, ALU.mult).then_inc(out_done, 1)

        @block.gpsimd
        def _(pool):
            nc.gpsimd.memset(g_pad[:, :, 0:PAD], 0.0)
            nc.gpsimd.memset(g_pad[:, :, PAD + T:GW], 0.0).then_inc(pad_ready, 1)
            pool.wait_ge(small_in, 16)
            tmp = area(A_TMP, T)
            for i in range(KT // 2):
                n = 2 * i + 1
                pool.wait_ge(pair_done, n + 1)
                for j in range(TAPS):
                    if i or j:
                        pool.wait_ge(pool_tap, i * TAPS + j)
                    nc.gpsimd.tensor_tensor(tmp, g_pad[:, n, j:j + T], col("conv_w", n * TAPS + j).to_broadcast([P, T]),
                                            ALU.mult).then_inc(pool_mul, 1)
                    pool.wait_ge(pool_mul, i * TAPS + j + 1)
                    nc.gpsimd.tensor_tensor(conv[:, n, :], tmp, conv[:, n, :] if j else col("conv_b", n).to_broadcast([P, T]),
                                            ALU.add).then_inc(pool_tap, 1)


def kernel(**inputs):
    import numpy as np
    import concourse.bacc as _bacc
    from concourse.bass_utils import run_bass_kernel_spmd as _run

    a = {k: np.asarray(v) for k, v in inputs.items()}
    f = np.float32

    def columns(w):
        n = w.shape[1] // P
        return w.reshape(KT, P, n, P).transpose(2, 1, 0, 3).reshape(n, P, D)

    def tiles(v):
        return v.reshape(-1, P).T

    def pairs(m, n):
        return np.stack([m, n], axis=1).reshape(-1, P, D)

    w_in = columns(a["w_in"][0])
    qkv = NH + 2 * NKV
    w_q, w_k, w_v = w_in[0:NH], w_in[NH:NH + NKV], w_in[NH + NKV:qkv]
    conv_a, conv_b = w_in[qkv:qkv + KT], w_in[qkv + KT:qkv + 2 * KT]
    gate_a, gate_c = w_in[qkv + 2 * KT:qkv + 3 * KT], w_in[qkv + 3 * KT:qkv + 4 * KT]
    order = np.concatenate([np.arange(HD2) + HD2 * (8 * kt + 4 * half + r)
                            for kt in range(2) for r in range(4) for half in range(2)])
    s_in = a["swa_w_in_2"][0]
    s_q = columns(s_in[:, 0:D][:, order])
    s_kv = columns(s_in[:, D:])
    s_out = columns(a["swa_w_out_2"][0][order, :])
    gu = columns(a["ffn_w_gate_up_2"][0])
    panels = np.concatenate([
        columns(a["w_mod"][0]), pairs(conv_a, conv_b), w_k, w_v, w_q, pairs(gate_a, columns(a["w_attn_o"][0])),
        pairs(gate_c, columns(a["w_conv_o"][0])), columns(a["w_out"][0]), columns(a["peer_wq"][0]),
        a["peer_u"][0].reshape(NK, P, KT, P).transpose(0, 3, 2, 1).reshape(NK, P, D), a["peer_v"][0].reshape(NK, P, D),
        s_kv, s_q, s_out, pairs(gu[0:FT], gu[FT:]), a["ffn_w_down_2"][0].reshape(FT, P, D)])
    assert panels.shape == (PANELS, P, D)

    half, quarter = P // 2, P // 4
    pos = np.arange(T)
    inv = (np.float32(10000.0) ** (-np.arange(0, half, 2, dtype=f) / half)).astype(f)
    ang = np.concatenate([(p[:, None].astype(f) * inv).T for p in (pos // 64, pos // 64, pos % 64, pos % 64)])
    rope = np.stack([np.cos(ang), np.sin(ang)], axis=1).astype(f)
    perm = np.zeros((P, P), f)
    for d in range(P):
        first = d % half < quarter
        perm[d + quarter if first else d - quarter, d] = -1.0 if first else 1.0
    gap = (P + np.arange(P))[:, None] - np.arange(2 * P)[None, :]
    dist = np.where((gap >= 0) & (gap < P), gap, 1e30).astype(f)
    dist = np.stack([dist, np.full_like(dist, 1e30)], axis=1)
    slopes = -np.exp2(-8.0 * np.arange(1, NH2 + 1, dtype=f) / NH2).astype(f)

    wide = lambda v: np.broadcast_to(v, (P, v.shape[-1]))
    parts = {
        "b_mod": tiles(a["b_mod"][0]), "norm1": tiles(a["norm1_g"][0]), "norm2": tiles(a["norm2_g"][0]),
        "final1": tiles(a["final_norm_g"]), "conv_w": a["conv_dw"][0].T.reshape(KT, P, TAPS).transpose(1, 0, 2).reshape(P, -1),
        "conv_b": tiles(a["conv_b"][0]), "ln_g": tiles(a["conv_ln_g"][0]), "ln_b": tiles(a["conv_ln_b"][0]),
        "q_g": tiles(a["q_norm_g"][0]), "k_g": tiles(a["k_norm_g"][0]), "mix": tiles(a["norm_mix_2"][0]),
        "ffn": tiles(a["norm_ffn_2"][0]), "final2": tiles(a["final_norm_2"]),
        "c": np.stack([tiles(a["c"][0]), tiles(a["c_ctx"])], axis=2).reshape(P, -1),
        "sinks": wide(a["swa_sinks_2"][0]), "slopes": wide(slopes), "ident": np.eye(P, dtype=f),
        "ones": np.ones((P, P), f), "perm": perm, "iota": wide(np.arange(P, dtype=f)), "zero": np.zeros((P, 1), f)}
    small = np.concatenate([parts[n] for n in SMALL], axis=1)
    assert small.shape == (P, SMALL_N)
    arrays = {
        "panels": panels, "small": small,
        "xT": a["x"][0].T.reshape(KT, P, T).transpose(1, 0, 2), "ctxT": a["ctx"][0].T.reshape(KT, P, CTX).transpose(1, 0, 2),
        "rope": rope, "keys": a["peer_keys"][0].reshape(HP, NK, P).transpose(2, 0, 1), "dist": dist}
    arrays = {k: np.ascontiguousarray(v) for k, v in arrays.items()}

    nc = _bacc.Bacc("TRN2", target_bir_lowering=False, num_devices=1)
    aps = [nc.dram_tensor(k, v.shape, mybir.dt.from_np(v.dtype), kind="ExternalInput").ap() for k, v in arrays.items()]
    w_d = nc.dram_tensor("w_scratch", (NK, P, T), F32, kind="Internal").ap()
    ge_d = nc.dram_tensor("gelu_scratch", (NK, P, T), F32, kind="Internal").ap()
    out = nc.dram_tensor("out", (P, KT, T), F32, kind="ExternalOutput").ap()
    build(nc, *aps, w_d, ge_d, out)
    r = _run(nc, [arrays], core_ids=[0])
    return np.ascontiguousarray(r.results[0]["out"].transpose(2, 1, 0).reshape(1, T, D))
```

```python
from contextlib import ExitStack

import concourse.bass as bass
from concourse import mybir

F32 = mybir.dt.float32
F32R = mybir.dt.float32r
BF16 = mybir.dt.bfloat16
U32 = mybir.dt.uint32
ACT = mybir.ActivationFunctionType
ALU = mybir.AluOpType
AX = mybir.AxisListType

P = 128
D = 1024
KT = D // P
T = 512
TT = T // P
CTX = 256
S1 = T + CTX
ST = S1 // P
NH, NKV = 8, 2
TAPS = 31
PAD = TAPS // 2
GW = T + 2 * PAD
HP = 16
PH = 8
TOPK = 16
NK = 128
NH2, NKV2, HD2 = 16, 4, 64
FF = 2816
FT = FF // P
EPS = 1e-6

MOD_N = 6 * KT
MOD = 0
U = MOD + MOD_N
KV = U + 2 * KT
Q = KV + 4
AO = Q + NH
CO = AO + 2 * KT
WO = CO + 2 * KT
WQ = WO + KT
EU = WQ + HP
EV = EU + NK
SW = EV + NK
SO = SW + 12
GU = SO + KT
DN = GU + 2 * FT
PANELS = DN + FT

E_SOFT = 52
E_TURN = 52
E_W = 56
RAW = 4
SPLIT = 2
BANKS = 4

SMALL = {}
_at = 0
for _name, _n in (("b_mod", MOD_N), ("norm1", KT), ("norm2", KT), ("final1", KT), ("conv_w", KT * TAPS),
                  ("conv_b", KT), ("ln_g", KT), ("ln_b", KT), ("q_g", 1), ("k_g", 1), ("mix", KT), ("ffn", KT),
                  ("final2", KT), ("c", 2 * KT), ("sinks", NH2), ("slopes", NH2), ("ident", P), ("ones", P),
                  ("perm", P), ("iota", P), ("zero", 1)):
    SMALL[_name] = (_at, _n)
    _at += _n
SMALL_N = _at

ARENA = 20736
A_G = 0
A_CONV = A_G + KT * GW
A_K = A_CONV + KT * T
A_V = A_K + NKV * S1
A_Q = A_V + ST * 2 * P
A_TMP = A_Q + NH * T
A_X = A_TMP + T
A_XCTX = A_X
A_COS = A_X
A_SIN = A_COS + T
A_QN = A_SIN + T
A_ROT = A_QN + 2 * T
A_P = A_X
A_PT = A_P + 2 * S1
A_M = A_X
A_XEND = A_X + 4608
assert A_XEND <= ARENA
A_S = 0
A_STAGE = (0, 8192)
A_V1 = 8192
A_I1 = A_V1 + 64 * TOPK
A_BS = A_I1 + 64 * TOPK
A_IJ = A_BS + 32 * TOPK
A_TK = A_IJ + 64 * TOPK
A_KEYS = A_TK + 2304
A_QK = 16384
A_TI = A_QK + 2 * T
A_TJ = A_TI + T
A_GE = A_TJ + T
A_BF = A_GE + 4 * T
assert A_KEYS + HP * P <= 16384 and A_BF + T // 2 <= ARENA
A_WR, A_GR, A_Z = 0, 4 * T, 8 * T
A_Q2 = 0
A_K2 = A_Q2 + 8 * T
A_V2 = A_K2 + 2 * T
A_DIST = A_V2 + TT * 2 * P
A_S2 = A_DIST + 2 * 256
A_PT2 = A_S2 + 2 * 1024
A_FF = 0


def build(nc, panels, small, xT_d, ctxT_d, rope_d, keys_d, dist_d, w_d, ge_d, out):
    with ExitStack() as ctx:
        def sb(name, shape, dt=F32):
            return ctx.enter_context(nc.sbuf_tensor(name, shape, dt))

        def sem(name):
            return ctx.enter_context(nc.semaphore(name))

        x = sb("x", [P, KT, T])
        raw = sb("raw", [P, RAW, D])
        whi = sb("whi", [P, SPLIT, D], F32R)
        wlo = sb("wlo", [P, SPLIT, D], F32R)
        a_hi = sb("a_hi", [P, KT, T], F32R)
        a_lo = sb("a_lo", [P, KT, T], F32R)
        b_hi = sb("b_hi", [P, KT, T], F32R)
        b_lo = sb("b_lo", [P, KT, T], F32R)
        sm = sb("sm", [P, SMALL_N])
        mod = sb("mod", [P, MOD_N, 2])
        gs1 = sb("gs1", [P, KT])
        gs1c = sb("gs1c", [P, KT])
        gs2 = sb("gs2", [P, KT])
        c_act = sb("c_act", [P, KT, 2])
        iota_b = sb("iota_b", [P, P], BF16)
        tiny = sb("tiny", [P, 64])
        sq = sb("sq", [P, 2, T])
        rstd = sb("rstd", [P, T])
        nt = sb("nt", [P, 2, T])
        ar = sb("ar", [P, ARENA])
        ps = ctx.enter_context(nc.psum_tensor("ps", [P, 8, T], F32))

        def area(at, *dims):
            n = 1
            for d in dims:
                n *= d
            v = ar[:, at:at + n]
            if len(dims) == 2:
                v = v.rearrange("p (a b) -> p a b", a=dims[0])
            elif len(dims) == 3:
                v = v.rearrange("p (a b c) -> p a b c", a=dims[0], b=dims[1])
            return v

        def col(name, i=0, n=1):
            at = SMALL[name][0] + i
            return sm[:, at:at + n]

        ident, ones, perm = col("ident", 0, P), col("ones", 0, P), col("perm", 0, P)
        f32 = lambda ap: ap.bitcast(F32)

        landed = [sem(f"landed{i}") for i in range(RAW)]
        hi_ready = sem("hi_ready")
        lo_ready = sem("lo_ready")
        used = sem("used")
        bank_free = sem("bank_free")
        small_in, x_in, ctx_in, rope_in, keys_in, dist_in = (
            sem(n) for n in ("small_in", "x_in", "ctx_in", "rope_in", "keys_in", "dist_in"))
        c_ready, mod_ready, mod_done = sem("c_ready"), sem("mod_ready"), sem("mod_done")
        sq_ready, sq_used, rt_ready, rstd_ready = (
            sem(n) for n in ("sq_ready", "sq_used", "rt_ready", "rstd_ready"))
        nt_ready, nhi_ready, h_ready = (sem(n) for n in ("nt_ready", "nhi_ready", "h_ready"))
        x_ready = sem("x_ready")
        gate_ready, pair_done = sem("gate_ready"), sem("pair_done")
        pad_ready, tap_done, pool_mul, pool_tap = (
            sem(n) for n in ("pad_ready", "tap_done", "pool_mul", "pool_tap"))
        ksq, kstat, krt, krstd, kn, krot, kcos, ksin, k_done = (
            sem(n) for n in ("ksq", "kstat", "krt", "krstd", "kn", "krot", "kcos", "ksin", "k_done"))
        v_feat_ready, v_turned, v_done = sem("v_feat_ready"), sem("v_turned"), sem("v_done")
        qs_ready, sc_ready, mx_ready, p_ready, rs_ready, pn_ready, pt_ready, pt_done, pv_ready, ohi_ready, o_ready = (
            sem(n) for n in ("qs_ready", "sc_ready", "mx_ready", "p_ready", "rs_ready", "pn_ready", "pt_ready",
                             "pt_done", "pv_ready", "ohi_ready", "o_ready"))
        cv_sum, cv_mu, cv_xc, cv_sq, cv_used, cv_var, cv_rt, cv_rstd, cv_t, cv_act, cv_hi, cv_ready = (
            sem(n) for n in ("cv_sum", "cv_mu", "cv_xc", "cv_sq", "cv_used", "cv_var", "cv_rt", "cv_rstd", "cv_t",
                             "cv_act", "cv_hi", "cv_ready"))
        co_mul = sem("co_mul")
        mhi_ready, m_ready = sem("mhi_ready"), sem("m_ready")
        qk_ready, s_ready, s_done = sem("qk_ready"), sem("s_ready"), sem("s_done")
        lv1, lv2, soft, soft_d, soft_e, ijw_t, ijw = (sem(n) for n in ("lv1", "lv2", "soft", "soft_d", "soft_e", "ijw_t", "ijw"))
        hot_ready, w_ready, w_staged = (sem(n) for n in ("hot_ready", "w_ready", "w_staged"))
        w_out = [sem(f"w_out{i}") for i in range(2)]
        ge_out = [sem(f"ge_out{i}") for i in range(4)]
        wg_in = [sem(f"wg_in{i}") for i in range(4)]
        z_ready, zhi_ready, zlo_ready, y_done = (sem(n) for n in ("z_ready", "zhi_ready", "zlo_ready", "y_done"))
        v2_feat, v2_turned, v2_done = sem("v2_feat"), sem("v2_turned"), sem("v2_done")
        sc2, bias2, mx2, nmx2, e2, snk2, den2, rec2, pn2, pt2, ptc2, pv2, ohi2, o2 = (
            sem(n) for n in ("sc2", "bias2", "mx2", "nmx2", "e2", "snk2", "den2", "rec2", "pn2", "pt2", "ptc2",
                             "pv2", "ohi2", "o2"))
        act_done, dhi_ready, dlo_ready, y2_done, out_done = (
            sem(n) for n in ("act_done", "dhi_ready", "dlo_ready", "y2_done", "out_done"))

        g_pad = area(A_G, KT, GW)
        conv = area(A_CONV, KT, T)
        kT = area(A_K, NKV, S1)
        v_tok = area(A_V, ST, 2 * P)
        qT = area(A_Q, NH, T)
        v_feat = area(A_Q, NKV, S1)
        q_slot = nt
        x_ctx = area(A_XCTX, KT, CTX)
        cos, sin = area(A_COS, T), area(A_SIN, T)
        q_n = area(A_QN, 2, T)
        q_rot = area(A_ROT, 2, T)
        prob = area(A_P, 2, S1)
        probT = area(A_PT, ST, T)
        merged = area(A_M, KT, T)
        scores = area(A_S, 64, NK)
        stage = [area(a, P, 64) for a in A_STAGE]
        v1, i1 = area(A_V1, 64, TOPK), area(A_I1, 64, TOPK)
        best = area(A_BS, 32, TOPK)
        ij = area(A_IJ, 2, 32 * TOPK)
        keys = area(A_KEYS, HP, P)
        q_key = area(A_QK, 2, T)
        tok_i, tok_j = area(A_TI, T), area(A_TJ, T)
        ge_slot = area(A_GE, 4, T)
        w_ring, ge_ring, z = area(A_WR, 4, T), area(A_GR, 4, T), area(A_Z, 2, T)
        hot = [v[:, :, :].rearrange("p a b -> p (a b)").bitcast(BF16).rearrange("p (t k n) -> p t k n", t=4, k=4)
               for v in (sq, nt)]
        tok_w = [q_key[:, 0, :], q_key[:, 1, :], rstd[:, :]]
        w_bf = area(A_BF, T // 2).bitcast(BF16)
        q2 = area(A_Q2, 8, T)
        k2 = area(A_K2, 2, T)
        v2 = area(A_V2, TT, 2 * P)
        v2_feat_sb = area(A_S2, 2, T)
        dist = area(A_DIST, 2, 256)
        s2 = area(A_S2, 2, 1024)
        p2T = area(A_PT2, 2, 512)
        hid = area(A_FF, FT, T)

        def r_of(g):
            return g - U if g < EV else g - U - NK


        block = ctx.enter_context(nc.Block())

        @block.sync
        def _(sp):
            sp.dma_start(sm[:, :], small).then_inc(small_in, 16)

            def load(g, u):
                sp.dma_start(raw[:, u, :], panels[g]).then_inc(landed[u], 16)

            def load_dyn(i, g0, u):
                sp.wait_ge(lo_ready, i * 4 + (g0 + u - RAW + 1 - U))
                send(i, g0, u)

            def send(i, g0, u):
                sp.dma_start(raw[:, u, :], panels[bass.ds(i * 4 + (g0 + u), 1)].rearrange("a p n -> (a p) n")).then_inc(landed[u], 16)

            for u in range(RAW):
                load(u, u)
            sp.dma_start(x[:, :, :], xT_d).then_inc(x_in, 16)
            sp.dma_start(x_ctx, ctxT_d).then_inc(ctx_in, 16)
            with sp.Fori(0, U // 4) as i:
                for u in range(4):
                    sp.wait_ge(used, i * 4 + (u + 1))
                    send(i, RAW, u)
            with sp.Fori(0, (KV - U - RAW) // 4) as i:
                for u in range(4):
                    load_dyn(i, U + RAW, u)
            sp.wait_ge(h_ready, 2 * KT)
            sp.dma_start(area(A_COS, 2, T), rope_d).then_inc(rope_in, 16)
            with sp.Fori(0, (WQ - KV) // 4) as i:
                for u in range(4):
                    load_dyn(i, KV, u)
            for u in range(4):
                load_dyn(0, WQ, u)
            sp.wait_ge(h_ready, 3 * KT)
            sp.dma_start(keys, keys_d).then_inc(keys_in, 16)
            with sp.Fori(1, (EV - WQ) // 4) as i:
                for u in range(4):
                    load_dyn(i, WQ, u)

            def load_wg(i, u):
                sp.dma_start(w_ring[:, u, :], w_d[bass.ds(i * 4 + u, 1)].rearrange("a p n -> (a p) n")).then_inc(wg_in[u], 16)
                sp.dma_start(ge_ring[:, u, :], ge_d[bass.ds(i * 4 + u, 1)].rearrange("a p n -> (a p) n")).then_inc(wg_in[u], 16)

            for done in w_out:
                sp.wait_ge(done, 16 * 4)
            for u in range(4):
                sp.wait_ge(ge_out[u], 16)
                load_wg(0, u)
            for u in range(4):
                load_dyn(0, EV, u)
            for done in ge_out:
                sp.wait_ge(done, 16 * (NK // 4))
            with sp.Fori(1, NK // 4) as i:
                for u in range(4):
                    load_dyn(i, EV, u)
                    sp.wait_ge(z_ready, i * 4 + (u - 4 + 1))
                    load_wg(i, u)
            sp.wait_ge(z_ready, NK)
            sp.dma_start(area(A_DIST, 2, 256), dist_d).then_inc(dist_in, 16)
            with sp.Fori(0, (PANELS - SW) // 4) as i:
                for u in range(4):
                    load_dyn(i, SW, u)
            for u in range((PANELS - SW) % 4):
                load_dyn(0, PANELS - 2, u)
            sp.wait_ge(out_done, KT)
            sp.dma_start(out, x[:, :, :]).then_inc(x_in, 16)
            sp.wait_ge(x_in, 32)

        @block.tensor
        def _(pe):
            def panel(g, u, bank, hi, lo, free, ready=None):
                pe.wait_ge(lo_ready, g + (1 - U))
                pe.wait_ge(bank_free, free)
                for k in range(KT):
                    if ready:
                        pe.wait_ge(ready[0], ready[1] + k + 1)
                    w_h = whi[:, u % SPLIT, k * P:(k + 1) * P]
                    w_l = wlo[:, u % SPLIT, k * P:(k + 1) * P]
                    pe.matmul(bank, w_h, hi[:, k, :], start=(k == 0), stop=False)
                    pe.matmul(bank, w_h, lo[:, k, :], start=False, stop=False)
                    last = pe.matmul(bank, w_l, hi[:, k, :], start=False, stop=(k == KT - 1))
                last.then_inc(used, 1)

            def strips(first, count, hi, lo, after=None, ready=None):
                def four(i, ready=None):
                    for u in range(4):
                        panel(i * 4 + (first + u), u, ps[:, u, :], hi, lo, i * 4 + (r_of(first) + u + 1), ready if u == 0 else None)
                        if after:
                            after(i, u)
                    if after:
                        after(i, 4)
                four(0, ready)
                if count > 4:
                    with pe.Fori(1, count // 4) as i:
                        four(i)

            def norm_stats(n, src_width=T):
                for k in range(KT):
                    pe.wait_ge(sq_ready, n * KT + k + 1)
                    pe.matmul(ps[:, 4, 0:src_width], ones, sq[:, k % 2, 0:src_width], start=(k == 0),
                              stop=(k == KT - 1)).then_inc(sq_used, 1)

            pe.wait_ge(c_ready, 1)
            with pe.Fori(0, MOD_N // 4) as i:
                for u in range(4):
                    pe.wait_ge(landed[u], i * 16 + 16)
                    for k in range(KT):
                        last = pe.matmul(ps[:, 7, bass.ds(i * 8 + 2 * u, 2)], raw[:, u, k * P:(k + 1) * P], c_act[:, k, :],
                                         start=(k == 0), stop=(k == KT - 1))
                    last.then_inc(used, 1)
            norm_stats(0)
            pe.wait_ge(rt_ready, 1)
            norm_stats(1, CTX)

            strips(U, 2 * KT, a_hi, a_lo, ready=(h_ready, 0))

            def split3(bank, wu, k, hi, lo, first, last):
                w_h = whi[:, wu % SPLIT, k * P:(k + 1) * P]
                w_l = wlo[:, wu % SPLIT, k * P:(k + 1) * P]
                pe.matmul(bank, w_h, hi, start=first, stop=False)
                pe.matmul(bank, w_h, lo, start=False, stop=False)
                return pe.matmul(bank, w_l, hi, start=False, stop=last)

            def head_stats(n, width=T):
                pe.wait_ge(ksq, n + 1)
                if n:
                    pe.wait_ge(krt, n)
                pe.matmul(ps[:, 4, 0:width], ones, sq[:, n % 2, 0:width], start=True, stop=True).then_inc(kstat, 1)

            def head_rot(n, m):
                pe.wait_ge(kn, n + 1)
                if m:
                    pe.wait_ge(ksin, m)
                pe.matmul(ps[:, 5, :], perm, q_n[:, n % 2, :], start=True, stop=True).then_inc(krot, 1)

            pe.wait_ge(h_ready, 2 * KT)
            for u in range(4):
                g = KV + u
                pe.wait_ge(lo_ready, g + (1 - U))
                pe.wait_ge(bank_free, r_of(g) + 1)
                for k in range(KT):
                    split3(ps[:, u, :], u, k, a_hi[:, k, :], a_lo[:, k, :], k == 0, k == KT - 1)
                for k in range(KT):
                    last = split3(ps[:, 6 + u // 2, u % 2 * CTX:(u % 2 + 1) * CTX], u, k, b_hi[:, k, 0:CTX], b_lo[:, k, 0:CTX], k == 0, k == KT - 1)
                last.then_inc(used, 1)
            for u in range(2):
                head_stats(2 * u)
                head_stats(2 * u + 1, CTX)
                head_rot(2 * u, u)
            for u in range(2):
                pe.wait_ge(v_feat_ready, 2 * (u + 1))
                pe.wait_ge(ksin, 2)
                if u:
                    pe.wait_ge(v_done, 1)
                for s in range(ST):
                    last = pe.transpose(ps[:, 4 + s // 3, (s % 3) * P:(s % 3 + 1) * P],
                                        v_feat[:, u, s * P:(s + 1) * P], ident)
                last.then_inc(v_turned, 1)

            def q_after(i, u):
                for v in ((u - 1,) if 0 < u < 4 else (3,) if u == 4 else ()):
                    n = i * 4 + (4 + v)
                    pe.wait_ge(ksq, n + 1)
                    pe.wait_ge(krt, n)
                    pe.matmul(ps[:, 4, :], ones, sq[:, v % 2, :], start=True, stop=True).then_inc(kstat, 1)
                    pe.wait_ge(kn, n + 1)
                    pe.wait_ge(ksin, i * 4 + (2 + v))
                    pe.matmul(ps[:, 5, :], perm, q_n[:, v % 2, :], start=True, stop=True).then_inc(krot, 1)

            pe.wait_ge(v_done, NKV)
            strips(Q, NH, a_hi, a_lo, q_after)

            pe.wait_ge(k_done, NKV + NH)
            pe.wait_ge(v_done, NKV)
            pe.wait_ge(bank_free, r_of(AO) + 4)

            def att_scores(i, hu, t):
                n = (i * 2 + hu) * TT + t
                b = 2 * (t % 2)
                kv = ATT_KV[0]
                pe.matmul(ps[:, b, :], q_slot[:, hu, t * P:(t + 1) * P], kT[:, kv, 0:T], start=True, stop=True)
                pe.matmul(ps[:, b + 1, 0:CTX], q_slot[:, hu, t * P:(t + 1) * P], kT[:, kv, T:S1], start=True,
                          stop=True).then_inc(sc_ready, 1)

            ATT_KV = [0]
            for half in range(NKV):
                ATT_KV[0] = half
                with pe.Fori(2 * half, 2 * half + 2) as i:
                    for hu in range(2):
                        h = i * 2 + hu
                        pe.wait_ge(qs_ready, h + 1)
                        att_scores(i, hu, 0)
                        for t in range(TT):
                            n = h * TT + t
                            if t + 1 < TT:
                                att_scores(i, hu, t + 1)
                            pe.wait_ge(pn_ready, n + 1)
                            if t:
                                pe.wait_ge(pt_done, n)
                            for s in range(ST):
                                last = pe.transpose(ps[:, 4 + s // 3, (s % 3) * P:(s % 3 + 1) * P],
                                                    prob[:, t % 2, s * P:(s + 1) * P], ident)
                            last.then_inc(pt_ready, 1)
                        pe.wait_ge(pt_done, (h + 1) * TT)
                        for s in range(ST):
                            last = pe.matmul(ps[:, 6 + hu, :], v_tok[:, s, half * P:(half + 1) * P], probT[:, s, :],
                                             start=(s == 0), stop=(s == ST - 1))
                        last.then_inc(pv_ready, 1)

            pe.wait_ge(o_ready, NH)
            with pe.Fori(0, 2 * KT // 4) as i:
                for u in range(4):
                    hi, lo = (a_hi, a_lo) if u % 2 == 0 else (b_hi, b_lo)
                    panel(i * 4 + (AO + u), u, ps[:, u, :], hi, lo, i * 4 + (r_of(AO) + u + 1))

            pe.wait_ge(tap_done, 6 * TAPS)
            pe.wait_ge(pool_tap, 2 * TAPS)
            for k in range(KT):
                last = pe.matmul(ps[:, 4, :], ones, conv[:, k, :], start=(k == 0), stop=(k == KT - 1))
            last.then_inc(cv_sum, 1)
            for k in range(KT):
                pe.wait_ge(cv_sq, k + 1)
                pe.matmul(ps[:, 5, :], ones, sq[:, k % 2, :], start=(k == 0), stop=(k == KT - 1)).then_inc(cv_used, 1)

            pe.wait_ge(cv_ready, KT)
            with pe.Fori(0, 2 * KT // 4) as i:
                for u in range(4):
                    hi, lo = (a_hi, a_lo) if u % 2 == 0 else (b_hi, b_lo)
                    panel(i * 4 + (CO + u), u, ps[:, u, :], hi, lo, i * 4 + (r_of(CO) + u + 1))
            strips(WO, KT, a_hi, a_lo, ready=(m_ready, 0))

            norm_stats(2)
            pe.wait_ge(keys_in, 16)

            def key_scores(i, u):
                for v in ((u - 1,) if 0 < u < 4 else (3,) if u == 4 else ()):
                    pe.wait_ge(qk_ready, i * 4 + (v + 1))
                    if not isinstance(i, int) or i:
                        pe.wait_ge(s_done, i * 4 + (v - 3))
                    for t in range(TT):
                        last = pe.matmul(ps[:, 4 + v, t * P:(t + 1) * P], q_key[:, v % 2, t * P:(t + 1) * P],
                                         keys[:, bass.ds(i * 4 + v, 1), :], start=True, stop=True)
                    last.then_inc(s_ready, 1)

            strips(WQ, HP, b_hi, b_lo, key_scores, (h_ready, 2 * KT))

            strips(EU, E_TURN, b_hi, b_lo)

            pe.wait_ge(soft, 1)
            for a in range(3):
                src = ij[:, a, :] if a < 2 else best.rearrange("p a b -> p (a b)")
                for t in range(TT):
                    last = pe.transpose(ps[:, 4 + a, t * P:(t + 1) * P], src[:, t * P:(t + 1) * P], ident)
            last.then_inc(ijw_t, 1)

            strips(EU + E_TURN, E_W - E_TURN, b_hi, b_lo)

            def token_w(i, u):
                if u == 4:
                    return
                for v in range(2):
                    n = i * 8 + (2 * u + v)
                    pe.wait_ge(hot_ready, n + 1)
                    if not isinstance(n, int) or n >= 4:
                        pe.wait_ge(w_ready, n - 3)
                    bank = 4 + (2 * u + v) % 4
                    for t in range(4):
                        for c in range(1, 4):
                            last = pe.matmul(ps[:, bank, t * P:(t + 1) * P], hot[v][:, t, 0, :], hot[v][:, t, c, :],
                                             start=(c == 1), stop=(c == 3))
                    last.then_inc(w_staged, 1)

            strips(EU + E_W, T // 8, b_hi, b_lo, token_w)
            strips(EU + E_W + T // 8, NK - E_W - T // 8, b_hi, b_lo)

            pe.wait_ge(bank_free, r_of(EU) + NK + 4)
            pe.wait_ge(w_ready, P)

            def rows(g, u, n, zsem, hi, lo, slot, start, stop, nsem):
                pe.wait_ge(lo_ready, g + (1 - U))
                pe.wait_ge(zsem, n + 1)
                for d in range(KT):
                    w_h = whi[:, u % SPLIT, d * P:(d + 1) * P]
                    w_l = wlo[:, u % SPLIT, d * P:(d + 1) * P]
                    pe.matmul(ps[:, d, :], w_h, hi[:, slot, :], start=start, stop=False)
                    pe.matmul(ps[:, d, :], w_h, lo[:, slot, :], start=False, stop=False)
                    last = pe.matmul(ps[:, d, :], w_l, hi[:, slot, :], start=False, stop=stop)
                last.then_inc(used, 1)

            for u in range(4):
                rows(EV + u, u, u, zlo_ready, a_hi, a_lo, u, u == 0, False, None)
            with pe.Fori(1, NK // 4 - 1) as i:
                for u in range(4):
                    rows(i * 4 + (EV + u), u, i * 4 + u, zlo_ready, a_hi, a_lo, u, False, False, None)
            for u in range(4):
                n = NK - 4 + u
                rows(EV + n, u, n, zlo_ready, a_hi, a_lo, u, False, n == NK - 1, None)

            pe.wait_ge(y_done, KT)
            norm_stats(3)
            norm_stats(4)
            pe.wait_ge(h_ready, 4 * KT)

            for u in range(4):
                panel(SW + u, u, ps[:, u, :], a_hi, a_lo, r_of(SW) + u + 1)
            for u in range(2):
                pe.wait_ge(v2_feat, u + 1)
                for s in range(TT):
                    last = pe.transpose(ps[:, 4 + u, s * P:(s + 1) * P], v2_feat_sb[:, u, s * P:(s + 1) * P], ident)
                last.then_inc(v2_turned, 1)
            strips(SW + 4, 8, a_hi, a_lo)

            pe.wait_ge(bank_free, r_of(SO) + 4)
            pe.wait_ge(v2_done, 2)
            groups = [(b, kt, half) for b in range(TT) for kt in range(2) for half in range(2)]

            def swa_scores(n):
                b, kt, half = groups[n]
                rows_ = slice(half * HD2, (half + 1) * HD2)
                if n >= 2:
                    pe.wait_ge(bias2, 4 * (n - 1))
                for r in range(4):
                    dst = ps[:, 2 * (n % 2) + r // 2, (r % 2) * 256 + (P if b == 0 else 0):(r % 2) * 256 + 256]
                    last = pe.matmul(dst, q2[rows_, kt * 4 + r, b * P:(b + 1) * P],
                                     k2[rows_, kt, max(b - 1, 0) * P:(b + 1) * P], start=True, stop=True)
                last.then_inc(sc2, 1)

            def swa_values(n):
                b, kt, half = groups[n]
                tiles = (1,) if b == 0 else (0, 1)
                pe.wait_ge(pn2, n + 1)
                if n:
                    pe.wait_ge(ptc2, n)
                for s in tiles:
                    for r in range(4):
                        last = pe.transpose(ps[:, 4 + s, r * P:(r + 1) * P], s2[:, n % 2, r * 256 + s * P:r * 256 + (s + 1) * P], ident)
                last.then_inc(pt2, 1)
                pe.wait_ge(ptc2, n + 1)
                if n >= 2:
                    pe.wait_ge(o2, n - 1)
                rows_ = slice(half * HD2, (half + 1) * HD2)
                kv = 2 * kt + half
                for s in tiles:
                    last = pe.matmul(ps[rows_, 6 + n % 2, :], v2[:, b - 1 + s, kv * HD2:(kv + 1) * HD2], p2T[:, s, :],
                                     start=(s == tiles[0]), stop=(s == 1))
                last.then_inc(pv2, 1)

            swa_scores(0)
            for n in range(len(groups)):
                if n + 1 < len(groups):
                    swa_scores(n + 1)
                swa_values(n)

            pe.wait_ge(o2, len(groups))
            strips(SO, KT, b_hi, b_lo)
            norm_stats(5)
            pe.wait_ge(h_ready, 5 * KT)
            strips(GU, 2 * FT, a_hi, a_lo)
            pe.wait_ge(bank_free, r_of(DN) + 4)
            for u in range(4):
                rows(DN + u, u, u, dlo_ready, b_hi, b_lo, u, u == 0, False, None)
            with pe.Fori(1, FT // 4) as i:
                for u in range(4):
                    rows(i * 4 + (DN + u), u, i * 4 + u, dlo_ready, b_hi, b_lo, u, False, False, None)
            for u in range(FT % 4):
                n = FT - FT % 4 + u
                rows(DN + n, u, n, dlo_ready, b_hi, b_lo, u, False, n == FT - 1, None)
            pe.wait_ge(y2_done, KT)
            norm_stats(6)

        @block.scalar
        def _(act):
            def hi(g, u, i=None):
                act.wait_ge(landed[u % RAW], (g // 4 + 1) * 16 if i is None else i)
                act.wait_ge(used, g - SPLIT + 1)
                act.activation(whi[:, u % SPLIT, :], raw[:, u % RAW, :], ACT.Copy).then_inc(hi_ready, 1)

            def hi_next(i, first, u):
                hi(i * 4 + (first + u + 1), u + 1, (i + (first + u + 1) // 4 + 1) * 16)

            def step(i, first, u):
                hi_next(i, first, u)
                act.wait_ge(used, i * 4 + (first + u + 1))

            def norm_sq(n, src, width=T):
                for k in range(KT):
                    if n or k >= 2:
                        act.wait_ge(sq_used, n * KT + k - 1)
                    act.activation(sq[:, k % 2, 0:width], src[:, k, 0:width], ACT.Square).then_inc(sq_ready, 1)
                act.wait_ge(sq_used, (n + 1) * KT)
                act.activation(rstd[:, 0:width], ps[:, 4, 0:width], ACT.Sqrt, bias=EPS, scale=1.0 / D).then_inc(rt_ready, 1)

            def norm_hi(n, dst, shift, width=T):
                for k in range(KT):
                    act.wait_ge(nt_ready, n * KT + k + 1)
                    act.activation(dst[:, k, 0:width], nt[:, k % 2, 0:width], ACT.Identity, bias=shift(k)).then_inc(nhi_ready, 1)

            act.wait_ge(small_in, 16)
            c_in = col("c", 0, 2 * KT).rearrange("p (a b) -> p a b", b=2)
            act.activation(c_act[:, :, :], c_in, ACT.Silu).then_inc(c_ready, 1)
            act.wait_ge(x_in, 16)
            norm_sq(0, x)
            norm_hi(0, a_hi, lambda k: mod[:, k, 0:1])
            act.wait_ge(ctx_in, 16)
            act.wait_ge(h_ready, KT)
            norm_sq(1, x_ctx, CTX)
            norm_hi(1, b_hi, lambda k: mod[:, k, 1:2], CTX)
            hi(U, 0)

            def gates(first, count, bank_of):
                with act.Fori(0, count // 4) as i:
                    for u in range(4):
                        step(i, first, u)
                        if u % 2:
                            act.activation(sq[:, u // 2, :], ps[:, bank_of(u), :], ACT.Sigmoid).then_inc(gate_ready, 1)

            gates(U, 2 * KT, lambda u: u)

            def head_sq(n, src, width=T):
                act.activation(sq[:, n % 2, 0:width], src, ACT.Square).then_inc(ksq, 1)

            def head_rt(n, width=T):
                act.wait_ge(kstat, n + 1)
                act.activation(rstd[:, 0:width], ps[:, 4, 0:width], ACT.Sqrt, bias=EPS, scale=1.0 / P).then_inc(krt, 1)

            for u in range(4):
                hi_next(0, KV, u)
            act.wait_ge(used, KV + 2)
            for u in range(2):
                if u:
                    act.wait_ge(kn, 2)
                head_sq(2 * u, ps[:, u, :])
                head_sq(2 * u + 1, ps[:, 6, u * CTX:(u + 1) * CTX], CTX)
                for n, w in ((2 * u, T), (2 * u + 1, CTX)):
                    if n:
                        act.wait_ge(kn, n)
                    head_rt(n, w)
            with act.Fori(0, NH // 4) as i:
                for u in range(5):
                    if u < 4:
                        step(i, Q, u)
                        head_sq(u, ps[:, u, :])
                        act.wait_ge(kstat, i * 4 + (4 + u + 1))
                        act.wait_ge(kn, i * 4 + (4 + u))
                        act.activation(rstd[:, :], ps[:, 4, :], ACT.Sqrt, bias=EPS, scale=1.0 / P).then_inc(krt, 1)

            def att(i, hu, t):
                n = (i * 2 + hu) * TT + t
                act.wait_ge(mx_ready, n + 1)
                act.activation(prob[:, t % 2, :], ps[:, 2 * (t % 2):2 * (t % 2) + 2, :].rearrange("p a b -> p (a b)")[:, 0:S1],
                               ACT.Exp, bias=tiny[:, t:t + 1], scale=P ** -0.5, accum_out=tiny[:, 8 + t:9 + t]).then_inc(p_ready, 1)

            def att_T(i, hu, t):
                n = (i * 2 + hu) * TT + t
                act.wait_ge(pt_ready, n + 1)
                act.activation(probT[:, :, t * P:(t + 1) * P].rearrange("p (a s) n -> p a s n", a=2),
                               ps[:, 4:6, 0:3 * P].rearrange("p a (s n) -> p a s n", n=P), ACT.Copy).then_inc(pt_done, 1)

            with act.Fori(0, NH // 2) as i:
                for hu in range(2):
                    att(i, hu, 0)
                    for t in range(TT):
                        if t + 1 < TT:
                            att(i, hu, t + 1)
                        att_T(i, hu, t)
                    act.wait_ge(pv_ready, i * 2 + (hu + 1))
                    act.activation(b_hi[:, bass.ds(i * 2 + hu, 1), :], ps[:, 6 + hu, :], ACT.Copy).then_inc(ohi_ready, 1)

            gates(AO, 2 * KT, lambda u: u - 1)

            for k in range(KT):
                act.wait_ge(cv_xc, k + 1)
                if k >= 2:
                    act.wait_ge(cv_used, k - 1)
                act.activation(sq[:, k % 2, :], conv[:, k, :], ACT.Square).then_inc(cv_sq, 1)
            act.wait_ge(cv_used, KT)
            act.activation(rstd[:, :], ps[:, 5, :], ACT.Sqrt, bias=EPS, scale=1.0 / D).then_inc(cv_rt, 1)
            for k in range(KT):
                act.wait_ge(cv_t, k + 1)
                if k >= 2:
                    act.wait_ge(cv_ready, k - 1)
                act.activation(sq[:, k % 2, :], nt[:, k % 2, :], ACT.Silu, bias=col("ln_b", k), scale=col("ln_g", k)).then_inc(cv_act, 1)
                act.wait_ge(cv_act, k + 1)
                act.activation(b_hi[:, k, :], sq[:, k % 2, :], ACT.Copy).then_inc(cv_hi, 1)

            gates(CO, 2 * KT, lambda u: u - 1)
            act.wait_ge(used, WO)
            for k in range(KT):
                act.wait_ge(pair_done, KT + k + 1)
                act.activation(a_hi[:, k, :], merged[:, k, :], ACT.Copy).then_inc(mhi_ready, 1)

            def only_panels(first, count):
                with act.Fori(0, count // 4) as i:
                    for u in range(4):
                        hi_next(i, first, u)

            only_panels(WO, KT)
            act.wait_ge(x_ready, KT)
            norm_sq(2, x)
            norm_hi(2, b_hi, lambda k: mod[:, 3 * KT + k, 0:1])

            with act.Fori(0, HP // 4) as i:
                for u in range(4):
                    step(i, WQ, u)
                    act.activation(q_key[:, u % 2, :], ps[:, u, :], ACT.Copy)\
                       .then_inc(bank_free, 1)
                    act.wait_ge(bank_free, i * 4 + (4 + r_of(WQ) + u + 1))
                    act.sem_inc(qk_ready, 1)

            def gelu(i, u):
                hi_next(i, EU, u)
                act.wait_ge(used, i * 4 + (EU + u + 1))
                if not isinstance(i, int) or i:
                    act.wait_ge(ge_out[u], i * 16)
                act.activation(ge_slot[:, u, :], ps[:, u, :], ACT.Gelu).then_inc(bank_free, 1)
                act.wait_ge(bank_free, i * 4 + (4 + r_of(EU) + u + 1))
                act.dma_start(ge_d[bass.ds(i * 4 + u, 1)].rearrange("a p n -> (a p) n"), ge_slot[:, u, :]).then_inc(ge_out[u], 16)

            for u in range(4):
                gelu(0, u)
            with act.Fori(1, E_SOFT // 4) as i:
                for u in range(4):
                    gelu(i, u)
            act.wait_ge(soft_d, 1)
            act.activation(best, best, ACT.Exp).then_inc(soft_e, 1)
            with act.Fori(E_SOFT // 4, E_W // 4) as i:
                for u in range(4):
                    gelu(i, u)

            def stage_w(j, chunk, c, u):
                for v in range(2):
                    batch = 8 * c + 2 * u + v
                    act.wait_ge(w_staged, j * 32 + (chunk * 16 + batch + 1))
                    act.activation(stage[chunk][:, :, batch * 4:batch * 4 + 4],
                                   ps[:, 4 + batch % 4, :].rearrange("p (t k) -> p k t", t=4), ACT.Copy).then_inc(w_ready, 1)

            def chunks(j):
                for chunk in range(2):
                    for c in range(2):
                        for u in range(4):
                            gelu(j * 4 + (E_W // 4 + 2 * chunk + c), u)
                            if c == u == 0 and (not isinstance(j, int) or j):
                                act.wait_ge(w_out[chunk], j * 16)
                            stage_w(j, chunk, c, u)
                    act.wait_ge(w_ready, j * 32 + (chunk + 1) * 16)
                    act.dma_start(w_d.rearrange("i j (c t) -> c j i t", t=64)[bass.ds(j * 2 + chunk, 1)].rearrange("c j i t -> (c j) i t"),
                                  stage[chunk]).then_inc(w_out[chunk], 16)

            chunks(0)
            with act.Fori(1, 4) as j:
                chunks(j)

            with act.Fori(E_W // 4 + T // 32, NK // 4) as i:
                for u in range(4):
                    gelu(i, u)

            def z_hi(i, u):
                n = i * 4 + u
                act.wait_ge(z_ready, n + 1)
                if not isinstance(n, int) or n >= 4:
                    act.wait_ge(used, n + (EV - 4 + 1))
                act.activation(a_hi[:, u % 4, :], z[:, u % 2, :], ACT.Copy).then_inc(zhi_ready, 1)

            z_hi(0, 0)
            for u in range(4):
                z_hi(0, u + 1)
                hi_next(0, EV, u)
            with act.Fori(1, NK // 4 - 1) as i:
                for u in range(4):
                    z_hi(i, u + 1)
                    hi_next(i, EV, u)
            for u in range(4):
                if u < 3:
                    z_hi(NK // 4 - 1, u + 1)
                hi_next(NK // 4 - 1, EV, u)

            act.wait_ge(y_done, KT)
            norm_sq(3, x)
            act.wait_ge(x_ready, 2 * KT)
            norm_sq(4, x)
            norm_hi(3, a_hi, lambda k: col("zero"))
            only_panels(SW, 12)

            groups = [(b, kt, half) for b in range(TT) for kt in range(2) for half in range(2)]

            def swa_exp(n):
                o = 32 * (n % 2)
                act.wait_ge(nmx2, n + 1)
                for r in range(4):
                    last = act.activation(s2[:, n % 2, r * 256:(r + 1) * 256], s2[:, n % 2, r * 256:(r + 1) * 256], ACT.Exp,
                                          bias=tiny[:, o + 4 + r:o + 5 + r], accum_out=tiny[:, o + 8 + r:o + 9 + r])
                    last.then_inc(e2, 1)
                for r in range(4):
                    h = 8 * groups[n][1] + 4 * groups[n][2] + r
                    act.activation(tiny[:, o + 12 + r:o + 13 + r], col("sinks", h), ACT.Exp, bias=tiny[:, o + 4 + r:o + 5 + r]).then_inc(snk2, 1)

            def swa_out(n):
                b, kt, half = groups[n]
                act.wait_ge(pt2, n + 1)
                if b == 0:
                    act.activation(p2T[:, 1, :], ps[:, 5, :], ACT.Copy).then_inc(ptc2, 1)
                else:
                    act.activation(p2T[:, :, :], ps[:, 4:6, :], ACT.Copy).then_inc(ptc2, 1)
                act.wait_ge(pv2, n + 1)
                rows_ = slice(half * HD2, (half + 1) * HD2)
                act.activation(b_hi[rows_, kt * 4:kt * 4 + 4, b * P:(b + 1) * P],
                               ps[rows_, 6 + n % 2, :].rearrange("p (r t) -> p r t", r=4), ACT.Copy).then_inc(ohi2, 1)

            swa_exp(0)
            for n in range(len(groups)):
                if n + 1 < len(groups):
                    swa_exp(n + 1)
                swa_out(n)

            only_panels(SO, KT)
            act.wait_ge(x_ready, 3 * KT)
            norm_sq(5, x)
            norm_hi(4, a_hi, lambda k: col("zero"))
            with act.Fori(0, 2 * FT // 4) as i:
                for u in range(4):
                    step(i, GU, u)
                    if u % 2 == 0:
                        act.activation(sq[:, u // 2, :], ps[:, u, :], ACT.Silu).then_inc(gate_ready, 1)

            def hid_hi(i, u):
                n = i * 4 + u
                if not isinstance(n, int) or n >= 4:
                    act.wait_ge(used, n + (DN - 4 + 1))
                act.activation(b_hi[:, u % 4, :], hid[:, bass.ds(n, 1), :] if not isinstance(n, int) else hid[:, n, :],
                               ACT.Copy).then_inc(dhi_ready, 1)

            act.wait_ge(act_done, FT)
            hid_hi(0, 0)
            for u in range(4):
                hid_hi(0, u + 1)
                hi_next(0, DN, u)
            with act.Fori(1, FT // 4) as i:
                for u in range(4):
                    hid_hi(i, u + 1)
                    hi_next(i, DN, u)
            hid_hi(FT // 4, 1)
            hi_next(FT // 4, DN, 0)
            act.wait_ge(y2_done, KT)
            norm_sq(6, x)

        @block.vector
        def _(dve):
            def lo(g, u):
                dve.wait_ge(hi_ready, g + (1 - U))
                dve.tensor_tensor(wlo[:, u % SPLIT, :], raw[:, u % RAW, :], f32(whi[:, u % SPLIT, :]), ALU.subtract).then_inc(lo_ready, 1)

            def lo_next(i, first, u):
                lo(i * 4 + (first + u + 1), u + 1)

            def done(i, first, u):
                dve.wait_ge(used, i * 4 + (first + u + 1))

            def step(i, first, u):
                lo_next(i, first, u)
                dve.wait_ge(used, i * 4 + (first + u + 1))

            def norm_rstd(n, width=T):
                dve.wait_ge(rt_ready, n + 1)
                dve.reciprocal(rstd[:, 0:width], rstd[:, 0:width]).then_inc(rstd_ready, 1)
                dve.wait_ge(rstd_ready, n + 1)

            def norm_apply(m, src, gain, shift, hi_, lo_, width=T):
                def low(k):
                    dve.wait_ge(nhi_ready, m * KT + k + 1)
                    dve.scalar_tensor_tensor(lo_[:, k, 0:width], nt[:, k % 2, 0:width], shift(k), f32(hi_[:, k, 0:width]),
                                             ALU.add, ALU.subtract).then_inc(h_ready, 1)
                for k in range(KT):
                    if k >= 2:
                        low(k - 2)
                        dve.wait_ge(h_ready, m * KT + k - 1)
                    elif m:
                        dve.wait_ge(h_ready, m * KT)
                    dve.scalar_tensor_tensor(nt[:, k % 2, 0:width], src[:, k, 0:width], gain(k), rstd[:, 0:width],
                                             ALU.mult, ALU.mult).then_inc(nt_ready, 1)
                low(KT - 2)
                low(KT - 1)

            dve.wait_ge(used, U)
            dve.tensor_tensor(mod[:, :, :], ps[:, 7, 0:2 * MOD_N].rearrange("p (n c) -> p n c", c=2),
                              col("b_mod", 0, MOD_N).unsqueeze(2).to_broadcast([P, MOD_N, 2]), ALU.add).then_inc(mod_done, 1)
            dve.wait_ge(mod_done, 1)
            for dst, at, c, gname in ((gs1, KT, 0, "norm1"), (gs1c, KT, 1, "norm1"), (gs2, 4 * KT, 0, "norm2")):
                dve.scalar_tensor_tensor(dst[:, :], mod[:, at:at + KT, c], 1.0, col(gname, 0, KT), ALU.add, ALU.mult).then_inc(mod_done, 1)
            for _ in range(4):
                dve.sem_inc(bank_free, 1)
            dve.wait_ge(mod_done, 4)
            dve.wait_ge(x_in, 16)
            norm_rstd(0)
            norm_apply(0, x, lambda k: gs1[:, k:k + 1], lambda k: mod[:, k, 0:1], a_hi, a_lo)
            norm_rstd(1, CTX)
            norm_apply(1, x_ctx, lambda k: gs1c[:, k:k + 1], lambda k: mod[:, k, 1:2], b_hi, b_lo, CTX)

            def taps(i, odd, lo_tap, hi_tap):
                for j in range(lo_tap, hi_tap):
                    n = i * TAPS + (odd * (KT // 2) * TAPS + j)
                    acc = conv[:, bass.ds(i * 2 + odd, 1), :]
                    src = g_pad[:, bass.ds(i * 2 + odd, 1), j:j + T]
                    w = sm[:, bass.ds(i * (2 * TAPS) + (SMALL["conv_w"][0] + odd * TAPS + j), 1)]
                    if j == 0:
                        b = sm[:, bass.ds(i * 2 + (SMALL["conv_b"][0] + odd), 1)]
                        dve.tensor_scalar(acc, src, w, b, ALU.mult, ALU.add).then_inc(tap_done, 1)
                    else:
                        dve.wait_ge(tap_done, n)
                        dve.scalar_tensor_tensor(acc, src, w, acc, ALU.mult, ALU.add).then_inc(tap_done, 1)

            dve.wait_ge(pad_ready, 1)
            with dve.Fori(0, KT // 2) as i:
                for u in range(4):
                    if u % 2:
                        done(i, U, u)
                        p = i * 2 + u // 2
                        dve.wait_ge(gate_ready, p + 1)
                        dve.tensor_tensor(g_pad[:, bass.ds(p, 1), PAD:PAD + T], sq[:, u // 2, :], ps[:, u - 1, :],
                                          ALU.mult).then_inc(pair_done, 1)
                        dve.wait_ge(pair_done, p + 1)
                        dve.sem_inc(bank_free, 2)
                        taps(i, 0, u // 2 * 16, min(u // 2 * 16 + 16, TAPS))

            def head(n, m, src, gain, dst, width=T, rotate=True):
                dve.wait_ge(krt, n + 1)
                dve.reciprocal(rstd[:, 0:width], rstd[:, 0:width]).then_inc(krstd, 1)
                dve.wait_ge(krstd, n + 1)
                if not rotate:
                    return dve.scalar_tensor_tensor(dst, src, gain, rstd[:, 0:width], ALU.mult, ALU.mult).then_inc(kn, 1)
                dve.scalar_tensor_tensor(q_n[:, n % 2, :], src, gain, rstd[:, :], ALU.mult, ALU.mult).then_inc(kn, 1)

            def turn(n, m, slot, dst):
                dve.wait_ge(kn, n + 1)
                dve.tensor_tensor(q_rot[:, 0, :], q_n[:, slot, :], cos, ALU.mult).then_inc(kcos, 1)
                dve.wait_ge(krot, m + 1)
                dve.tensor_tensor(q_rot[:, 1, :], ps[:, 5, :], sin, ALU.mult).then_inc(ksin, 1)
                dve.wait_ge(kcos, m + 1)
                dve.wait_ge(ksin, m + 1)
                dve.tensor_tensor(dst, q_rot[:, 0, :], q_rot[:, 1, :], ALU.add).then_inc(k_done, 1)
                dve.wait_ge(k_done, m + 1)

            dve.wait_ge(rope_in, 16)
            for u in range(2):
                dve.wait_ge(used, KV + 2)
                head(2 * u, u, ps[:, u, :], col("k_g"), None)
                head(2 * u + 1, u, ps[:, 6, u * CTX:(u + 1) * CTX], col("k_g"), kT[:, u, T:S1], CTX, False)
                dve.wait_ge(kn, 2 * u + 2)
                dve.sem_inc(bank_free, 1)
                turn(2 * u, u, 0, kT[:, u, 0:T])
            dve.wait_ge(used, KV + 4)
            for u in range(2):
                dve.tensor_copy(v_feat[:, u, 0:T], ps[:, 2 + u, :]).then_inc(v_feat_ready, 1)
                dve.tensor_copy(v_feat[:, u, T:S1], ps[:, 7, u * CTX:(u + 1) * CTX]).then_inc(v_feat_ready, 1)
            dve.wait_ge(v_feat_ready, 4)
            dve.sem_inc(bank_free, 2)
            for u in range(2):
                dve.wait_ge(v_turned, u + 1)
                dve.tensor_copy(v_tok[:, :, u * P:(u + 1) * P].rearrange("p (a s) n -> p a s n", a=2),
                                ps[:, 4:6, 0:3 * P].rearrange("p a (s n) -> p a s n", n=P)).then_inc(v_done, 1)
            with dve.Fori(0, NH // 4) as i:
                for u in range(4):
                    done(i, Q, u)
                    n = i * 4 + (4 + u)
                    m = i * 4 + (2 + u)
                    dve.wait_ge(krt, n + 1)
                    dve.reciprocal(rstd[:, :], rstd[:, :]).then_inc(krstd, 1)
                    dve.wait_ge(krstd, n + 1)
                    dve.scalar_tensor_tensor(q_n[:, u % 2, :], ps[:, u, :], col("q_g"), rstd[:, :], ALU.mult, ALU.mult).then_inc(kn, 1)
                    dve.wait_ge(kn, n + 1)
                    dve.sem_inc(bank_free, 1)
                    turn(n, m, u % 2, qT[:, bass.ds(i * 4 + u, 1), :])

            def att_max(i, hu, t):
                n = (i * 2 + hu) * TT + t
                dve.wait_ge(sc_ready, n + 1)
                dve.tensor_reduce(tiny[:, 4 + t:5 + t], ps[:, 2 * (t % 2):2 * (t % 2) + 2, :].rearrange("p a b -> p (a b)")[:, 0:S1],
                                  AX.X, ALU.max).then_inc(rs_ready, 1)
                dve.wait_ge(rs_ready, n * 3 + 1)

            def att_in(i, hu, t):
                n3 = ((i * 2 + hu) * TT + t) * 3
                dve.wait_ge(sc_ready, (i * 2 + hu) * TT + (t + 1))
                dve.tensor_reduce(tiny[:, 4 + t:5 + t], ps[:, 2 * (t % 2):2 * (t % 2) + 2, :].rearrange("p a b -> p (a b)")[:, 0:S1],
                                  AX.X, ALU.max).then_inc(rs_ready, 1)

            def att_neg(i, hu, t, done):
                dve.wait_ge(rs_ready, done)
                dve.tensor_scalar(tiny[:, t:t + 1], tiny[:, 4 + t:5 + t], -(P ** -0.5), None, ALU.mult).then_inc(mx_ready, 1)

            def att_norm(i, hu, t, done):
                n = (i * 2 + hu) * TT + t
                dve.wait_ge(p_ready, n + 1)
                dve.reciprocal(tiny[:, 12 + t:13 + t], tiny[:, 8 + t:9 + t]).then_inc(rs_ready, 1)
                dve.wait_ge(rs_ready, done)
                dve.tensor_scalar(prob[:, t % 2, :], prob[:, t % 2, :], tiny[:, 12 + t:13 + t], None, ALU.mult).then_inc(pn_ready, 1)

            with dve.Fori(0, NH // 2) as i:
                for hu in range(2):
                    h = i * 2 + hu
                    c = h * (2 * TT)
                    dve.tensor_copy(q_slot[:, hu, :], qT[:, bass.ds(h, 1), :]).then_inc(qs_ready, 1)
                    k = 0
                    for t in range(-1, TT):
                        if t + 1 < TT:
                            att_in(i, hu, t + 1)
                            k += 1
                            att_neg(i, hu, t + 1, c + k)
                        if t >= 0:
                            k += 1
                            att_norm(i, hu, t, c + k)
                    dve.wait_ge(ohi_ready, h + 1)
                    dve.tensor_tensor(b_lo[:, bass.ds(h, 1), :], ps[:, 6 + hu, :], f32(b_hi[:, bass.ds(h, 1), :]), ALU.subtract).then_inc(o_ready, 1)

            with dve.Fori(0, 2) as i:
                for u in range(KT):
                    if u % 2:
                        p = i * (KT // 2) + u // 2
                        dve.wait_ge(used, i * KT + (AO + u + 1))
                        dve.wait_ge(gate_ready, p + (KT + 1))
                        dve.tensor_tensor(merged[:, bass.ds(p, 1), :], sq[:, u // 2 % 2, :], ps[:, u % 4, :], ALU.mult).then_inc(co_mul, 1)
                        dve.wait_ge(co_mul, p + 1)
                        dve.sem_inc(bank_free, 2)
                        taps(i, 1, u // 2 * 8, min(u // 2 * 8 + 8, TAPS))

            dve.wait_ge(cv_sum, 1)
            dve.tensor_scalar(nt[:, 0, :], ps[:, 4, :], 1.0 / D, None, ALU.mult).then_inc(cv_mu, 1)
            dve.wait_ge(cv_mu, 1)
            for k in range(KT):
                dve.tensor_tensor(conv[:, k, :], conv[:, k, :], nt[:, 0, :], ALU.subtract).then_inc(cv_xc, 1)
            dve.wait_ge(cv_rt, 1)
            dve.reciprocal(rstd[:, :], rstd[:, :]).then_inc(cv_rstd, 1)
            dve.wait_ge(cv_rstd, 1)
            dve.wait_ge(cv_xc, KT)
            for k in range(KT + 1):
                if k < KT:
                    if k >= 2:
                        dve.wait_ge(cv_act, k - 1)
                    dve.tensor_tensor(nt[:, k % 2, :], conv[:, k, :], rstd[:, :], ALU.mult).then_inc(cv_t, 1)
                if k:
                    dve.wait_ge(cv_hi, k)
                    dve.tensor_tensor(b_lo[:, k - 1, :], sq[:, (k - 1) % 2, :], f32(b_hi[:, k - 1, :]), ALU.subtract).then_inc(cv_ready, 1)

            with dve.Fori(0, KT // 2) as i:
                for u in range(4):
                    if u % 2:
                        done(i, CO, u)
                        p = i * 2 + u // 2
                        dve.wait_ge(gate_ready, p + (2 * KT + 1))
                        dve.tensor_tensor(nt[:, u // 2, :], sq[:, u // 2, :], ps[:, u, :], ALU.mult).then_inc(co_mul, 1)
                        dve.wait_ge(co_mul, p + (KT + 1))
                        dve.sem_inc(bank_free, 2)
                        dve.tensor_tensor(merged[:, bass.ds(p, 1), :], merged[:, bass.ds(p, 1), :], nt[:, u // 2, :], ALU.add).then_inc(pair_done, 1)
            for k in range(KT):
                dve.wait_ge(mhi_ready, k + 1)
                dve.tensor_tensor(a_lo[:, k, :], merged[:, k, :], f32(a_hi[:, k, :]), ALU.subtract).then_inc(m_ready, 1)

            def add_to_x(first, count, gain, ready0, arrived):
                with dve.Fori(0, count // 4) as i:
                    for u in range(4):
                        arrived(i, first, u)
                        n = i * 4 + u
                        xn = x[:, bass.ds(n, 1), :]
                        if gain is None:
                            dve.tensor_tensor(xn, ps[:, u, :], xn, ALU.add).then_inc(x_ready, 1)
                        else:
                            dve.scalar_tensor_tensor(xn, ps[:, u, :], mod[:, bass.ds(n + gain, 1), 0], xn, ALU.mult, ALU.add).then_inc(x_ready, 1)
                        dve.wait_ge(x_ready, n + (ready0 + 1))
                        dve.sem_inc(bank_free, 1)

            add_to_x(WO, KT, 2 * KT, 0, done)
            norm_rstd(2)
            norm_apply(2, x, lambda k: gs2[:, k:k + 1], lambda k: mod[:, 3 * KT + k, 0:1], b_hi, b_lo)

            sc4 = scores.rearrange("p (t c) n -> p t c n", t=TT)
            with dve.Fori(0, HP // 4) as i:
                for u in range(1, 5):
                        dve.wait_ge(s_ready, i * 4 + u)
                        dve.tensor_copy(sc4[:, :, bass.ds(i * 4 + (u - 1), 1), :].rearrange("p t c n -> p t (c n)"),
                                        ps[:, 3 + u, :].rearrange("p (t n) -> p t n", n=P)).then_inc(s_done, 1)

            held = tiny[:, 56:60]
            iota16 = col("iota", 0, TOPK)
            flat = lambda ap: ap.rearrange("p a b -> p (a b)")
            row = lambda ap, n: ap[:, bass.ds(n, 1), :].rearrange("p a n -> p (a n)")

            def chains(sem_, base, count):
                total, mark = [0], [0] * count

                def did(c, ins):
                    ins.then_inc(sem_, 1)
                    total[0] += 1
                    mark[c] = total[0]

                def after(c):
                    dve.wait_ge(sem_, base + mark[c])
                    dve.memset(held[:, c:c + 1], 0.0)
                return did, after, total

            def top16(did, after, src, rep, vals, idx):
                all_ = range(len(src))
                for c in all_:
                    after(c)
                    did(c, dve.max(vals[c][:, 0:8], src[c]))
                for c in all_:
                    after(c)
                    did(c, dve.max_index(idx[c][:, 0:8], vals[c][:, 0:8], src[c]))
                    did(c, dve.match_replace(rep[c], vals[c][:, 0:8], src[c], -3.0e38))
                for c in all_:
                    after(c)
                    did(c, dve.max(vals[c][:, 8:16], rep[c]))
                for c in all_:
                    after(c)
                    did(c, dve.max_index(idx[c][:, 8:16], vals[c][:, 8:16], rep[c]))

            A, C1 = A_TK, 4
            words = 2 * NK + 2 * TOPK
            s_in = [area(A + c * words, NK) for c in range(C1)]
            s_rep = [area(A + c * words + NK, NK) for c in range(C1)]
            v16 = [area(A + c * words + 2 * NK, TOPK) for c in range(C1)]
            i16 = [area(A + c * words + 2 * NK + TOPK, TOPK).bitcast(U32) for c in range(C1)]
            L1 = 8 * C1
            with dve.Fori(0, 64 // C1) as i:
                did, after, total = chains(lv1, i * L1, C1)
                for c in range(C1):
                    did(c, dve.tensor_copy(s_in[c], row(scores, i * C1 + c)))
                top16(did, after, s_in, s_rep, v16, i16)
                for c in range(C1):
                    after(c)
                    did(c, dve.tensor_copy(row(v1, i * C1 + c), v16[c]))
                    did(c, dve.tensor_copy(row(i1, i * C1 + c), i16[c]))
                after(C1 - 1)
                assert total[0] == L1
            C2 = 2
            words = 2 * TOPK * TOPK + 4 * TOPK + 2 * TOPK * TOPK
            at = lambda c, o: A + c * words + o
            cand = [area(at(c, 0), TOPK, TOPK) for c in range(C2)]
            cand_rep = [area(at(c, 256), TOPK * TOPK) for c in range(C2)]
            b16 = [area(at(c, 512), TOPK) for c in range(C2)]
            pos = [area(at(c, 528), TOPK).bitcast(U32) for c in range(C2)]
            pos2 = [area(at(c, 544), 2, TOPK).bitcast(U32) for c in range(C2)]
            eq = [area(at(c, 576), 2, TOPK * TOPK) for c in range(C2)]
            assert 2 * words <= A_KEYS - A_TK
            L2 = 12 * C2
            with dve.Fori(0, 32 // C2) as i:
                did, after, total = chains(lv2, i * L2, C2)
                for c in range(C2):
                    n = i * C2 + c
                    did(c, dve.tensor_tensor(cand[c], row(v1, n * 2).unsqueeze(2).to_broadcast([P, TOPK, TOPK]),
                                             row(v1, n * 2 + 1).unsqueeze(1).to_broadcast([P, TOPK, TOPK]), ALU.add))
                top16(did, after, [flat(v) for v in cand], cand_rep, b16, pos)
                for c in range(C2):
                    after(c)
                    did(c, dve.tensor_copy(row(best, i * C2 + c), b16[c]))
                    did(c, dve.tensor_scalar(pos2[c][:, 0, :], pos[c], 4, None, ALU.logical_shift_right))
                    did(c, dve.tensor_scalar(pos2[c][:, 1, :], pos[c], TOPK - 1, None, ALU.bitwise_and))
                for c in range(C2):
                    after(c)
                    did(c, dve.tensor_tensor(eq[c].rearrange("p c (k a) -> p (c k) a", a=TOPK),
                                             pos2[c].rearrange("p c k -> p (c k)").unsqueeze(2).to_broadcast([P, 2 * TOPK, TOPK]),
                                             iota16.unsqueeze(1).to_broadcast([P, 2 * TOPK, TOPK]), ALU.is_equal))
                eq5 = [v.rearrange("p c (k a) -> p c k a", a=TOPK) for v in eq]
                for c in range(C2):
                    after(c)
                    did(c, dve.tensor_tensor(eq5[c], eq5[c], i1[:, bass.ds((i * C2 + c) * 2, 2), :].unsqueeze(2).to_broadcast([P, 2, TOPK, TOPK]),
                                             ALU.mult))
                for c in range(C2):
                    after(c)
                    did(c, dve.tensor_reduce(ij[:, :, bass.ds((i * C2 + c) * TOPK, TOPK)], eq5[c], AX.X, ALU.add))
                after(C2 - 1)
                assert total[0] == L2
            mx = area(A, 32)
            dve.tensor_copy(mx.unsqueeze(2), best[:, :, 0:1]).then_inc(mx_ready, 1)
            dve.wait_ge(mx_ready, NH * TT + 1)
            dve.tensor_tensor(best, best, mx.unsqueeze(2).to_broadcast([P, 32, TOPK]), ALU.subtract).then_inc(soft_d, 1)
            dve.wait_ge(soft_e, 1)
            den = area(A + 32, 32)
            dve.tensor_reduce(den, best, AX.X, ALU.add).then_inc(mx_ready, 1)
            dve.wait_ge(mx_ready, NH * TT + 2)
            dve.reciprocal(mx, den).then_inc(mx_ready, 1)
            dve.wait_ge(mx_ready, NH * TT + 3)
            dve.tensor_tensor(best, best, mx.unsqueeze(2).to_broadcast([P, 32, TOPK]), ALU.mult).then_inc(soft, 1)
            dve.wait_ge(ijw_t, 1)
            dve.tensor_copy(tok_i, ps[:, 4, :]).then_inc(ijw, 1)
            dve.tensor_copy(tok_j, ps[:, 5, :]).then_inc(ijw, 1)
            dve.tensor_copy(w_bf, ps[:, 6, :]).then_inc(ijw, 1)
            dve.tensor_copy(iota_b[:, :], col("iota", 0, P)).then_inc(ijw, 1)
            dve.wait_ge(ijw, 3)
            dve.tensor_copy(tok_w[0], w_bf).then_inc(ijw, 1)
            dve.wait_ge(ijw, 5)
            dve.tensor_tensor(tok_w[2], ps[:, 6, :], tok_w[0], ALU.subtract).then_inc(ijw, 1)
            dve.wait_ge(ijw, 6)
            dve.tensor_copy(w_bf, tok_w[2]).then_inc(ijw, 1)
            dve.wait_ge(ijw, 7)
            dve.tensor_copy(tok_w[1], w_bf).then_inc(ijw, 1)
            dve.wait_ge(ijw, 8)
            dve.tensor_tensor(tok_w[2], tok_w[2], tok_w[1], ALU.subtract).then_inc(ijw, 1)
            dve.wait_ge(ijw, 9)
            def one_hot(n, v):
                for t in range(4):
                    at = bass.ds(n * 4 + t, 1) if not isinstance(n, int) else slice(n * 4 + t, n * 4 + t + 1)
                    dve.tensor_scalar(hot[v][:, t, 0, :], iota_b[:, :], tok_j[:, at], None, ALU.is_equal)
                    for c in range(3):
                        last = dve.tensor_scalar(hot[v][:, t, c + 1, :], iota_b[:, :], tok_i[:, at], tok_w[c][:, at],
                                                 ALU.is_equal, ALU.mult)
                last.then_inc(hot_ready, 1)

            one_hot(0, 0)
            one_hot(1, 1)
            with dve.Fori(1, T // 8) as i:
                for v in range(2):
                    dve.wait_ge(w_staged, i * 2 + (v - 1))
                    one_hot(i * 2 + v, v)

            def weigh(i, u):
                n = i * 4 + u
                slot, times = u % 4, u // 4
                dve.wait_ge(wg_in[slot], (i + times + 1) * 32)
                if not isinstance(n, int) or n >= 2:
                    dve.wait_ge(zlo_ready, n - 1)
                dve.tensor_tensor(z[:, u % 2, :], w_ring[:, slot, :], ge_ring[:, slot, :], ALU.mult).then_inc(z_ready, 1)

            def z_lo(i, u):
                dve.wait_ge(zhi_ready, i * 4 + (u + 1))
                dve.tensor_tensor(a_lo[:, u % 4, :], z[:, u % 2, :], f32(a_hi[:, u % 4, :]), ALU.subtract).then_inc(zlo_ready, 1)

            weigh(0, 0)
            weigh(0, 1)
            z_lo(0, 0)
            dve.wait_ge(lo_ready, EV - U + 1)
            with dve.Fori(0, NK // 4 - 1) as i:
                for u in range(4):
                    weigh(i, u + 2)
                    lo_next(i, EV, u)
                    z_lo(i, u + 1)
            for u in range(4):
                if u < 2:
                    weigh(NK // 4 - 1, u + 2)
                lo_next(NK // 4 - 1, EV, u)
                if u < 3:
                    z_lo(NK // 4 - 1, u + 1)
            dve.wait_ge(used, SW)
            for k in range(KT):
                dve.scalar_tensor_tensor(x[:, k, :], ps[:, k, :], mod[:, 5 * KT + k, 0:1], x[:, k, :], ALU.mult, ALU.add).then_inc(y_done, 1)
            norm_rstd(3)
            dve.wait_ge(y_done, KT)
            for k in range(KT):
                dve.scalar_tensor_tensor(x[:, k, :], x[:, k, :], col("final1", k), rstd[:, :], ALU.mult, ALU.mult).then_inc(x_ready, 1)
            norm_rstd(4)
            norm_apply(3, x, lambda k: col("mix", k), lambda k: col("zero"), a_hi, a_lo)

            for u in range(4):
                lo_next(0, SW, u)
            for u in range(2):
                dve.wait_ge(used, SW + u + 1)
                dve.tensor_copy(k2[:, u, :], ps[:, u, :]).then_inc(bank_free, 1)
            for u in range(2):
                dve.wait_ge(used, SW + u + 3)
                dve.tensor_copy(v2_feat_sb[:, u, :], ps[:, 2 + u, :]).then_inc(v2_feat, 1)
            dve.wait_ge(v2_feat, 2)
            dve.sem_inc(bank_free, 2)
            for u in range(2):
                dve.wait_ge(v2_turned, u + 1)
                dve.tensor_copy(v2[:, :, u * P:(u + 1) * P], ps[:, 4 + u, :].rearrange("p (s n) -> p s n", n=P)).then_inc(v2_done, 1)
            with dve.Fori(0, 2) as i:
                for u in range(4):
                    step(i, SW + 4, u)
                    dve.tensor_scalar(q2[:, bass.ds(i * 4 + u, 1), :], ps[:, u, :], HD2 ** -0.5, None, ALU.mult).then_inc(bank_free, 1)

            groups = [(b, kt, half) for b in range(TT) for kt in range(2) for half in range(2)]

            def swa_bias(n):
                b, kt, half = groups[n]
                o = 32 * (n % 2)
                dve.wait_ge(sc2, n + 1)
                if n >= 2:
                    dve.wait_ge(pt2, n - 1)
                if b == 0:
                    for r in range(4):
                        h = 8 * kt + 4 * half + r
                        dve.tensor_scalar(s2[:, n % 2, r * 256:r * 256 + P], dist[:, 1, 0:P], col("slopes", h), None, ALU.mult)
                for r in range(4):
                    h = 8 * kt + 4 * half + r
                    at = P if b == 0 else 0
                    dve.scalar_tensor_tensor(s2[:, n % 2, r * 256 + at:(r + 1) * 256], dist[:, 0, at:256], col("slopes", h),
                                             ps[:, 2 * (n % 2) + r // 2, (r % 2) * 256 + at:(r % 2) * 256 + 256],
                                             ALU.mult, ALU.add).then_inc(bias2, 1)
                dve.wait_ge(bias2, 4 * (n + 1))
                dve.tensor_reduce(tiny[:, o:o + 4], s2[:, n % 2, :].rearrange("p (r n) -> p r n", r=4), AX.X, ALU.max).then_inc(mx2, 1)
                dve.wait_ge(mx2, 2 * n + 1)
                h = 8 * kt + 4 * half
                dve.tensor_tensor(tiny[:, o:o + 4], tiny[:, o:o + 4], col("sinks", h, 4), ALU.max).then_inc(mx2, 1)
                dve.wait_ge(mx2, 2 * n + 2)
                dve.tensor_scalar(tiny[:, o + 4:o + 8], tiny[:, o:o + 4], -1.0, None, ALU.mult).then_inc(nmx2, 1)

            def swa_norm(n):
                o = 32 * (n % 2)
                dve.wait_ge(e2, 4 * (n + 1))
                dve.wait_ge(snk2, 4 * (n + 1))
                dve.tensor_tensor(tiny[:, o + 16:o + 20], tiny[:, o + 8:o + 12], tiny[:, o + 12:o + 16], ALU.add).then_inc(den2, 1)
                dve.wait_ge(den2, n + 1)
                dve.reciprocal(tiny[:, o + 20:o + 24], tiny[:, o + 16:o + 20]).then_inc(rec2, 1)
                dve.wait_ge(rec2, n + 1)
                pr = s2[:, n % 2, :].rearrange("p (r n) -> p r n", r=4)
                dve.tensor_tensor(pr, pr, tiny[:, o + 20:o + 24].unsqueeze(2).to_broadcast([P, 4, 256]), ALU.mult).then_inc(pn2, 1)

            def swa_lo(n):
                b, kt, half = groups[n]
                rows_ = slice(half * HD2, (half + 1) * HD2)
                dve.wait_ge(ohi2, n + 1)
                at = slice(b * P, (b + 1) * P)
                dve.tensor_tensor(b_lo[rows_, kt * 4:kt * 4 + 4, at], ps[rows_, 6 + n % 2, :].rearrange("p (r t) -> p r t", r=4),
                                  f32(b_hi[rows_, kt * 4:kt * 4 + 4, at]), ALU.subtract).then_inc(o2, 1)

            dve.wait_ge(dist_in, 16)
            dve.wait_ge(bank_free, r_of(SO) + 4)
            swa_bias(0)
            for n in range(len(groups)):
                if n + 1 < len(groups):
                    swa_bias(n + 1)
                swa_norm(n)
                swa_lo(n)

            add_to_x(SO, KT, None, 2 * KT, step)
            norm_rstd(5)
            norm_apply(4, x, lambda k: col("ffn", k), lambda k: col("zero"), a_hi, a_lo)

            with dve.Fori(0, 2 * FT // 4) as i:
                for u in range(4):
                    step(i, GU, u)
                    if u % 2:
                        p = i * 2 + u // 2
                        dve.wait_ge(gate_ready, p + (3 * KT + 1))
                        dve.tensor_tensor(hid[:, bass.ds(p, 1), :], sq[:, u // 2, :], ps[:, u, :], ALU.mult).then_inc(act_done, 1)
                        dve.wait_ge(act_done, p + 1)
                        dve.sem_inc(bank_free, 2)

            def hid_lo(i, u):
                n = i * 4 + u
                dve.wait_ge(dhi_ready, n + 1)
                dve.tensor_tensor(b_lo[:, u % 4, :], hid[:, bass.ds(n, 1), :] if not isinstance(n, int) else hid[:, n, :],
                                  f32(b_hi[:, u % 4, :]), ALU.subtract).then_inc(dlo_ready, 1)

            hid_lo(0, 0)
            with dve.Fori(0, FT // 4) as i:
                for u in range(4):
                    hid_lo(i, u + 1)
                    lo_next(i, DN, u)
            hid_lo(FT // 4, 1)
            lo_next(FT // 4, DN, 0)
            dve.wait_ge(used, PANELS)
            for k in range(KT):
                dve.tensor_tensor(x[:, k, :], ps[:, k, :], x[:, k, :], ALU.add).then_inc(y2_done, 1)
            norm_rstd(6)
            dve.wait_ge(y2_done, KT)
            for k in range(KT):
                dve.scalar_tensor_tensor(x[:, k, :], x[:, k, :], col("final2", k), rstd[:, :], ALU.mult, ALU.mult).then_inc(out_done, 1)

        @block.gpsimd
        def _(pool):
            nc.gpsimd.memset(g_pad[:, :, 0:PAD], 0.0)
            nc.gpsimd.memset(g_pad[:, :, PAD + T:GW], 0.0).then_inc(pad_ready, 1)
            pool.wait_ge(small_in, 16)

            def lo(g, u):
                pool.wait_ge(hi_ready, g + (1 - U))
                nc.gpsimd.tensor_tensor(wlo[:, u % SPLIT, :], raw[:, u % RAW, :], f32(whi[:, u % SPLIT, :]), ALU.subtract).then_inc(lo_ready, 1)

            with pool.Fori(0, (AO - U) // 4) as i:
                for u in range(4):
                    lo(i * 4 + (U + u), u)
            lo(AO, 0)
            tmp = area(A_TMP, T)
            pool.wait_ge(pair_done, KT)
            for i in range(2):
                n = 2 * i + 5
                for j in range(TAPS):
                    if i or j:
                        pool.wait_ge(pool_tap, i * TAPS + j)
                    nc.gpsimd.tensor_tensor(tmp, g_pad[:, n, j:j + T], col("conv_w", n * TAPS + j).to_broadcast([P, T]),
                                            ALU.mult).then_inc(pool_mul, 1)
                    pool.wait_ge(pool_mul, i * TAPS + j + 1)
                    nc.gpsimd.tensor_tensor(conv[:, n, :], tmp, conv[:, n, :] if j else col("conv_b", n).to_broadcast([P, T]),
                                            ALU.add).then_inc(pool_tap, 1)
            with pool.Fori(0, (EV - AO) // 4) as i:
                for u in range(4):
                    lo(i * 4 + (AO + 1 + u), u + 1)


def kernel(**inputs):
    import numpy as np
    import concourse.bacc as _bacc
    from concourse.bass_utils import run_bass_kernel_spmd as _run

    a = {k: np.asarray(v) for k, v in inputs.items()}
    f = np.float32

    def columns(w):
        n = w.shape[1] // P
        return w.reshape(KT, P, n, P).transpose(2, 1, 0, 3).reshape(n, P, D)

    def tiles(v):
        return v.reshape(-1, P).T

    def pairs(m, n):
        return np.stack([m, n], axis=1).reshape(-1, P, D)

    w_in = columns(a["w_in"][0])
    qkv = NH + 2 * NKV
    w_q, w_k, w_v = w_in[0:NH], w_in[NH:NH + NKV], w_in[NH + NKV:qkv]
    conv_a, conv_b = w_in[qkv:qkv + KT], w_in[qkv + KT:qkv + 2 * KT]
    gate_a, gate_c = w_in[qkv + 2 * KT:qkv + 3 * KT], w_in[qkv + 3 * KT:qkv + 4 * KT]
    order = np.concatenate([np.arange(HD2) + HD2 * (8 * kt + 4 * half + r)
                            for kt in range(2) for r in range(4) for half in range(2)])
    s_in = a["swa_w_in_2"][0]
    s_q = columns(s_in[:, 0:D][:, order])
    s_kv = columns(s_in[:, D:])
    s_out = columns(a["swa_w_out_2"][0][order, :])
    gu = columns(a["ffn_w_gate_up_2"][0])
    panels = np.concatenate([
        columns(a["w_mod"][0]), pairs(conv_a, conv_b), w_k, w_v, w_q, pairs(gate_a, columns(a["w_attn_o"][0])),
        pairs(gate_c, columns(a["w_conv_o"][0])), columns(a["w_out"][0]), columns(a["peer_wq"][0]),
        a["peer_u"][0].reshape(NK, P, KT, P).transpose(0, 3, 2, 1).reshape(NK, P, D), a["peer_v"][0].reshape(NK, P, D),
        s_kv, s_q, s_out, pairs(gu[0:FT], gu[FT:]), a["ffn_w_down_2"][0].reshape(FT, P, D)])
    assert panels.shape == (PANELS, P, D)

    half, quarter = P // 2, P // 4
    pos = np.arange(T)
    inv = (np.float32(10000.0) ** (-np.arange(0, half, 2, dtype=f) / half)).astype(f)
    ang = np.concatenate([(p[:, None].astype(f) * inv).T for p in (pos // 64, pos // 64, pos % 64, pos % 64)])
    rope = np.stack([np.cos(ang), np.sin(ang)], axis=1).astype(f)
    perm = np.zeros((P, P), f)
    for d in range(P):
        first = d % half < quarter
        perm[d + quarter if first else d - quarter, d] = -1.0 if first else 1.0
    gap = (P + np.arange(P))[:, None] - np.arange(2 * P)[None, :]
    dist = np.where((gap >= 0) & (gap < P), gap, 1e30).astype(f)
    dist = np.stack([dist, np.full_like(dist, 1e30)], axis=1)
    slopes = -np.exp2(-8.0 * np.arange(1, NH2 + 1, dtype=f) / NH2).astype(f)

    wide = lambda v: np.broadcast_to(v, (P, v.shape[-1]))
    parts = {
        "b_mod": tiles(a["b_mod"][0]), "norm1": tiles(a["norm1_g"][0]), "norm2": tiles(a["norm2_g"][0]),
        "final1": tiles(a["final_norm_g"]), "conv_w": a["conv_dw"][0].T.reshape(KT, P, TAPS).transpose(1, 0, 2).reshape(P, -1),
        "conv_b": tiles(a["conv_b"][0]), "ln_g": tiles(a["conv_ln_g"][0]), "ln_b": tiles(a["conv_ln_b"][0]),
        "q_g": tiles(a["q_norm_g"][0]), "k_g": tiles(a["k_norm_g"][0]), "mix": tiles(a["norm_mix_2"][0]),
        "ffn": tiles(a["norm_ffn_2"][0]), "final2": tiles(a["final_norm_2"]),
        "c": np.stack([tiles(a["c"][0]), tiles(a["c_ctx"])], axis=2).reshape(P, -1),
        "sinks": wide(a["swa_sinks_2"][0]), "slopes": wide(slopes), "ident": np.eye(P, dtype=f),
        "ones": np.ones((P, P), f), "perm": perm, "iota": wide(np.arange(P, dtype=f)), "zero": np.zeros((P, 1), f)}
    small = np.concatenate([parts[n] for n in SMALL], axis=1)
    assert small.shape == (P, SMALL_N)
    arrays = {
        "panels": panels, "small": small,
        "xT": a["x"][0].T.reshape(KT, P, T).transpose(1, 0, 2), "ctxT": a["ctx"][0].T.reshape(KT, P, CTX).transpose(1, 0, 2),
        "rope": rope, "keys": a["peer_keys"][0].reshape(HP, NK, P).transpose(2, 0, 1), "dist": dist}
    arrays = {k: np.ascontiguousarray(v) for k, v in arrays.items()}

    nc = _bacc.Bacc("TRN2", target_bir_lowering=False, num_devices=1)
    aps = [nc.dram_tensor(k, v.shape, mybir.dt.from_np(v.dtype), kind="ExternalInput").ap() for k, v in arrays.items()]
    w_d = nc.dram_tensor("w_scratch", (NK, P, T), F32, kind="Internal").ap()
    ge_d = nc.dram_tensor("gelu_scratch", (NK, P, T), F32, kind="Internal").ap()
    out = nc.dram_tensor("out", (P, KT, T), F32, kind="ExternalOutput").ap()
    build(nc, *aps, w_d, ge_d, out)
    r = _run(nc, [arrays], core_ids=[0])
    return np.ascontiguousarray(r.results[0]["out"].transpose(2, 1, 0).reshape(1, T, D))
```

```python
from contextlib import ExitStack

import concourse.bass as bass
from concourse import mybir

F32 = mybir.dt.float32
F32R = mybir.dt.float32r
BF16 = mybir.dt.bfloat16
U32 = mybir.dt.uint32
ACT = mybir.ActivationFunctionType
ALU = mybir.AluOpType
AX = mybir.AxisListType

P = 128
D = 1024
KT = D // P
T = 512
TT = T // P
CTX = 256
S1 = T + CTX
ST = S1 // P
NH, NKV = 8, 2
TAPS = 31
PAD = TAPS // 2
GW = T + 2 * PAD
HP = 16
TOPK = 16
NK = 128
NH2, HD2 = 16, 64
FF = 2816
FT = FF // P
EPS = 1e-6

MOD_N = 6 * KT
RAW_SLOTS = 4
MOD1 = 2 * KT
MOD2A = 3 * KT
MOD_RING = RAW_SLOTS
U = MOD1
KV = U + 2 * KT
Q = KV + 4
AO = Q + NH
GC = AO + 2 * KT
CO = GC + KT
WO = CO + KT
WQ = WO + KT
EU = WQ + HP
EV = EU + NK
SW = EV + NK
SO = SW + 12
GU = SO + KT
DN = GU + 2 * FT
PANELS = DN + FT

E_SOFT = 52
E_TURN = 52
E_W = 56
RAW = RAW_SLOTS
SPLIT = 2
BANKS = 4

SMALL = {}
_at = 0
for _name, _n in (("b_mod", MOD_N), ("norm1", KT), ("norm2", KT), ("final1", KT), ("conv_w", KT * TAPS),
                  ("conv_b", KT), ("ln_g", KT), ("ln_b", KT), ("q_g", 1), ("k_g", 1), ("mix", KT), ("ffn", KT),
                  ("final2", KT), ("c", 2 * KT), ("sinks", NH2), ("slopes", NH2), ("ident", P), ("ones", P),
                  ("perm", P), ("iota", P), ("zero", 1)):
    SMALL[_name] = (_at, _n)
    _at += _n
SMALL_N = _at

ARENA = 20736
A_G = 0
A_CONV = A_G + KT * GW
A_K = A_CONV + KT * T
A_V = A_K + NKV * S1
A_Q = A_V + ST * 2 * P
A_TMP = A_Q + NH * T
A_X = A_TMP + T
A_MOD = A_CONV
A_XCTX = A_MOD + (MOD1 - MOD_RING) * D
A_COS = A_X
A_SIN = A_COS + T
A_QN = A_SIN + T
A_ROT = A_QN + 2 * T
A_VF = A_ROT + 2 * T
A_P = A_X
A_PT = A_P + TT * S1
A_M = A_X
A_MOD2 = A_K
A_FOLD = A_MOD2 + RAW_SLOTS * D
A_GATE = A_G
A_XEND = A_X + 4608
assert A_XEND <= ARENA
A_S = 0
A_STAGE = (0, 8192)
A_V1 = 8192
A_I1 = A_V1 + 64 * TOPK
A_BS = A_I1 + 64 * TOPK
A_IJ = A_BS + 32 * TOPK
A_TK = A_IJ + 64 * TOPK
A_KEYS = A_TK + 2304
A_QK = 16384
A_TI = A_QK + 2 * T
A_TJ = A_TI + T
A_GE = A_TJ + T
A_BF = A_GE + 4 * T
assert A_FOLD + 8 * P <= A_KEYS and A_KEYS + HP * P <= 16384 and A_BF + T // 2 <= ARENA
A_WR, A_GR, A_Z = 0, 4 * T, 8 * T
A_Q2 = 0
A_K2 = A_Q2 + 8 * T
A_V2 = A_K2 + 2 * T
A_DIST = A_V2 + TT * 2 * P
A_S2 = A_DIST + 2 * 256
A_PT2 = A_S2 + 3 * 1024
A_FF = 0


def build(nc, panels, mod2_d, small, xT_d, ctxT_d, rope_d, keys_d, dist_d, w_d, ge_d, out):
    with ExitStack() as ctx:
        def sb(name, shape, dt=F32):
            return ctx.enter_context(nc.sbuf_tensor(name, shape, dt))

        def sem(name):
            return ctx.enter_context(nc.semaphore(name))

        x = sb("x", [P, KT, T])
        raw = sb("raw", [P, RAW, D])
        whi = sb("whi", [P, SPLIT, D], F32R)
        wlo = sb("wlo", [P, SPLIT, D], F32R)
        a_hi = sb("a_hi", [P, KT, T], F32R)
        a_lo = sb("a_lo", [P, KT, T], F32R)
        b_hi = sb("b_hi", [P, KT, T], F32R)
        b_lo = sb("b_lo", [P, KT, T], F32R)
        sm = sb("sm", [P, SMALL_N])
        mod = sb("mod", [P, MOD_N, 2])
        gs1 = sb("gs1", [P, KT])
        gs1c = sb("gs1c", [P, KT])
        gs2 = sb("gs2", [P, KT])
        c_act = sb("c_act", [P, KT, 2])
        iota_b = sb("iota_b", [P, P], BF16)
        tiny = sb("tiny", [P, 64])
        sq = sb("sq", [P, 2, T])
        rstd = sb("rstd", [P, T])
        nt = sb("nt", [P, 2, T])
        ar = sb("ar", [P, ARENA])
        ps = ctx.enter_context(nc.psum_tensor("ps", [P, 8, T], F32))

        def area(at, *dims):
            n = 1
            for d in dims:
                n *= d
            v = ar[:, at:at + n]
            if len(dims) == 2:
                v = v.rearrange("p (a b) -> p a b", a=dims[0])
            elif len(dims) == 3:
                v = v.rearrange("p (a b c) -> p a b c", a=dims[0], b=dims[1])
            return v

        def col(name, i=0, n=1):
            at = SMALL[name][0] + i
            return sm[:, at:at + n]

        ident, ones, perm = col("ident", 0, P), col("ones", 0, P), col("perm", 0, P)
        f32 = lambda ap: ap.bitcast(F32)

        def sems(names):
            return [sem(n) for n in names.split()]

        landed = [sem(f"landed{i}") for i in range(RAW)]
        hi_ready = sem("hi_ready")
        lo_ready = sem("lo_ready")
        used = sem("used")
        bank_done = sem("bank_done")
        bank_free = sem("bank_free")
        small_in, x_in, ctx_in, rope_in, keys_in, dist_in, out_written = sems(
            "small_in x_in ctx_in rope_in keys_in dist_in out_written")
        mod_in = [sem(f"mod_in{i}") for i in range(3)]
        mod2_in = [sem(f"mod2_in{i}") for i in range(4)]
        c_ready, folds, folds2, summed2, mod_done = sems("c_ready folds folds2 summed2 mod_done")
        sq_ready, sq_used, rt_ready, rstd_ready, nt_ready, nhi_ready, h_ready = sems(
            "sq_ready sq_used rt_ready rstd_ready nt_ready nhi_ready h_ready")
        x_ready = sem("x_ready")
        gate_ready, pair_done, co_mul = sems("gate_ready pair_done co_mul")
        pad_ready, tap_done, tap5_done, tap6_done, pool_mul, pool_tap = sems(
            "pad_ready tap_done tap5_done tap6_done pool_mul pool_tap")
        ksq, kstat, krt, krstd, kn, krot, kcos, ksin, k_done = sems("ksq kstat krt krstd kn krot kcos ksin k_done")
        v_feat_ready, v_turned, v_done = sems("v_feat_ready v_turned v_done")
        qs_ready, sc_ready, top_ready, mx_ready, p_ready, rs_ready, pn_ready, pt_ready, pt_done, pv_ready, ohi_ready, o_ready = sems(
            "qs_ready sc_ready top_ready mx_ready p_ready rs_ready pn_ready pt_ready pt_done pv_ready ohi_ready o_ready")
        cv_sum, cv_mu, cv_xc, cv_sq, cv_used, cv_rt, cv_rstd, cv_t, cv_act, cv_hi, cv_ready = sems(
            "cv_sum cv_mu cv_xc cv_sq cv_used cv_rt cv_rstd cv_t cv_act cv_hi cv_ready")
        mhi_ready, m_ready = sems("mhi_ready m_ready")
        qk_ready, s_ready, s_done, lv1, lv2, soft_d, soft_e, soft, ijw_t, ijw = sems(
            "qk_ready s_ready s_done lv1 lv2 soft_d soft_e soft ijw_t ijw")
        hot_ready, w_staged, w_ready = sems("hot_ready w_staged w_ready")
        w_out = [sem(f"w_out{i}") for i in range(2)]
        ge_out = [sem(f"ge_out{i}") for i in range(4)]
        wg_in = [sem(f"wg_in{i}") for i in range(4)]
        z_ready, zhi_ready, zlo_ready, y_done, y1_ready = sems("z_ready zhi_ready zlo_ready y_done y1_ready")
        v2_feat, v2_turned, v2_done = sems("v2_feat v2_turned v2_done")
        sc2, bias2, mx2, nmx2, e2, snk2, den2, rec2, pn2, pt2, ptc2, pv2, ohi2, o2 = sems(
            "sc2 bias2 mx2 nmx2 e2 snk2 den2 rec2 pn2 pt2 ptc2 pv2 ohi2 o2")
        act_done, dhi_ready, dlo_ready, y2_done, out_done = sems("act_done dhi_ready dlo_ready y2_done out_done")

        g_pad = area(A_G, KT, GW)
        conv = area(A_CONV, KT, T)
        kT = area(A_K, NKV, S1)
        v_tok = area(A_V, ST, 2 * P)
        qT = area(A_Q, NH, T)
        v_feat = area(A_VF, NKV, S1)
        q_slot = nt
        x_ctx = area(A_XCTX, KT, CTX)
        rstd_c = area(A_XCTX + KT * CTX, CTX)
        mod_panels = area(A_MOD, MOD1 - MOD_RING, D)
        fold1 = nt[:, :, :].rearrange("p a b -> p (a b)").rearrange("p (s c n) -> p s c n", s=4, c=2)
        mod2_ring = area(A_MOD2, RAW, D)
        fold2 = area(A_FOLD, 8, P)
        gate_c = area(A_GATE, KT, T)
        cos, sin = area(A_COS, T), area(A_SIN, T)
        q_n = area(A_QN, 2, T)
        q_rot = area(A_ROT, 2, T)
        prob = area(A_P, TT, S1)
        probT = area(A_PT, 2, ST, P)
        merged = area(A_M, KT, T)
        scores = area(A_S, 64, NK)
        stage = [area(a, P, 64) for a in A_STAGE]
        v1, i1 = area(A_V1, 64, TOPK), area(A_I1, 64, TOPK)
        best = area(A_BS, 32, TOPK)
        ij = area(A_IJ, 2, 32 * TOPK)
        keys = area(A_KEYS, HP, P)
        q_key = area(A_QK, 2, T)
        tok_i, tok_j = area(A_TI, T), area(A_TJ, T)
        ge_slot = area(A_GE, 4, T)
        w_ring, ge_ring, z = area(A_WR, 4, T), area(A_GR, 4, T), area(A_Z, 2, T)
        hot = [v[:, :, :].rearrange("p a b -> p (a b)").bitcast(BF16).rearrange("p (t k n) -> p t k n", t=4, k=4)
               for v in (sq, nt)]
        tok_w = [q_key[:, 0, :], q_key[:, 1, :], rstd[:, :]]
        w_bf = area(A_BF, T // 2).bitcast(BF16)
        q2 = area(A_Q2, 8, T)
        k2 = area(A_K2, 2, T)
        v2 = area(A_V2, TT, 2 * P)
        v2_feat_sb = area(A_S2, 2, T)
        dist = area(A_DIST, 2, 256)
        s2 = area(A_S2, 3, 1024)
        p2T = area(A_PT2, 2, 512)
        hid = area(A_FF, FT, T)

        def r_of(g):
            return g - U if g < EV else g - U - NK

        ROUNDS = 1 + (MOD_RING - MOD1) // RAW

        block = ctx.enter_context(nc.Block())

        @block.sync
        def _(sp):
            sp.dma_start(sm[:, :], small).then_inc(small_in, 16)

            def load(g, u):
                sp.dma_start(raw[:, u, :], panels[g]).then_inc(landed[u], 16)

            def load_dyn(i, g0, u):
                sp.wait_ge(lo_ready, i * 4 + (g0 + u - RAW + 1 - U))
                send(i, g0, u)

            def send(i, g0, u):
                sp.dma_start(raw[:, (g0 + u) % RAW, :],
                             panels[bass.ds(i * 4 + (g0 + u), 1)].rearrange("a p n -> (a p) n")).then_inc(landed[(g0 + u) % RAW], 16)

            for u in range(RAW):
                load(u, u)

            def load_mod(h):
                at = slice(MOD_RING + h * RAW, MOD_RING + (h + 1) * RAW)
                sp.dma_start(mod_panels[:, h * RAW:(h + 1) * RAW, :], panels[at].rearrange("a p n -> p a n")).then_inc(mod_in[h], 16)

            load_mod(0)
            load_mod(1)
            sp.dma_start(x[:, :, :], xT_d).then_inc(x_in, 16)
            load_mod(2)
            sp.dma_start(x_ctx, ctxT_d).then_inc(ctx_in, 16)
            for u in range(RAW):
                sp.wait_ge(used, u + 1)
                load(U + u, u)
            with sp.Fori(0, (KV - U - RAW) // 4) as i:
                for u in range(4):
                    load_dyn(i, U + RAW, u)
            for u in range(RAW):
                load_dyn(0, KV, u)
            sp.wait_ge(h_ready, 2 * KT)
            sp.dma_start(area(A_COS, 2, T), rope_d).then_inc(rope_in, 16)
            with sp.Fori(1, (GC + RAW - KV) // 4) as i:
                for u in range(4):
                    load_dyn(i, KV, u)

            def load_mod2(n, slot):
                sp.dma_start(mod2_ring[:, slot, :], mod2_d[bass.ds(n, 1)].rearrange("a p n -> (a p) n")).then_inc(mod2_in[slot], 16)

            sp.wait_ge(o_ready, NH + 2)
            for n in range(4):
                load_mod2(n, n)

            def next_mod2(pair):
                sp.wait_ge(folds2, (pair + 1) * 2 * KT)
                for n in (2 * pair + 4, 2 * pair + 5):
                    load_mod2(n, n % 4)

            behind = {1: 0, 2: 1, 3: 2, 7: 3, 8: 4, 9: 5, 10: 6, 11: 7, 12: 8, 13: 9, 14: 10, 15: 11}
            for n in range(2 * KT):
                load_dyn(0, GC + RAW + n, 0)
                if n in behind:
                    next_mod2(behind[n])
            with sp.Fori(0, (WQ - WO - RAW) // 4) as i:
                for u in range(4):
                    load_dyn(i, WO + RAW, u)
            for u in range(4):
                load_dyn(0, WQ, u)
            sp.wait_ge(h_ready, 3 * KT)
            sp.dma_start(keys, keys_d).then_inc(keys_in, 16)
            for pair in (12, 13):
                next_mod2(pair)
            with sp.Fori(1, (EV - WQ) // 4) as i:
                for u in range(4):
                    load_dyn(i, WQ, u)

            def load_wg(i, u):
                sp.dma_start(w_ring[:, u, :], w_d[bass.ds(i * 4 + u, 1)].rearrange("a p n -> (a p) n")).then_inc(wg_in[u], 16)
                sp.dma_start(ge_ring[:, u, :], ge_d[bass.ds(i * 4 + u, 1)].rearrange("a p n -> (a p) n")).then_inc(wg_in[u], 16)

            for done in w_out:
                sp.wait_ge(done, 16 * 4)
            for u in range(4):
                sp.wait_ge(ge_out[u], 16)
                load_wg(0, u)
            for u in range(4):
                load_dyn(0, EV, u)
            for done in ge_out:
                sp.wait_ge(done, 16 * (NK // 4))
            with sp.Fori(1, NK // 4) as i:
                for u in range(4):
                    load_dyn(i, EV, u)
                    sp.wait_ge(z_ready, i * 4 + (u - 4 + 1))
                    load_wg(i, u)
            sp.wait_ge(z_ready, NK)
            sp.dma_start(area(A_DIST, 2, 256), dist_d).then_inc(dist_in, 16)
            with sp.Fori(0, (PANELS - SW) // 4) as i:
                for u in range(4):
                    load_dyn(i, SW, u)
            for u in range((PANELS - SW) % 4):
                load_dyn(0, PANELS - 2, u)
            for k in range(KT):
                sp.wait_ge(out_done, k + 1)
                sp.dma_start(out[:, k, :], x[:, k, :]).then_inc(out_written, 16)
            sp.wait_ge(out_written, 16 * KT)

        @block.tensor
        def _(pe):
            def panel(g, u, bank, hi, lo, free, ready=None):
                pe.wait_ge(lo_ready, g + (1 - U))
                pe.wait_ge(bank_free, free)
                for k in range(KT):
                    if ready:
                        pe.wait_ge(ready[0], ready[1] + k + 1)
                    w_h = whi[:, u % SPLIT, k * P:(k + 1) * P]
                    w_l = wlo[:, u % SPLIT, k * P:(k + 1) * P]
                    pe.matmul(bank, w_h, hi[:, k, :], start=(k == 0), stop=False)
                    pe.matmul(bank, w_h, lo[:, k, :], start=False, stop=False)
                    last = pe.matmul(bank, w_l, hi[:, k, :], start=False, stop=(k == KT - 1))
                last.then_inc(used, 1)

            def strips(first, count, hi, lo, after=None, ready=None):
                def four(i, ready=None):
                    for u in range(4):
                        panel(i * 4 + (first + u), u, ps[:, u, :], hi, lo, i * 4 + (r_of(first) + u + 1), ready if u == 0 else None)
                        if after:
                            after(i, u)
                    if after:
                        after(i, 4)
                four(0, ready)
                if count > 4:
                    with pe.Fori(1, count // 4) as i:
                        four(i)

            def norm_stat(n, k, src_width=T):
                pe.wait_ge(sq_ready, n * KT + k + 1)
                pe.matmul(ps[:, 4, 0:src_width], ones, sq[:, k % 2, 0:src_width], start=(k == 0),
                          stop=(k == KT - 1)).then_inc(sq_used, 1)

            def norm_stats(n, src_width=T):
                for k in range(KT):
                    norm_stat(n, k, src_width)

            def stats_after(n):
                def after(i, u):
                    if u < 4 and i * 4 + u:
                        norm_stat(n, i * 4 + u - 1)
                return after

            def mod_panel(n, src):
                for k in range(KT):
                    last = pe.matmul(ps[:, 7, 2 * n:2 * n + 2], src[:, k * P:(k + 1) * P], c_act[:, k, :],
                                     start=(k == 0), stop=(k == KT - 1))
                last.then_inc(used, 1)

            def mod_sums(h):
                for n in range(MOD_RING + h * RAW, MOD_RING + (h + 1) * RAW):
                    pe.wait_ge(folds, (n - MOD_RING + 1) * 2 * KT)
                    for c in range(2):
                        last = pe.matmul(ps[:, 7, 2 * n + c:2 * n + c + 1], fold1[:, n % 4, c, :], ones[:, 0:1], start=True, stop=True)
                    last.then_inc(used, 1)

            pe.wait_ge(c_ready, 1)
            for n in range(MOD_RING):
                pe.wait_ge(landed[n], 16)
                mod_panel(n, raw[:, n, :])
            mod_sums(0)
            norm_stats(0)
            pe.wait_ge(mod_in[2], 16)
            for n in range(MOD_RING + 2 * RAW, MOD1):
                mod_panel(n, mod_panels[:, n - MOD_RING, :])
            mod_sums(1)
            pe.wait_ge(rt_ready, 1)
            norm_stats(1, CTX)

            strips(U, 2 * KT, a_hi, a_lo, ready=(h_ready, 0))

            def split3(bank, wu, k, hi, lo, first, last):
                w_h = whi[:, wu % SPLIT, k * P:(k + 1) * P]
                w_l = wlo[:, wu % SPLIT, k * P:(k + 1) * P]
                pe.matmul(bank, w_h, hi, start=first, stop=False)
                pe.matmul(bank, w_h, lo, start=False, stop=False)
                return pe.matmul(bank, w_l, hi, start=False, stop=last)

            def head_stats(n, slot, width=T):
                pe.wait_ge(ksq, n + 1)
                if not isinstance(n, int) or n:
                    pe.wait_ge(krt, n)
                pe.matmul(ps[:, 4, 0:width], ones, sq[:, slot, 0:width], start=True, stop=True).then_inc(kstat, 1)

            def head_rot(m, slot, normed):
                pe.wait_ge(kn, normed)
                if not isinstance(m, int) or m:
                    pe.wait_ge(ksin, m)
                pe.matmul(ps[:, 5, :], perm, q_n[:, slot, :], start=True, stop=True).then_inc(krot, 1)

            def kv_panel(u):
                g = KV + u
                pe.wait_ge(lo_ready, g + (1 - U))
                pe.wait_ge(bank_free, r_of(g) + 1)
                for k in range(KT):
                    split3(ps[:, u, :], u, k, a_hi[:, k, :], a_lo[:, k, :], k == 0, k == KT - 1)
                for k in range(KT):
                    if u == 0:
                        pe.wait_ge(h_ready, KT + k + 1)
                    last = split3(ps[:, 6 + u // 2, u % 2 * CTX:(u % 2 + 1) * CTX], u, k, b_hi[:, k, 0:CTX], b_lo[:, k, 0:CTX], k == 0, k == KT - 1)
                last.then_inc(used, 1)

            def turn_values(u):
                if u == 0:
                    pe.wait_ge(kn, 4)
                    pe.wait_ge(v_feat_ready, 4)
                else:
                    pe.wait_ge(v_done, 1)
                for s in range(ST):
                    last = pe.transpose(ps[:, 6 + s // 3, (s % 3) * P:(s % 3 + 1) * P],
                                        v_feat[:, u, s * P:(s + 1) * P], ident)
                last.then_inc(v_turned, 1)

            kv_panel(0)
            kv_panel(1)
            head_stats(0, 0)
            kv_panel(2)
            head_rot(0, 0, 1)
            head_stats(1, 1, CTX)
            kv_panel(3)
            head_stats(2, 0)

            def q_after(i, u):
                h = i * 4 + u
                if u == 4:
                    return
                if not isinstance(h, int) or h:
                    head_rot(h, u % 2, h + 3)
                if isinstance(h, int) and h == 0:
                    head_stats(3, 1, CTX)
                else:
                    head_stats(h + 3, (u + 1) % 2)
                if isinstance(h, int) and 2 <= h < 4:
                    turn_values(h - 2)

            strips(Q, NH, a_hi, a_lo, q_after)
            head_rot(NH, 0, NH + 3)
            head_stats(NH + 3, 1)
            head_rot(NH + 1, 1, NH + 4)

            pe.wait_ge(v_done, NKV)
            pe.wait_ge(bank_free, r_of(AO) + 4)

            def att_scores(i, s):
                hu, t = s // TT % 2, s % TT
                b = 2 * (t % 2)
                if t == 0:
                    pe.wait_ge(qs_ready, i * 2 + (s // TT + 1))
                pe.matmul(ps[:, b, :], q_slot[:, hu, t * P:(t + 1) * P], kT[:, hu, 0:T], start=True, stop=True)
                pe.matmul(ps[:, b + 1, 0:CTX], q_slot[:, hu, t * P:(t + 1) * P], kT[:, hu, T:S1], start=True,
                          stop=True).then_inc(sc_ready, 1)

            def att_step(i, s, ahead=True):
                n = i * (2 * TT) + s
                hu, t = s // TT, s % TT
                pe.wait_ge(pn_ready, n + 1)
                for j in range(ST):
                    last = pe.transpose(ps[:, 4 + j // 3, (j % 3) * P:(j % 3 + 1) * P], prob[:, t, j * P:(j + 1) * P], ident)
                last.then_inc(pt_ready, 1)
                if ahead:
                    pe.wait_ge(p_ready, n + 2)
                    att_scores(i, s + 3)
                pe.wait_ge(pt_done, n + 1)
                if t == 0:
                    pe.wait_ge(o_ready, i * 2 + (hu + 1))
                for j in range(ST):
                    last = pe.matmul(ps[:, 6 + hu, t * P:(t + 1) * P], v_tok[:, j, hu * P:(hu + 1) * P], probT[:, t % 2, j, :],
                                     start=(j == 0), stop=(j == ST - 1))
                last.then_inc(pv_ready, 1)

            att_scores(0, 0)
            att_scores(0, 1)
            pe.wait_ge(p_ready, 1)
            att_scores(0, 2)
            for s in range(2 * TT):
                att_step(0, s)
            with pe.Fori(1, NH // 2 - 1) as i:
                for s in range(2 * TT):
                    att_step(i, s)
            for s in range(2 * TT):
                att_step(NH // 2 - 1, s, s + 3 < 2 * TT)

            pe.wait_ge(o_ready, NH + 2)
            with pe.Fori(0, 2 * KT // 4) as i:
                for u in range(4):
                    hi, lo = (a_hi, a_lo) if u % 2 == 0 else (b_hi, b_lo)
                    panel(i * 4 + (AO + u), u, ps[:, u, :], hi, lo, i * 4 + (r_of(AO) + u + 1))

            def gate_panel(k):
                panel(GC + k, k % 4, ps[:, k % 4, :], a_hi, a_lo, r_of(GC) + k + 1)

            gate_panel(0)
            pe.wait_ge(tap_done, 5 * TAPS)
            pe.wait_ge(tap5_done, TAPS)
            pe.wait_ge(tap6_done, TAPS)
            pe.wait_ge(pool_tap, TAPS)
            for k in range(KT):
                last = pe.matmul(ps[:, 4, :], ones, conv[:, k, :], start=(k == 0), stop=(k == KT - 1))
            last.then_inc(cv_sum, 1)
            gate_panel(1)
            gate_panel(2)
            for k in range(KT):
                pe.wait_ge(cv_sq, k + 1)
                pe.matmul(ps[:, 5, :], ones, sq[:, k % 2, :], start=(k == 0), stop=(k == KT - 1)).then_inc(cv_used, 1)
            for k in range(3, KT):
                gate_panel(k)

            def mod2_sums(pair, bank):
                pe.wait_ge(folds2, (pair + 1) * 2 * KT)
                for n in (2 * pair, 2 * pair + 1):
                    pe.matmul(ps[:, bank, n:n + 1], fold2[:, n % 8, :], ones[:, 0:1], start=True, stop=True).then_inc(summed2, 1)

            for k in range(KT):
                panel(CO + k, k % 4, ps[:, k % 4, :], b_hi, b_lo, r_of(CO) + k + 1, (cv_ready, 0) if k == 0 else None)
                for pair in ((k,) if k < 4 else (2 * k - 4, 2 * k - 3)):
                    mod2_sums(pair, 6)
            strips(WO, KT, a_hi, a_lo, stats_after(2), (m_ready, 0))
            norm_stat(2, KT - 1)
            def key_scores(i, u):
                for v in ((u - 1,) if 0 < u < 4 else (3,) if u == 4 else ()):
                    if isinstance(i, int) and i == v == 0:
                        pe.wait_ge(keys_in, 16)
                    pe.wait_ge(qk_ready, i * 4 + (v + 1))
                    if not isinstance(i, int) or i:
                        pe.wait_ge(s_done, i * 4 + (v - 3))
                    for t in range(TT):
                        last = pe.matmul(ps[:, 4 + v, t * P:(t + 1) * P], q_key[:, v % 2, t * P:(t + 1) * P],
                                         keys[:, bass.ds(i * 4 + v, 1), :], start=True, stop=True)
                    last.then_inc(s_ready, 1)

            strips(WQ, HP, b_hi, b_lo, key_scores, (h_ready, 2 * KT))
            pe.wait_ge(s_done, HP - 3)
            for pair in range(MOD2A // 2, (MOD_N - MOD1) // 2):
                mod2_sums(pair, 4)

            strips(EU, E_TURN, b_hi, b_lo)

            pe.wait_ge(soft, 1)
            for a in range(3):
                src = ij[:, a, :] if a < 2 else best.rearrange("p a b -> p (a b)")
                for t in range(TT):
                    last = pe.transpose(ps[:, 4 + a, t * P:(t + 1) * P], src[:, t * P:(t + 1) * P], ident)
            last.then_inc(ijw_t, 1)

            strips(EU + E_TURN, E_W - E_TURN, b_hi, b_lo)

            def token_w(i, u):
                if u == 4:
                    return
                for v in range(2):
                    n = i * 8 + (2 * u + v)
                    pe.wait_ge(hot_ready, n + 1)
                    if not isinstance(n, int) or n >= 4:
                        pe.wait_ge(w_ready, n - 3)
                    bank = 4 + (2 * u + v) % 4
                    for t in range(4):
                        for c in range(1, 4):
                            last = pe.matmul(ps[:, bank, t * P:(t + 1) * P], hot[v][:, t, 0, :], hot[v][:, t, c, :],
                                             start=(c == 1), stop=(c == 3))
                    last.then_inc(w_staged, 1)

            strips(EU + E_W, T // 8, b_hi, b_lo, token_w)
            strips(EU + E_W + T // 8, NK - E_W - T // 8, b_hi, b_lo)

            pe.wait_ge(bank_free, r_of(EU) + NK + 4)
            pe.wait_ge(w_ready, P)

            def rows(g, u, n, split, hi, lo, first=False, last=False):
                pe.wait_ge(lo_ready, g + (1 - U))
                pe.wait_ge(split, n + 1)
                for d in range(KT):
                    w_h = whi[:, u % SPLIT, d * P:(d + 1) * P]
                    w_l = wlo[:, u % SPLIT, d * P:(d + 1) * P]
                    pe.matmul(ps[:, d, :], w_h, hi[:, u, :], start=first, stop=False)
                    pe.matmul(ps[:, d, :], w_h, lo[:, u, :], start=False, stop=False)
                    end = pe.matmul(ps[:, d, :], w_l, hi[:, u, :], start=False, stop=last)
                    if d == KT - 1:
                        end.then_inc(used, 1)
                    elif last:
                        end.then_inc(bank_done, 1)

            for u in range(4):
                rows(EV + u, u, u, zlo_ready, a_hi, a_lo, u == 0)
            with pe.Fori(1, NK // 4 - 1) as i:
                for u in range(4):
                    rows(i * 4 + (EV + u), u, i * 4 + u, zlo_ready, a_hi, a_lo)
            for u in range(4):
                n = NK - 4 + u
                rows(EV + n, u, n, zlo_ready, a_hi, a_lo, last=n == NK - 1)

            pe.wait_ge(y_done, 5)
            norm_stats(3)
            norm_stats(4)

            for u in range(4):
                panel(SW + u, u, ps[:, u, :], a_hi, a_lo, r_of(SW) + u + 1, (h_ready, 3 * KT) if u == 0 else None)
            for u in range(2):
                pe.wait_ge(v2_feat, u + 1)
                for s in range(TT):
                    last = pe.transpose(ps[:, 4 + u, s * P:(s + 1) * P], v2_feat_sb[:, u, s * P:(s + 1) * P], ident)
                last.then_inc(v2_turned, 1)
            strips(SW + 4, 8, a_hi, a_lo)

            pe.wait_ge(bank_free, r_of(SO) + 4)
            pe.wait_ge(v2_done, 2)
            groups = [(b, kt, half) for b in range(TT) for kt in range(2) for half in range(2)]

            def swa_scores(n):
                b, kt, half = groups[n]
                rows_ = slice(half * HD2, (half + 1) * HD2)
                if n >= 2:
                    pe.wait_ge(bias2, 4 * (n - 1))
                for r in range(4):
                    dst = ps[:, 2 * (n % 2) + r // 2, (r % 2) * 256 + (P if b == 0 else 0):(r % 2) * 256 + 256]
                    last = pe.matmul(dst, q2[rows_, kt * 4 + r, b * P:(b + 1) * P],
                                     k2[rows_, kt, max(b - 1, 0) * P:(b + 1) * P], start=True, stop=True)
                last.then_inc(sc2, 1)

            def swa_turn(n):
                b, kt, half = groups[n]
                tiles = (1,) if b == 0 else (0, 1)
                pe.wait_ge(pn2, n + 1)
                if n:
                    pe.wait_ge(ptc2, n)
                for s in tiles:
                    for r in range(4):
                        last = pe.transpose(ps[:, 4 + s, r * P:(r + 1) * P], s2[:, n % 3, r * 256 + s * P:r * 256 + (s + 1) * P], ident)
                last.then_inc(pt2, 1)

            def swa_values(n):
                b, kt, half = groups[n]
                tiles = (1,) if b == 0 else (0, 1)
                pe.wait_ge(ptc2, n + 1)
                if n >= 2:
                    pe.wait_ge(o2, n - 1)
                rows_ = slice(half * HD2, (half + 1) * HD2)
                kv = 2 * kt + half
                for s in tiles:
                    last = pe.matmul(ps[rows_, 6 + n % 2, :], v2[:, b - 1 + s, kv * HD2:(kv + 1) * HD2], p2T[:, s, :],
                                     start=(s == tiles[0]), stop=(s == 1))
                last.then_inc(pv2, 1)

            for n in range(3):
                swa_scores(n)
            for n in range(len(groups)):
                swa_turn(n)
                if n + 3 < len(groups):
                    swa_scores(n + 3)
                swa_values(n)

            pe.wait_ge(o2, len(groups))
            strips(SO, KT, b_hi, b_lo, stats_after(5))
            norm_stat(5, KT - 1)
            strips(GU, 2 * FT, a_hi, a_lo, ready=(h_ready, 4 * KT))
            pe.wait_ge(bank_free, r_of(DN) + 4)
            for u in range(4):
                rows(DN + u, u, u, dlo_ready, b_hi, b_lo, u == 0)
            with pe.Fori(1, FT // 4) as i:
                for u in range(4):
                    rows(i * 4 + (DN + u), u, i * 4 + u, dlo_ready, b_hi, b_lo)
            for u in range(FT % 4):
                n = FT - FT % 4 + u
                rows(DN + n, u, n, dlo_ready, b_hi, b_lo, last=n == FT - 1)
            pe.wait_ge(y2_done, 5)
            norm_stats(6)

        @block.scalar
        def _(act):
            def hi(g, u, i=None):
                act.wait_ge(landed[u % RAW], (g // 4 + ROUNDS) * 16 if i is None else i)
                act.wait_ge(used, g - SPLIT + 1)
                act.activation(whi[:, u % SPLIT, :], raw[:, u % RAW, :], ACT.Copy).then_inc(hi_ready, 1)

            def hi_next(i, first, u):
                hi(i * 4 + (first + u + 1), first + u + 1, (i + ((first + u + 1) // 4 + ROUNDS)) * 16)

            def step(i, first, u):
                hi_next(i, first, u)
                act.wait_ge(used, i * 4 + (first + u + 1))

            def norm_sq_tile(n, k, src, width=T):
                if n or k >= 2:
                    act.wait_ge(sq_used, n * KT + k - 1)
                act.activation(sq[:, k % 2, 0:width], src[:, k, 0:width], ACT.Square).then_inc(sq_ready, 1)

            def norm_sq(n, src, width=T, rt=rstd[:, :], tiles=range(KT), made=None):
                for k in tiles:
                    if made:
                        act.wait_ge(made, k + 1)
                    norm_sq_tile(n, k, src, width)
                act.wait_ge(sq_used, (n + 1) * KT)
                act.activation(rt, ps[:, 4, 0:width], ACT.Sqrt, bias=EPS, scale=1.0 / D).then_inc(rt_ready, 1)

            def norm_hi(n, dst, shift, width=T):
                for k in range(KT):
                    act.wait_ge(nt_ready, n * KT + k + 1)
                    act.activation(dst[:, k, 0:width], nt[:, k % 2, 0:width], ACT.Identity, bias=shift(k)).then_inc(nhi_ready, 1)

            act.wait_ge(small_in, 16)
            c_in = col("c", 0, 2 * KT).rearrange("p (a b) -> p a b", b=2)
            act.activation(c_act[:, :, :], c_in, ACT.Silu).then_inc(c_ready, 1)
            act.wait_ge(x_in, 16)
            norm_sq(0, x)
            act.wait_ge(ctx_in, 16)
            norm_sq(1, x_ctx, CTX, rstd_c)
            hi(U, 0)
            norm_hi(0, a_hi, lambda k: mod[:, k, 0:1])
            def gates(first, count, bank_of):
                with act.Fori(0, count // 4) as i:
                    for u in range(4):
                        step(i, first, u)
                        if u % 2:
                            act.activation(sq[:, u // 2, :], ps[:, bank_of(u), :], ACT.Sigmoid).then_inc(gate_ready, 1)

            gates(U, 2 * KT, lambda u: u)
            norm_hi(1, b_hi, lambda k: mod[:, k, 1:2], CTX)

            def head_sq(n, slot, src, width=T):
                act.activation(sq[:, slot, 0:width], src, ACT.Square).then_inc(ksq, 1)

            def head_rt(n, width=T):
                act.wait_ge(kstat, n + 1)
                if not isinstance(n, int) or n:
                    act.wait_ge(kn, n)
                act.activation(rstd[:, 0:width], ps[:, 4, 0:width], ACT.Sqrt, bias=EPS, scale=1.0 / P).then_inc(krt, 1)

            hi_next(0, KV, 0)
            hi_next(0, KV, 1)
            act.wait_ge(pair_done, KT)
            act.wait_ge(used, KV + 1)
            head_sq(0, 0, ps[:, 0, :])
            hi_next(0, KV, 2)
            act.wait_ge(used, KV + 2)
            head_sq(1, 1, ps[:, 6, 0:CTX], CTX)
            head_rt(0)
            head_sq(2, 0, ps[:, 1, :])
            hi_next(0, KV, 3)
            head_rt(1, CTX)
            act.wait_ge(kn, 2)
            head_sq(3, 1, ps[:, 6, CTX:2 * CTX], CTX)
            head_rt(2)
            def q_step(i, u):
                step(i, Q, u)
                head_sq(None, u % 2, ps[:, u, :])
                head_rt(i * 4 + (u + 3), CTX if isinstance(i, int) and i * 4 + u == 0 else T)

            for u in range(4):
                q_step(0, u)
            with act.Fori(1, NH // 4) as i:
                for u in range(4):
                    q_step(i, u)
            head_rt(NH + 3)

            def att_exp(i, s):
                t = s % TT
                act.wait_ge(mx_ready, i * (2 * TT) + (s + 1))
                act.activation(prob[:, t, :], ps[:, 2 * (t % 2):2 * (t % 2) + 2, :].rearrange("p a b -> p (a b)")[:, 0:S1],
                               ACT.Exp, bias=tiny[:, t:t + 1], scale=P ** -0.5, accum_out=tiny[:, 8 + t:9 + t]).then_inc(p_ready, 1)

            def att_out(m, h, hu):
                act.wait_ge(pv_ready, (m + 1) * TT)
                act.activation(b_hi[:, bass.ds(h, 1), :] if not isinstance(h, int) else b_hi[:, h, :], ps[:, 6 + hu, :],
                               ACT.Copy).then_inc(ohi_ready, 1)

            def att_step(i, s, ahead=True):
                n = i * (2 * TT) + s
                hu, t = s // TT, s % TT
                if ahead:
                    att_exp(i, s + 1)
                act.wait_ge(pt_ready, n + 1)
                if not isinstance(n, int) or n >= 2:
                    act.wait_ge(pv_ready, n - 1)
                act.activation(probT[:, t % 2, :, :].rearrange("p (a s) n -> p a s n", a=2),
                               ps[:, 4:6, 0:3 * P].rearrange("p a (s n) -> p a s n", n=P), ACT.Copy).then_inc(pt_done, 1)
                if t == 0 and hu:
                    att_out(i * 2, i, 0)
                elif t == 0 and (not isinstance(i, int) or i):
                    att_out(i * 2 - 1, i + (NH // 2 - 1), 1)

            att_exp(0, 0)
            for s in range(2 * TT):
                att_step(0, s)
            with act.Fori(1, NH // 2 - 1) as i:
                for s in range(2 * TT):
                    att_step(i, s)
            for s in range(2 * TT):
                att_step(NH // 2 - 1, s, s + 1 < 2 * TT)
            att_out(NH - 1, NH - 1, 1)

            gates(AO, 2 * KT, lambda u: u - 1)

            def gate_step(k, panel_=True, gate=True):
                if panel_:
                    hi_next(k // 4, GC, k % 4)
                if gate:
                    act.wait_ge(used, GC + k + 1)
                    act.wait_ge(cv_sum, 1)
                    act.activation(gate_c[:, k, :], ps[:, k % 4, :], ACT.Sigmoid).then_inc(bank_free, 1)

            def conv_act(k):
                act.wait_ge(cv_t, k + 1)
                if k >= 2:
                    act.wait_ge(cv_ready, k - 1)
                act.activation(sq[:, k % 2, :], nt[:, k % 2, :], ACT.Silu, bias=col("ln_b", k), scale=col("ln_g", k)).then_inc(cv_act, 1)
                act.wait_ge(cv_act, k + 1)
                act.activation(b_hi[:, k, :], sq[:, k % 2, :], ACT.Copy).then_inc(cv_hi, 1)

            gate_step(0)
            gate_step(1)
            for k in range(KT):
                act.wait_ge(cv_xc, k + 1)
                if k >= 2:
                    act.wait_ge(cv_used, k - 1)
                act.activation(sq[:, k % 2, :], conv[:, k, :], ACT.Square).then_inc(cv_sq, 1)
            gate_step(2)
            gate_step(3, gate=False)
            act.wait_ge(cv_used, KT)
            act.activation(rstd[:, :], ps[:, 5, :], ACT.Sqrt, bias=EPS, scale=1.0 / D).then_inc(cv_rt, 1)
            gate_step(3, panel_=False)
            gate_step(4, gate=False)
            for k in range(0, 3):
                conv_act(k)
            gate_step(4, panel_=False)
            gate_step(5, gate=False)
            for k in range(3, 6):
                conv_act(k)
            gate_step(5, panel_=False)
            gate_step(6, gate=False)
            for k in range(6, KT):
                conv_act(k)
            gate_step(6, panel_=False)
            gate_step(7)

            def merged_hi(k):
                act.wait_ge(pair_done, KT + k + 1)
                act.activation(a_hi[:, k, :], merged[:, k, :], ACT.Copy).then_inc(mhi_ready, 1)

            for k in range(KT):
                hi_next(k // 4, CO, k % 4)
                if k:
                    merged_hi(k - 1)
            merged_hi(KT - 1)

            def only_panels(first, count):
                with act.Fori(0, count // 4) as i:
                    for u in range(4):
                        hi_next(i, first, u)

            def panels_and_squares(first, n, ready0):
                for k in range(KT):
                    hi_next(k // 4, first, k % 4)
                    if k:
                        act.wait_ge(x_ready, ready0 + k)
                        norm_sq_tile(n, k - 1, x)
                act.wait_ge(x_ready, ready0 + KT)
                norm_sq(n, x, tiles=(KT - 1,))

            panels_and_squares(WO, 2, 0)
            norm_hi(2, b_hi, lambda k: mod[:, 3 * KT + k, 0:1])

            with act.Fori(0, HP // 4) as i:
                for u in range(4):
                    step(i, WQ, u)
                    act.activation(q_key[:, u % 2, :], ps[:, u, :], ACT.Copy)\
                       .then_inc(bank_free, 1)
                    act.wait_ge(bank_free, i * 4 + (4 + r_of(WQ) + u + 1))
                    act.sem_inc(qk_ready, 1)

            def gelu(i, u):
                hi_next(i, EU, u)
                act.wait_ge(used, i * 4 + (EU + u + 1))
                if not isinstance(i, int) or i:
                    act.wait_ge(ge_out[u], i * 16)
                act.activation(ge_slot[:, u, :], ps[:, u, :], ACT.Gelu).then_inc(bank_free, 1)
                act.wait_ge(bank_free, i * 4 + (4 + r_of(EU) + u + 1))
                act.dma_start(ge_d[bass.ds(i * 4 + u, 1)].rearrange("a p n -> (a p) n"), ge_slot[:, u, :]).then_inc(ge_out[u], 16)

            for u in range(4):
                gelu(0, u)
            with act.Fori(1, E_SOFT // 4) as i:
                for u in range(4):
                    gelu(i, u)
            act.wait_ge(soft_d, 1)
            act.activation(best, best, ACT.Exp).then_inc(soft_e, 1)
            with act.Fori(E_SOFT // 4, E_W // 4) as i:
                for u in range(4):
                    gelu(i, u)

            def stage_w(j, chunk, c, u):
                for v in range(2):
                    batch = 8 * c + 2 * u + v
                    act.wait_ge(w_staged, j * 32 + (chunk * 16 + batch + 1))
                    act.activation(stage[chunk][:, :, batch * 4:batch * 4 + 4],
                                   ps[:, 4 + batch % 4, :].rearrange("p (t k) -> p k t", t=4), ACT.Copy).then_inc(w_ready, 1)

            def chunks(j):
                for chunk in range(2):
                    for c in range(2):
                        for u in range(4):
                            gelu(j * 4 + (E_W // 4 + 2 * chunk + c), u)
                            if c == u == 0 and (not isinstance(j, int) or j):
                                act.wait_ge(w_out[chunk], j * 16)
                            stage_w(j, chunk, c, u)
                    act.wait_ge(w_ready, j * 32 + (chunk + 1) * 16)
                    act.dma_start(w_d.rearrange("i j (c t) -> c j i t", t=64)[bass.ds(j * 2 + chunk, 1)].rearrange("c j i t -> (c j) i t"),
                                  stage[chunk]).then_inc(w_out[chunk], 16)

            chunks(0)
            with act.Fori(1, 4) as j:
                chunks(j)

            with act.Fori(E_W // 4 + T // 32, NK // 4) as i:
                for u in range(4):
                    gelu(i, u)

            def z_hi(i, u):
                n = i * 4 + u
                act.wait_ge(z_ready, n + 1)
                if not isinstance(n, int) or n >= 4:
                    act.wait_ge(used, n + (EV - 4 + 1))
                act.activation(a_hi[:, u % 4, :], z[:, u % 2, :], ACT.Copy).then_inc(zhi_ready, 1)

            z_hi(0, 0)
            for u in range(4):
                z_hi(0, u + 1)
                hi_next(0, EV, u)
            with act.Fori(1, NK // 4 - 1) as i:
                for u in range(4):
                    z_hi(i, u + 1)
                    hi_next(i, EV, u)
            for u in range(4):
                if u < 3:
                    z_hi(NK // 4 - 1, u + 1)
                hi_next(NK // 4 - 1, EV, u)

            norm_sq(3, x, made=y_done)
            norm_sq(4, x, made=y1_ready)
            norm_hi(3, a_hi, lambda k: col("zero"))
            only_panels(SW, 12)

            groups = [(b, kt, half) for b in range(TT) for kt in range(2) for half in range(2)]

            def swa_exp(n):
                o = 16 * (n % 3)
                act.wait_ge(nmx2, 2 * (n + 1))
                for r in range(4):
                    act.activation(s2[:, n % 3, r * 256:(r + 1) * 256], s2[:, n % 3, r * 256:(r + 1) * 256], ACT.Exp,
                                   bias=tiny[:, o + 4 + r:o + 5 + r], accum_out=tiny[:, o + 8 + r:o + 9 + r]).then_inc(e2, 1)
                act.activation(tiny[:, o + 12:o + 16], tiny[:, o + 12:o + 16], ACT.Exp).then_inc(snk2, 1)

            def swa_out(n):
                b, kt, half = groups[n]
                act.wait_ge(pt2, n + 1)
                if b == 0:
                    act.activation(p2T[:, 1, :], ps[:, 5, :], ACT.Copy).then_inc(ptc2, 1)
                else:
                    act.activation(p2T[:, :, :], ps[:, 4:6, :], ACT.Copy).then_inc(ptc2, 1)

            def swa_hi(n):
                b, kt, half = groups[n]
                act.wait_ge(pv2, n + 1)
                rows_ = slice(half * HD2, (half + 1) * HD2)
                act.activation(b_hi[rows_, kt * 4:kt * 4 + 4, b * P:(b + 1) * P],
                               ps[rows_, 6 + n % 2, :].rearrange("p (r t) -> p r t", r=4), ACT.Copy).then_inc(ohi2, 1)

            swa_exp(0)
            for n in range(len(groups)):
                if n + 1 < len(groups):
                    swa_exp(n + 1)
                swa_out(n)
                if n:
                    swa_hi(n - 1)
            swa_hi(len(groups) - 1)

            panels_and_squares(SO, 5, KT)
            norm_hi(4, a_hi, lambda k: col("zero"))
            with act.Fori(0, 2 * FT // 4) as i:
                for u in range(4):
                    step(i, GU, u)
                    if u % 2 == 0:
                        act.activation(sq[:, u // 2, :], ps[:, u, :], ACT.Silu).then_inc(gate_ready, 1)

            def hid_hi(i, u):
                n = i * 4 + u
                if not isinstance(n, int) or n >= 4:
                    act.wait_ge(used, n + (DN - 4 + 1))
                act.activation(b_hi[:, u % 4, :], hid[:, bass.ds(n, 1), :] if not isinstance(n, int) else hid[:, n, :],
                               ACT.Copy).then_inc(dhi_ready, 1)

            act.wait_ge(act_done, FT)
            hid_hi(0, 0)
            for u in range(4):
                hid_hi(0, u + 1)
                hi_next(0, DN, u)
            with act.Fori(1, FT // 4) as i:
                for u in range(4):
                    hid_hi(i, u + 1)
                    hi_next(i, DN, u)
            hid_hi(FT // 4, 1)
            hi_next(FT // 4, DN, 0)
            norm_sq(6, x, made=y2_done)

        @block.vector
        def _(dve):
            def lo(g, u):
                dve.wait_ge(hi_ready, g + (1 - U))
                dve.tensor_tensor(wlo[:, u % SPLIT, :], raw[:, u % RAW, :], f32(whi[:, u % SPLIT, :]), ALU.subtract).then_inc(lo_ready, 1)

            def lo_next(i, first, u):
                lo(i * 4 + (first + u + 1), u + 1)

            def done(i, first, u):
                dve.wait_ge(used, i * 4 + (first + u + 1))

            def step(i, first, u):
                lo_next(i, first, u)
                dve.wait_ge(used, i * 4 + (first + u + 1))

            def norm_rstd(n, r=rstd[:, :]):
                dve.wait_ge(rt_ready, n + 1)
                dve.reciprocal(r, r).then_inc(rstd_ready, 1)
                dve.wait_ge(rstd_ready, n + 1)

            def norm_apply(m, src, gain, shift, hi_, lo_, width=T, r=rstd[:, :]):
                def low(k):
                    dve.wait_ge(nhi_ready, m * KT + k + 1)
                    dve.scalar_tensor_tensor(lo_[:, k, 0:width], nt[:, k % 2, 0:width], shift(k), f32(hi_[:, k, 0:width]),
                                             ALU.add, ALU.subtract).then_inc(h_ready, 1)
                for k in range(KT):
                    if k >= 2:
                        low(k - 2)
                        dve.wait_ge(h_ready, m * KT + k - 1)
                    elif m:
                        dve.wait_ge(h_ready, m * KT)
                    dve.scalar_tensor_tensor(nt[:, k % 2, 0:width], src[:, k, 0:width], gain(k), r,
                                             ALU.mult, ALU.mult).then_inc(nt_ready, 1)
                low(KT - 2)
                low(KT - 1)

            def fold(chains_, sem_, base):
                count = len(chains_)
                for k in range(KT):
                    for c, (dst, src, cond) in enumerate(chains_):
                        w, by = src[:, k * P:(k + 1) * P], c_act[:, k, cond:cond + 1]
                        if k == 0:
                            dve.tensor_scalar(dst, w, by, None, ALU.mult).then_inc(sem_, 1)
                        else:
                            dve.wait_ge(sem_, base + ((k - 1) * count + c + 1))
                            dve.scalar_tensor_tensor(dst, w, by, dst, ALU.mult, ALU.add).then_inc(sem_, 1)

            dve.wait_ge(c_ready, 1)
            for n in range(MOD_RING, MOD_RING + 2 * RAW):
                if n % 4 == 0:
                    dve.wait_ge(mod_in[n // 4 - 1], 16)
                if n >= MOD_RING + RAW:
                    dve.wait_ge(used, n - RAW + 1)
                fold([(fold1[:, n % 4, c, :], mod_panels[:, n - MOD_RING, :], c) for c in range(2)], folds, (n - MOD_RING) * 2 * KT)
            norm_rstd(0)
            norm_rstd(1, rstd_c)
            def add_bias(src, first, last, gains):
                n, cs = last - first, src.shape[-1] // (last - first)
                dve.tensor_tensor(mod[:, first:last, 0:cs], src.rearrange("p (n c) -> p n c", c=cs),
                                  col("b_mod", first, n).unsqueeze(2).to_broadcast([P, n, cs]), ALU.add).then_inc(mod_done, 1)
                dve.wait_ge(mod_done, 1 if first == 0 else 4)
                for dst, at, c, gname in gains:
                    dve.scalar_tensor_tensor(dst[:, :], mod[:, at:at + KT, c], 1.0, col(gname, 0, KT), ALU.add, ALU.mult).then_inc(mod_done, 1)

            dve.wait_ge(used, U)
            add_bias(ps[:, 7, 0:2 * MOD1], 0, MOD1, ((gs1, KT, 0, "norm1"), (gs1c, KT, 1, "norm1")))
            dve.sem_inc(bank_free, BANKS)
            dve.sem_inc(o_ready, 2)
            dve.wait_ge(mod_done, 3)
            norm_apply(0, x, lambda k: gs1[:, k:k + 1], lambda k: mod[:, k, 0:1], a_hi, a_lo)

            def tap(tile, j, done_, n, first):
                at = slice(tile, tile + 1) if isinstance(tile, int) else bass.ds(tile, 1)
                src = g_pad[:, at, j:j + T] if isinstance(j, int) else g_pad[:, at, bass.ds(j, T)]
                w = sm[:, bass.ds(tile * TAPS + j + SMALL["conv_w"][0], 1)]
                acc = conv[:, at, :]
                if first:
                    b = sm[:, bass.ds(tile + SMALL["conv_b"][0], 1)]
                    dve.tensor_scalar(acc, src, w, b, ALU.mult, ALU.add).then_inc(done_, 1)
                else:
                    dve.wait_ge(done_, n)
                    dve.scalar_tensor_tensor(acc, src, w, acc, ALU.mult, ALU.add).then_inc(done_, 1)

            dve.wait_ge(pad_ready, 1)
            with dve.Fori(0, 2) as i:
                for u in range(KT):
                    if u % 2:
                        p = i * (KT // 2) + u // 2
                        dve.wait_ge(used, i * KT + (U + u + 1))
                        dve.wait_ge(gate_ready, p + 1)
                        dve.tensor_tensor(g_pad[:, bass.ds(p, 1), PAD:PAD + T], sq[:, u // 2 % 2, :], ps[:, (u - 1) % 4, :],
                                          ALU.mult).then_inc(pair_done, 1)
                        dve.wait_ge(pair_done, p + 1)
                        dve.sem_inc(bank_free, 2)
                        for j in range(u // 2 * 8, min(u // 2 * 8 + 8, TAPS)):
                            tap(i, j, tap_done, i * TAPS + j, j == 0)

            def head_norm(n, src, gain, dst, width=T):
                dve.wait_ge(krt, n + 1)
                dve.reciprocal(rstd[:, 0:width], rstd[:, 0:width]).then_inc(krstd, 1)
                dve.wait_ge(krstd, n + 1)
                dve.scalar_tensor_tensor(dst, src, gain, rstd[:, 0:width], ALU.mult, ALU.mult).then_inc(kn, 1)
                dve.wait_ge(kn, n + 1)

            def head_turn(m, slot, dst):
                dve.tensor_tensor(q_rot[:, 0, :], q_n[:, slot, :], cos, ALU.mult).then_inc(kcos, 1)
                dve.wait_ge(krot, m + 1)
                dve.tensor_tensor(q_rot[:, 1, :], ps[:, 5, :], sin, ALU.mult).then_inc(ksin, 1)
                dve.wait_ge(kcos, m + 1)
                dve.wait_ge(ksin, m + 1)
                dve.tensor_tensor(dst, q_rot[:, 0, :], q_rot[:, 1, :], ALU.add).then_inc(k_done, 1)
                dve.wait_ge(k_done, m + 1)

            norm_apply(1, x_ctx, lambda k: gs1c[:, k:k + 1], lambda k: mod[:, k, 1:2], b_hi, b_lo, CTX, rstd_c)
            dve.wait_ge(rope_in, 16)
            head_norm(0, ps[:, 0, :], col("k_g"), q_n[:, 0, :])
            dve.sem_inc(bank_free, 1)
            head_norm(1, ps[:, 6, 0:CTX], col("k_g"), kT[:, 0, T:S1], CTX)
            head_turn(0, 0, kT[:, 0, 0:T])
            head_norm(2, ps[:, 1, :], col("k_g"), q_n[:, 1, :])
            dve.sem_inc(bank_free, 1)
            for u in range(2):
                dve.tensor_copy(v_feat[:, u, 0:T], ps[:, 2 + u, :]).then_inc(v_feat_ready, 1)
                dve.tensor_copy(v_feat[:, u, T:S1], ps[:, 7, u * CTX:(u + 1) * CTX]).then_inc(v_feat_ready, 1)
            dve.wait_ge(v_feat_ready, 4)
            dve.sem_inc(bank_free, 2)
            head_norm(3, ps[:, 6, CTX:2 * CTX], col("k_g"), kT[:, 1, T:S1], CTX)
            head_turn(1, 1, kT[:, 1, 0:T])

            def take_values(u):
                dve.wait_ge(v_turned, u + 1)
                dve.tensor_copy(v_tok[:, :, u * P:(u + 1) * P].rearrange("p (a s) n -> p a s n", a=2),
                                ps[:, 6:8, 0:3 * P].rearrange("p a (s n) -> p a s n", n=P)).then_inc(v_done, 1)

            def q_step(i, u):
                head_norm(i * 4 + (u + 4), ps[:, u, :], col("q_g"), q_n[:, u % 2, :])
                dve.sem_inc(bank_free, 1)
                head_turn(i * 4 + (u + 2), u % 2, qT[:, bass.ds(i * 4 + u, 1), :])

            for u in range(4):
                q_step(0, u)
                if u < 2:
                    take_values(u)
            with dve.Fori(1, NH // 4) as i:
                for u in range(4):
                    q_step(i, u)

            def att_queries(h, hu):
                dve.tensor_copy(q_slot[:, hu, :], qT[:, bass.ds(h, 1), :] if not isinstance(h, int) else qT[:, h, :]).then_inc(qs_ready, 1)

            def att_max(i, s):
                n = i * (2 * TT) + s
                t = s % TT
                dve.wait_ge(sc_ready, n + 1)
                dve.tensor_reduce(tiny[:, 4 + t:5 + t], ps[:, 2 * (t % 2):2 * (t % 2) + 2, :].rearrange("p a b -> p (a b)")[:, 0:S1],
                                  AX.X, ALU.max).then_inc(top_ready, 1)
                dve.wait_ge(top_ready, n + 1)
                dve.tensor_scalar(tiny[:, t:t + 1], tiny[:, 4 + t:5 + t], -(P ** -0.5), None, ALU.mult).then_inc(mx_ready, 1)

            def att_lo(m, h, hu):
                dve.wait_ge(ohi_ready, m + 1)
                at = bass.ds(h, 1) if not isinstance(h, int) else slice(h, h + 1)
                dve.tensor_tensor(b_lo[:, at, :], ps[:, 6 + hu, :].unsqueeze(1), f32(b_hi[:, at, :]), ALU.subtract).then_inc(o_ready, 1)

            def att_step(i, s, ahead=True, more=True):
                n = i * (2 * TT) + s
                hu, t = s // TT, s % TT
                dve.wait_ge(p_ready, n + 1)
                dve.reciprocal(tiny[:, 12 + t:13 + t], tiny[:, 8 + t:9 + t]).then_inc(rs_ready, 1)
                dve.wait_ge(rs_ready, n + 1)
                dve.tensor_scalar(prob[:, t, :], prob[:, t, :], tiny[:, 12 + t:13 + t], None, ALU.mult).then_inc(pn_ready, 1)
                if t == 0 and hu == 0:
                    att_queries(i + NH // 2, 1)
                elif t == 0 and more:
                    att_queries(i + 1, 0)
                if ahead:
                    att_max(i, s + 2)
                if not isinstance(n, int) or n < TAPS:
                    tap(2, n, tap_done, n + 2 * TAPS, isinstance(n, int) and n == 0)
                    tap(6, n, tap6_done, n, isinstance(n, int) and n == 0)
                if t == 1 and hu:
                    att_lo(i * 2, i, 0)
                elif t == 1 and (not isinstance(i, int) or i):
                    att_lo(i * 2 - 1, i + (NH // 2 - 1), 1)

            att_queries(0, 0)
            att_max(0, 0)
            att_max(0, 1)
            for s in range(2 * TT):
                att_step(0, s)
            with dve.Fori(1, NH // 2 - 1) as i:
                for s in range(2 * TT):
                    att_step(i, s)
            for s in range(2 * TT):
                att_step(NH // 2 - 1, s, s + 2 < 2 * TT, False)
            att_lo(NH - 1, NH - 1, 1)
            for p in range(KT):
                dve.wait_ge(used, AO + 2 * p + 2)
                dve.wait_ge(gate_ready, KT + p + 1)
                dve.tensor_tensor(merged[:, p, :], sq[:, p % 2, :], ps[:, 2 * p % 4 + 1, :], ALU.mult).then_inc(co_mul, 1)
                dve.wait_ge(co_mul, p + 1)
                dve.sem_inc(bank_free, 2)
                for n in range(4):
                    for j in (p % 4 * 8 + 2 * n, p % 4 * 8 + 2 * n + 1):
                        if j < TAPS:
                            tap(3 + p // 4, j, tap_done, (3 + p // 4) * TAPS + j, j == 0)
                    if p * 4 + n < TAPS:
                        tap(5, p * 4 + n, tap5_done, p * 4 + n, p * 4 + n == 0)

            def fold_pair(pair):
                if pair >= 4:
                    dve.wait_ge(summed2, 2 * (pair - 3))
                for n in (2 * pair, 2 * pair + 1):
                    dve.wait_ge(mod2_in[n % 4], (n // 4 + 1) * 16)
                fold([(fold2[:, n % 8, :], mod2_ring[:, n % 4, :], 0) for n in (2 * pair, 2 * pair + 1)], folds2, pair * 2 * KT)

            dve.wait_ge(cv_sum, 1)
            dve.tensor_scalar(nt[:, 0, :], ps[:, 4, :], 1.0 / D, None, ALU.mult).then_inc(cv_mu, 1)
            dve.wait_ge(cv_mu, 1)
            for k in range(KT):
                dve.tensor_tensor(conv[:, k, :], conv[:, k, :], nt[:, 0, :], ALU.subtract).then_inc(cv_xc, 1)
            for pair in range(3):
                fold_pair(pair)
            dve.wait_ge(cv_rt, 1)
            dve.reciprocal(rstd[:, :], rstd[:, :]).then_inc(cv_rstd, 1)
            dve.wait_ge(cv_rstd, 1)
            dve.wait_ge(cv_xc, KT)
            for k in range(KT + 1):
                if k < KT:
                    if k >= 2:
                        dve.wait_ge(cv_act, k - 1)
                    dve.tensor_tensor(nt[:, k % 2, :], conv[:, k, :], rstd[:, :], ALU.mult).then_inc(cv_t, 1)
                if k:
                    dve.wait_ge(cv_hi, k)
                    dve.tensor_tensor(b_lo[:, k - 1, :], sq[:, (k - 1) % 2, :], f32(b_hi[:, k - 1, :]), ALU.subtract).then_inc(cv_ready, 1)
            for pair in range(3, 5):
                fold_pair(pair)

            def merged_lo(k):
                dve.wait_ge(mhi_ready, k + 1)
                dve.tensor_tensor(a_lo[:, k, :], merged[:, k, :], f32(a_hi[:, k, :]), ALU.subtract).then_inc(m_ready, 1)

            dve.wait_ge(bank_free, r_of(CO) + BANKS)
            for k in range(KT):
                dve.wait_ge(used, CO + k + 1)
                dve.tensor_tensor(nt[:, k % 2, :], gate_c[:, k, :], ps[:, k % 4, :], ALU.mult).then_inc(co_mul, 1)
                dve.wait_ge(co_mul, KT + k + 1)
                dve.sem_inc(bank_free, 1)
                dve.tensor_tensor(merged[:, k, :], merged[:, k, :], nt[:, k % 2, :], ALU.add).then_inc(pair_done, 1)
                if k:
                    merged_lo(k - 1)
                if 5 + k < MOD2A // 2:
                    fold_pair(5 + k)
            merged_lo(KT - 1)
            dve.wait_ge(summed2, MOD2A)
            add_bias(ps[:, 6, 0:MOD2A], MOD1, MOD1 + MOD2A, ((gs2, 4 * KT, 0, "norm2"),))
            dve.wait_ge(mod_done, 5)

            def add_to_x(first, count, gain, ready0, arrived):
                with dve.Fori(0, count // 4) as i:
                    for u in range(4):
                        arrived(i, first, u)
                        n = i * 4 + u
                        xn = x[:, bass.ds(n, 1), :]
                        if gain is None:
                            dve.tensor_tensor(xn, ps[:, u, :], xn, ALU.add).then_inc(x_ready, 1)
                        else:
                            dve.scalar_tensor_tensor(xn, ps[:, u, :], mod[:, bass.ds(n + gain, 1), 0], xn, ALU.mult, ALU.add).then_inc(x_ready, 1)
                        dve.wait_ge(x_ready, n + (ready0 + 1))
                        dve.sem_inc(bank_free, 1)

            add_to_x(WO, KT, 2 * KT, 0, done)
            norm_rstd(2)
            norm_apply(2, x, lambda k: gs2[:, k:k + 1], lambda k: mod[:, 3 * KT + k, 0:1], b_hi, b_lo)

            for pair in range(MOD2A // 2, (MOD_N - MOD1) // 2):
                fold_pair(pair)
            sc4 = scores.rearrange("p (t c) n -> p t c n", t=TT)
            with dve.Fori(0, HP // 4) as i:
                for u in range(1, 5):
                        dve.wait_ge(s_ready, i * 4 + u)
                        dve.tensor_copy(sc4[:, :, bass.ds(i * 4 + (u - 1), 1), :].rearrange("p t c n -> p t (c n)"),
                                        ps[:, 3 + u, :].rearrange("p (t n) -> p t n", n=P)).then_inc(s_done, 1)

            dve.wait_ge(summed2, MOD_N - MOD1)
            dve.tensor_tensor(mod[:, MOD1 + MOD2A:MOD_N, 0], ps[:, 4, MOD2A:MOD_N - MOD1], col("b_mod", MOD1 + MOD2A, KT), ALU.add).then_inc(mod_done, 1)
            held = tiny[:, 56:60]
            iota16 = col("iota", 0, TOPK)
            flat = lambda ap: ap.rearrange("p a b -> p (a b)")
            row = lambda ap, n: ap[:, bass.ds(n, 1), :].rearrange("p a n -> p (a n)")

            def chains(sem_, base, count):
                total, mark = [0], [0] * count

                def did(c, ins):
                    ins.then_inc(sem_, 1)
                    total[0] += 1
                    mark[c] = total[0]

                def after(c):
                    dve.wait_ge(sem_, base + mark[c])
                    dve.memset(held[:, c:c + 1], 0.0)
                return did, after, total

            def top16(did, after, src, rep, vals, idx):
                all_ = range(len(src))
                for c in all_:
                    after(c)
                    did(c, dve.max(vals[c][:, 0:8], src[c]))
                for c in all_:
                    after(c)
                    did(c, dve.max_index(idx[c][:, 0:8], vals[c][:, 0:8], src[c]))
                    did(c, dve.match_replace(rep[c], vals[c][:, 0:8], src[c], -3.0e38))
                for c in all_:
                    after(c)
                    did(c, dve.max(vals[c][:, 8:16], rep[c]))
                for c in all_:
                    after(c)
                    did(c, dve.max_index(idx[c][:, 8:16], vals[c][:, 8:16], rep[c]))

            A, C1 = A_TK, 4
            words = 2 * NK + 2 * TOPK
            s_in = [area(A + c * words, NK) for c in range(C1)]
            s_rep = [area(A + c * words + NK, NK) for c in range(C1)]
            v16 = [area(A + c * words + 2 * NK, TOPK) for c in range(C1)]
            i16 = [area(A + c * words + 2 * NK + TOPK, TOPK).bitcast(U32) for c in range(C1)]
            L1 = 8 * C1
            with dve.Fori(0, 64 // C1) as i:
                did, after, total = chains(lv1, i * L1, C1)
                for c in range(C1):
                    did(c, dve.tensor_copy(s_in[c], row(scores, i * C1 + c)))
                top16(did, after, s_in, s_rep, v16, i16)
                for c in range(C1):
                    after(c)
                    did(c, dve.tensor_copy(row(v1, i * C1 + c), v16[c]))
                    did(c, dve.tensor_copy(row(i1, i * C1 + c), i16[c]))
                after(C1 - 1)
                assert total[0] == L1
            C2 = 2
            words = 2 * TOPK * TOPK + 4 * TOPK + 2 * TOPK * TOPK
            at = lambda c, o: A + c * words + o
            cand = [area(at(c, 0), TOPK, TOPK) for c in range(C2)]
            cand_rep = [area(at(c, 256), TOPK * TOPK) for c in range(C2)]
            b16 = [area(at(c, 512), TOPK) for c in range(C2)]
            pos = [area(at(c, 528), TOPK).bitcast(U32) for c in range(C2)]
            pos2 = [area(at(c, 544), 2, TOPK).bitcast(U32) for c in range(C2)]
            eq = [area(at(c, 576), 2, TOPK * TOPK) for c in range(C2)]
            assert 2 * words <= A_KEYS - A_TK
            L2 = 12 * C2
            with dve.Fori(0, 32 // C2) as i:
                did, after, total = chains(lv2, i * L2, C2)
                for c in range(C2):
                    n = i * C2 + c
                    did(c, dve.tensor_tensor(cand[c], row(v1, n * 2).unsqueeze(2).to_broadcast([P, TOPK, TOPK]),
                                             row(v1, n * 2 + 1).unsqueeze(1).to_broadcast([P, TOPK, TOPK]), ALU.add))
                top16(did, after, [flat(v) for v in cand], cand_rep, b16, pos)
                for c in range(C2):
                    after(c)
                    did(c, dve.tensor_copy(row(best, i * C2 + c), b16[c]))
                    did(c, dve.tensor_scalar(pos2[c][:, 0, :], pos[c], 4, None, ALU.logical_shift_right))
                    did(c, dve.tensor_scalar(pos2[c][:, 1, :], pos[c], TOPK - 1, None, ALU.bitwise_and))
                for c in range(C2):
                    after(c)
                    did(c, dve.tensor_tensor(eq[c].rearrange("p c (k a) -> p (c k) a", a=TOPK),
                                             pos2[c].rearrange("p c k -> p (c k)").unsqueeze(2).to_broadcast([P, 2 * TOPK, TOPK]),
                                             iota16.unsqueeze(1).to_broadcast([P, 2 * TOPK, TOPK]), ALU.is_equal))
                eq5 = [v.rearrange("p c (k a) -> p c k a", a=TOPK) for v in eq]
                for c in range(C2):
                    after(c)
                    did(c, dve.tensor_tensor(eq5[c], eq5[c], i1[:, bass.ds((i * C2 + c) * 2, 2), :].unsqueeze(2).to_broadcast([P, 2, TOPK, TOPK]),
                                             ALU.mult))
                for c in range(C2):
                    after(c)
                    did(c, dve.tensor_reduce(ij[:, :, bass.ds((i * C2 + c) * TOPK, TOPK)], eq5[c], AX.X, ALU.add))
                after(C2 - 1)
                assert total[0] == L2
            mx = area(A, 32)
            dve.tensor_copy(mx.unsqueeze(2), best[:, :, 0:1]).then_inc(mx_ready, 1)
            dve.wait_ge(mx_ready, NH * TT + 1)
            dve.tensor_tensor(best, best, mx.unsqueeze(2).to_broadcast([P, 32, TOPK]), ALU.subtract).then_inc(soft_d, 1)
            dve.wait_ge(soft_e, 1)
            den = area(A + 32, 32)
            dve.tensor_reduce(den, best, AX.X, ALU.add).then_inc(mx_ready, 1)
            dve.wait_ge(mx_ready, NH * TT + 2)
            dve.reciprocal(mx, den).then_inc(mx_ready, 1)
            dve.wait_ge(mx_ready, NH * TT + 3)
            dve.tensor_tensor(best, best, mx.unsqueeze(2).to_broadcast([P, 32, TOPK]), ALU.mult).then_inc(soft, 1)
            dve.wait_ge(ijw_t, 1)
            dve.tensor_copy(tok_i, ps[:, 4, :]).then_inc(ijw, 1)
            dve.tensor_copy(tok_j, ps[:, 5, :]).then_inc(ijw, 1)
            dve.tensor_copy(w_bf, ps[:, 6, :]).then_inc(ijw, 1)
            dve.tensor_copy(iota_b[:, :], col("iota", 0, P)).then_inc(ijw, 1)
            dve.wait_ge(ijw, 3)
            dve.tensor_copy(tok_w[0], w_bf).then_inc(ijw, 1)
            dve.wait_ge(ijw, 5)
            dve.tensor_tensor(tok_w[2], ps[:, 6, :], tok_w[0], ALU.subtract).then_inc(ijw, 1)
            dve.wait_ge(ijw, 6)
            dve.tensor_copy(w_bf, tok_w[2]).then_inc(ijw, 1)
            dve.wait_ge(ijw, 7)
            dve.tensor_copy(tok_w[1], w_bf).then_inc(ijw, 1)
            dve.wait_ge(ijw, 8)
            dve.tensor_tensor(tok_w[2], tok_w[2], tok_w[1], ALU.subtract).then_inc(ijw, 1)
            dve.wait_ge(ijw, 9)
            tok_j_b = w_bf
            dve.tensor_copy(tok_j_b, tok_j).then_inc(ijw, 1)
            dve.wait_ge(ijw, 10)

            def one_hot(n, v):
                dve.tensor_tensor(hot[v][:, :, 0, :], iota_b[:, :].unsqueeze(1).to_broadcast([P, 4, P]),
                                  tok_j_b[:, bass.ds(n * 4, 4)].unsqueeze(2).to_broadcast([P, 4, P]), ALU.is_equal)
                for t in range(4):
                    at = bass.ds(n * 4 + t, 1) if not isinstance(n, int) else slice(n * 4 + t, n * 4 + t + 1)
                    for c in range(3):
                        last = dve.tensor_scalar(hot[v][:, t, c + 1, :], iota_b[:, :], tok_i[:, at], tok_w[c][:, at],
                                                 ALU.is_equal, ALU.mult)
                last.then_inc(hot_ready, 1)

            one_hot(0, 0)
            one_hot(1, 1)
            with dve.Fori(1, T // 8) as i:
                for v in range(2):
                    dve.wait_ge(w_staged, i * 2 + (v - 1))
                    one_hot(i * 2 + v, v)

            def weigh(i, u):
                n = i * 4 + u
                slot, times = u % 4, u // 4
                dve.wait_ge(wg_in[slot], (i + times + 1) * 32)
                if not isinstance(n, int) or n >= 2:
                    dve.wait_ge(zlo_ready, n - 1)
                dve.tensor_tensor(z[:, u % 2, :], w_ring[:, slot, :], ge_ring[:, slot, :], ALU.mult).then_inc(z_ready, 1)

            def z_lo(i, u):
                dve.wait_ge(zhi_ready, i * 4 + (u + 1))
                dve.tensor_tensor(a_lo[:, u % 4, :], z[:, u % 2, :], f32(a_hi[:, u % 4, :]), ALU.subtract).then_inc(zlo_ready, 1)

            weigh(0, 0)
            weigh(0, 1)
            z_lo(0, 0)
            dve.wait_ge(lo_ready, EV - U + 1)
            with dve.Fori(0, NK // 4 - 1) as i:
                for u in range(4):
                    weigh(i, u + 2)
                    lo_next(i, EV, u)
                    z_lo(i, u + 1)
            for u in range(4):
                if u < 2:
                    weigh(NK // 4 - 1, u + 2)
                lo_next(NK // 4 - 1, EV, u)
                if u < 3:
                    z_lo(NK // 4 - 1, u + 1)
            dve.wait_ge(mod_done, 6)

            def await_bank(k, layer, first_of_next):
                if k < KT - 1:
                    dve.wait_ge(bank_done, layer * (KT - 1) + k + 1)
                else:
                    dve.wait_ge(used, first_of_next)

            for k in range(KT):
                await_bank(k, 0, SW)
                dve.scalar_tensor_tensor(x[:, k, :], ps[:, k, :], mod[:, 5 * KT + k, 0:1], x[:, k, :], ALU.mult, ALU.add).then_inc(y_done, 1)
            norm_rstd(3)
            dve.wait_ge(y_done, KT)
            for k in range(KT):
                dve.scalar_tensor_tensor(x[:, k, :], x[:, k, :], col("final1", k), rstd[:, :], ALU.mult, ALU.mult).then_inc(y1_ready, 1)
            norm_rstd(4)
            norm_apply(3, x, lambda k: col("mix", k), lambda k: col("zero"), a_hi, a_lo)

            for u in range(4):
                lo_next(0, SW, u)
            for u in range(2):
                dve.wait_ge(used, SW + u + 1)
                dve.tensor_copy(k2[:, u, :], ps[:, u, :]).then_inc(bank_free, 1)
            for u in range(2):
                dve.wait_ge(used, SW + u + 3)
                dve.tensor_copy(v2_feat_sb[:, u, :], ps[:, 2 + u, :]).then_inc(v2_feat, 1)
            dve.wait_ge(v2_feat, 2)
            dve.sem_inc(bank_free, 2)
            for u in range(2):
                dve.wait_ge(v2_turned, u + 1)
                dve.tensor_copy(v2[:, :, u * P:(u + 1) * P], ps[:, 4 + u, :].rearrange("p (s n) -> p s n", n=P)).then_inc(v2_done, 1)
            with dve.Fori(0, 2) as i:
                for u in range(4):
                    step(i, SW + 4, u)
                    dve.tensor_scalar(q2[:, bass.ds(i * 4 + u, 1), :], ps[:, u, :], HD2 ** -0.5, None, ALU.mult).then_inc(bank_free, 1)

            groups = [(b, kt, half) for b in range(TT) for kt in range(2) for half in range(2)]

            def swa_bias(n):
                b, kt, half = groups[n]
                o = 16 * (n % 3)
                dve.wait_ge(sc2, n + 1)
                if n >= 3:
                    dve.wait_ge(pt2, n - 2)
                if b == 0:
                    for r in range(4):
                        h = 8 * kt + 4 * half + r
                        dve.tensor_scalar(s2[:, n % 3, r * 256:r * 256 + P], dist[:, 1, 0:P], col("slopes", h), None, ALU.mult)
                for r in range(4):
                    h = 8 * kt + 4 * half + r
                    at = P if b == 0 else 0
                    dve.scalar_tensor_tensor(s2[:, n % 3, r * 256 + at:(r + 1) * 256], dist[:, 0, at:256], col("slopes", h),
                                             ps[:, 2 * (n % 2) + r // 2, (r % 2) * 256 + at:(r % 2) * 256 + 256],
                                             ALU.mult, ALU.add).then_inc(bias2, 1)
                dve.wait_ge(bias2, 4 * (n + 1))
                dve.tensor_reduce(tiny[:, o:o + 4], s2[:, n % 3, :].rearrange("p (r n) -> p r n", r=4), AX.X, ALU.max).then_inc(mx2, 1)
                dve.wait_ge(mx2, 2 * n + 1)
                h = 8 * kt + 4 * half
                dve.tensor_tensor(tiny[:, o:o + 4], tiny[:, o:o + 4], col("sinks", h, 4), ALU.max).then_inc(mx2, 1)
                dve.wait_ge(mx2, 2 * n + 2)
                dve.tensor_scalar(tiny[:, o + 4:o + 8], tiny[:, o:o + 4], -1.0, None, ALU.mult).then_inc(nmx2, 1)
                dve.tensor_tensor(tiny[:, o + 12:o + 16], col("sinks", h, 4), tiny[:, o:o + 4], ALU.subtract).then_inc(nmx2, 1)

            def swa_norm(n):
                o = 16 * (n % 3)
                dve.wait_ge(e2, 4 * (n + 1))
                dve.wait_ge(snk2, n + 1)
                dve.tensor_tensor(tiny[:, o + 8:o + 12], tiny[:, o + 8:o + 12], tiny[:, o + 12:o + 16], ALU.add).then_inc(den2, 1)
                dve.wait_ge(den2, n + 1)
                dve.reciprocal(tiny[:, o + 12:o + 16], tiny[:, o + 8:o + 12]).then_inc(rec2, 1)
                dve.wait_ge(rec2, n + 1)
                pr = s2[:, n % 3, :].rearrange("p (r n) -> p r n", r=4)
                dve.tensor_tensor(pr, pr, tiny[:, o + 12:o + 16].unsqueeze(2).to_broadcast([P, 4, 256]), ALU.mult).then_inc(pn2, 1)

            def swa_lo(n):
                b, kt, half = groups[n]
                rows_ = slice(half * HD2, (half + 1) * HD2)
                dve.wait_ge(ohi2, n + 1)
                at = slice(b * P, (b + 1) * P)
                dve.tensor_tensor(b_lo[rows_, kt * 4:kt * 4 + 4, at], ps[rows_, 6 + n % 2, :].rearrange("p (r t) -> p r t", r=4),
                                  f32(b_hi[rows_, kt * 4:kt * 4 + 4, at]), ALU.subtract).then_inc(o2, 1)

            dve.wait_ge(dist_in, 16)
            dve.wait_ge(bank_free, r_of(SO) + 4)
            swa_bias(0)
            swa_bias(1)
            for n in range(len(groups)):
                swa_norm(n)
                if n >= 2:
                    swa_lo(n - 2)
                if n + 2 < len(groups):
                    swa_bias(n + 2)
            swa_lo(len(groups) - 2)
            swa_lo(len(groups) - 1)

            add_to_x(SO, KT, None, KT, step)
            norm_rstd(5)
            norm_apply(4, x, lambda k: col("ffn", k), lambda k: col("zero"), a_hi, a_lo)

            with dve.Fori(0, 2 * FT // 4) as i:
                for u in range(4):
                    step(i, GU, u)
                    if u % 2:
                        p = i * 2 + u // 2
                        dve.wait_ge(gate_ready, p + (2 * KT + 1))
                        dve.tensor_tensor(hid[:, bass.ds(p, 1), :], sq[:, u // 2, :], ps[:, u, :], ALU.mult).then_inc(act_done, 1)
                        dve.wait_ge(act_done, p + 1)
                        dve.sem_inc(bank_free, 2)

            def hid_lo(i, u):
                n = i * 4 + u
                dve.wait_ge(dhi_ready, n + 1)
                dve.tensor_tensor(b_lo[:, u % 4, :], hid[:, bass.ds(n, 1), :] if not isinstance(n, int) else hid[:, n, :],
                                  f32(b_hi[:, u % 4, :]), ALU.subtract).then_inc(dlo_ready, 1)

            hid_lo(0, 0)
            with dve.Fori(0, FT // 4) as i:
                for u in range(4):
                    hid_lo(i, u + 1)
                    lo_next(i, DN, u)
            hid_lo(FT // 4, 1)
            lo_next(FT // 4, DN, 0)
            for k in range(KT):
                await_bank(k, 1, PANELS)
                dve.tensor_tensor(x[:, k, :], ps[:, k, :], x[:, k, :], ALU.add).then_inc(y2_done, 1)
            norm_rstd(6)
            dve.wait_ge(y2_done, KT)
            for k in range(KT):
                dve.scalar_tensor_tensor(x[:, k, :], x[:, k, :], col("final2", k), rstd[:, :], ALU.mult, ALU.mult).then_inc(out_done, 1)

        @block.gpsimd
        def _(pool):
            nc.gpsimd.memset(g_pad[:, :, 0:PAD], 0.0)
            nc.gpsimd.memset(g_pad[:, :, PAD + T:GW], 0.0).then_inc(pad_ready, 1)
            pool.wait_ge(small_in, 16)

            def lo(g, u):
                pool.wait_ge(hi_ready, g + (1 - U))
                nc.gpsimd.tensor_tensor(wlo[:, u % SPLIT, :], raw[:, u % RAW, :], f32(whi[:, u % SPLIT, :]), ALU.subtract).then_inc(lo_ready, 1)

            with pool.Fori(0, (AO - U) // 4) as i:
                for u in range(4):
                    lo(i * 4 + (U + u), u)
            lo(AO, 0)
            tmp = area(A_TMP, T)
            pool.wait_ge(pair_done, KT)
            n = KT - 1
            for j in range(TAPS):
                if j:
                    pool.wait_ge(pool_tap, j)
                nc.gpsimd.tensor_tensor(tmp, g_pad[:, n, j:j + T], col("conv_w", n * TAPS + j).to_broadcast([P, T]),
                                        ALU.mult).then_inc(pool_mul, 1)
                pool.wait_ge(pool_mul, j + 1)
                nc.gpsimd.tensor_tensor(conv[:, n, :], tmp, conv[:, n, :] if j else col("conv_b", n).to_broadcast([P, T]),
                                        ALU.add).then_inc(pool_tap, 1)
            with pool.Fori(0, (EV - AO) // 4) as i:
                for u in range(4):
                    lo(i * 4 + (AO + 1 + u), u + 1)


def kernel(**inputs):
    import numpy as np
    import concourse.bacc as _bacc
    from concourse.bass_utils import run_bass_kernel_spmd as _run

    a = {k: np.asarray(v) for k, v in inputs.items()}
    f = np.float32

    def columns(w):
        n = w.shape[1] // P
        return w.reshape(KT, P, n, P).transpose(2, 1, 0, 3).reshape(n, P, D)

    def tiles(v):
        return v.reshape(-1, P).T

    def pairs(m, n):
        return np.stack([m, n], axis=1).reshape(-1, P, D)

    w_in = columns(a["w_in"][0])
    qkv = NH + 2 * NKV
    w_q, w_k, w_v = w_in[0:NH], w_in[NH:NH + NKV], w_in[NH + NKV:qkv]
    conv_a, conv_b = w_in[qkv:qkv + KT], w_in[qkv + KT:qkv + 2 * KT]
    gate_a, gate_c = w_in[qkv + 2 * KT:qkv + 3 * KT], w_in[qkv + 3 * KT:qkv + 4 * KT]
    order = np.concatenate([np.arange(HD2) + HD2 * (8 * kt + 4 * half + r)
                            for kt in range(2) for r in range(4) for half in range(2)])
    s_in = a["swa_w_in_2"][0]
    s_q = columns(s_in[:, 0:D][:, order])
    s_kv = columns(s_in[:, D:])
    s_out = columns(a["swa_w_out_2"][0][order, :])
    gu = columns(a["ffn_w_gate_up_2"][0])
    w_mod = columns(a["w_mod"][0])
    panels = np.concatenate([
        w_mod[:MOD1], pairs(conv_a, conv_b), w_k, w_v, w_q, pairs(gate_a, columns(a["w_attn_o"][0])),
        gate_c, columns(a["w_conv_o"][0]), columns(a["w_out"][0]), columns(a["peer_wq"][0]),
        a["peer_u"][0].reshape(NK, P, KT, P).transpose(0, 3, 2, 1).reshape(NK, P, D), a["peer_v"][0].reshape(NK, P, D),
        s_kv, s_q, s_out, pairs(gu[0:FT], gu[FT:]), a["ffn_w_down_2"][0].reshape(FT, P, D)])
    assert panels.shape == (PANELS, P, D)

    half, quarter = P // 2, P // 4
    pos = np.arange(T)
    inv = (np.float32(10000.0) ** (-np.arange(0, half, 2, dtype=f) / half)).astype(f)
    ang = np.concatenate([(p[:, None].astype(f) * inv).T for p in (pos // 64, pos // 64, pos % 64, pos % 64)])
    rope = np.stack([np.cos(ang), np.sin(ang)], axis=1).astype(f)
    perm = np.zeros((P, P), f)
    for d in range(P):
        first = d % half < quarter
        perm[d + quarter if first else d - quarter, d] = -1.0 if first else 1.0
    gap = (P + np.arange(P))[:, None] - np.arange(2 * P)[None, :]
    dist = np.where((gap >= 0) & (gap < P), gap, 1e30).astype(f)
    dist = np.stack([dist, np.full_like(dist, 1e30)], axis=1)
    slopes = -np.exp2(-8.0 * np.arange(1, NH2 + 1, dtype=f) / NH2).astype(f)

    wide = lambda v: np.broadcast_to(v, (P, v.shape[-1]))
    parts = {
        "b_mod": tiles(a["b_mod"][0]), "norm1": tiles(a["norm1_g"][0]), "norm2": tiles(a["norm2_g"][0]),
        "final1": tiles(a["final_norm_g"]), "conv_w": a["conv_dw"][0].T.reshape(KT, P, TAPS).transpose(1, 0, 2).reshape(P, -1),
        "conv_b": tiles(a["conv_b"][0]), "ln_g": tiles(a["conv_ln_g"][0]), "ln_b": tiles(a["conv_ln_b"][0]),
        "q_g": tiles(a["q_norm_g"][0]), "k_g": tiles(a["k_norm_g"][0]), "mix": tiles(a["norm_mix_2"][0]),
        "ffn": tiles(a["norm_ffn_2"][0]), "final2": tiles(a["final_norm_2"]),
        "c": np.stack([tiles(a["c"][0]), tiles(a["c_ctx"])], axis=2).reshape(P, -1),
        "sinks": wide(a["swa_sinks_2"][0]), "slopes": wide(slopes), "ident": np.eye(P, dtype=f),
        "ones": np.ones((P, P), f), "perm": perm, "iota": wide(np.arange(P, dtype=f)), "zero": np.zeros((P, 1), f)}
    small = np.concatenate([parts[n] for n in SMALL], axis=1)
    assert small.shape == (P, SMALL_N)
    arrays = {
        "panels": panels, "mod2": w_mod[MOD1:], "small": small,
        "xT": a["x"][0].T.reshape(KT, P, T).transpose(1, 0, 2), "ctxT": a["ctx"][0].T.reshape(KT, P, CTX).transpose(1, 0, 2),
        "rope": rope, "keys": a["peer_keys"][0].reshape(HP, NK, P).transpose(2, 0, 1), "dist": dist}
    arrays = {k: np.ascontiguousarray(v) for k, v in arrays.items()}

    nc = _bacc.Bacc("TRN2", target_bir_lowering=False, num_devices=1)
    aps = [nc.dram_tensor(k, v.shape, mybir.dt.from_np(v.dtype), kind="ExternalInput").ap() for k, v in arrays.items()]
    w_d = nc.dram_tensor("w_scratch", (NK, P, T), F32, kind="Internal").ap()
    ge_d = nc.dram_tensor("gelu_scratch", (NK, P, T), F32, kind="Internal").ap()
    out = nc.dram_tensor("out", (P, KT, T), F32, kind="ExternalOutput").ap()
    build(nc, *aps, w_d, ge_d, out)
    r = _run(nc, [arrays], core_ids=[0])
    return np.ascontiguousarray(r.results[0]["out"].transpose(2, 1, 0).reshape(1, T, D))
```
